# Optimizing a Trainium2 kernel written in Bass

```python
import jax
import jax.numpy as jnp
from jax import lax
import numpy as np

D_MODEL = 1024
BATCH = 1
SEQ = 512
DEPTH = 2
DEC_BATCH = 8
DEC_SEQ = 1
PAST_LEN = 256
PAGE_SIZE = 128

N_MIXERS = 2
N_HEADS = 16
HEAD_DIM = 64
N_KV = 4
GROUP = N_HEADS // N_KV
Q_DIM = N_HEADS * HEAD_DIM
KV_DIM = N_KV * HEAD_DIM
ROT_DIM = HEAD_DIM // 4
ROPE_THETA = 500000.0
D_FF = 2816
BLOCK = 64
N_SEL = 8
WINDOW = 512
CMP_HIDDEN = 128
FORCE = 1.0e4
N_IDX = 8
IDX_DIM = 64
DSA_TOPK = 256
Q_BLOCK = 128
NSA_COLS = Q_DIM + 6 * KV_DIM + 3 * N_HEADS
DSA_COLS = Q_DIM + 2 * KV_DIM + N_IDX * IDX_DIM + IDX_DIM + N_IDX
RMS_EPS = 1e-6
NEG = -1e30

kernel_name = 'nsa_dsa_macaron_hybrid_step'

def rmsnorm(x, g):
    xf = x.astype(jnp.float32)
    y = xf * lax.rsqrt(jnp.mean(xf * xf, axis=-1, keepdims=True) + RMS_EPS)
    return y.astype(x.dtype) * g

def swiglu(h, w_in, w_out):
    gu = h @ w_in
    return (jax.nn.silu(gu[..., :D_FF]) * gu[..., D_FF:]) @ w_out

def rope(x, pos):
    half = ROT_DIM // 2
    inv = ROPE_THETA ** (-jnp.arange(half, dtype=jnp.float32) * 2.0 / ROT_DIM)
    ang = pos.astype(jnp.float32)[:, None] * inv[None, :]
    cos = jnp.cos(ang)[:, None, :].astype(x.dtype)
    sin = jnp.sin(ang)[:, None, :].astype(x.dtype)
    x1, x2, xp = x[..., :half], x[..., half:ROT_DIM], x[..., ROT_DIM:]
    return jnp.concatenate([x1 * cos - x2 * sin, x2 * cos + x1 * sin, xp], axis=-1)

def masked_softmax(s, mask):
    s = jnp.where(mask, s, NEG)
    p = jnp.where(mask, jnp.exp(s - jnp.max(s, axis=-1, keepdims=True)), 0.0)
    return p / jnp.maximum(jnp.sum(p, axis=-1, keepdims=True), 1e-30)

def gather_paged(pool, page_table, new_rows, pos, head=None):
    n_past = page_table.shape[1] * PAGE_SIZE
    bidx = jnp.arange(pos.shape[0]).reshape((-1,) + (1,) * (pos.ndim - 1))
    pp = jnp.clip(pos, 0, n_past - 1)
    phys = page_table[bidx, pp // PAGE_SIZE]
    off = pp % PAGE_SIZE
    nidx = jnp.clip(pos - n_past, 0, new_rows.shape[1] - 1)
    if head is None:
        past = pool[phys, off]
        new = new_rows[bidx, nidx]
    else:
        past = pool[phys, off, :, head]
        new = new_rows[bidx, nidx, :, head]
    in_past = (pos < n_past).reshape(pos.shape + (1,) * (past.ndim - pos.ndim))
    return jnp.where(in_past, past, new)

def compress(rows, pos_emb, w1, w2):
    b, lp = rows.shape[:2]
    blocks = rows.reshape(b, lp // BLOCK, BLOCK, 2, N_KV, HEAD_DIM)
    pre = (jnp.einsum('bnlckd,cldh->bnckh', blocks, w1)
           + jnp.einsum('lcd,cldh->ch', pos_emb, w1)[:, None, :])
    return jnp.einsum('bnckh,chd->bnckd', jax.nn.gelu(pre), w2)

def nsa_attend(q, qr, gates, qpos, kc, vc, sel_fn, kw, vw, kwpos):
    scale = HEAD_DIM ** -0.5
    nb = kc.shape[1]
    blk = jnp.arange(nb)
    s = jnp.einsum('btkgd,bnkd->btkgn', q, kc).astype(jnp.float32) * scale
    cmask = ((blk + 1) * BLOCK - 1)[None, :] <= qpos[:, None]
    p_cmp = masked_softmax(s, cmask[None, :, None, None, :])
    o_cmp = jnp.einsum('btkgn,bnkd->btkgd', p_cmp.astype(vc.dtype), vc)
    cur = (qpos // BLOCK)[:, None]
    imp = jnp.sum(p_cmp, axis=3)
    forced = (blk[None] == 0) | (blk[None] == cur) | (blk[None] == cur - 1)
    score = jnp.where(forced[None, :, None, :], FORCE, imp)
    score = jnp.where((blk[None] <= cur)[None, :, None, :], score, -1.0)
    nsel = min(N_SEL, nb)
    top_s, top_i = lax.top_k(score, nsel)
    spos5 = top_i[..., None] * BLOCK + jnp.arange(BLOCK)
    smask5 = (top_s >= 0)[..., None] & (spos5 <= qpos[None, :, None, None, None])
    flat = top_i.shape[:3] + (nsel * BLOCK,)
    spos, smask = spos5.reshape(flat), smask5.reshape(flat)
    ks, vs = sel_fn(spos)
    s = jnp.einsum('btkgd,btkmd->btkgm', qr, ks).astype(jnp.float32) * scale
    p = masked_softmax(s, smask[:, :, :, None, :])
    o_slc = jnp.einsum('btkgm,btkmd->btkgd', p.astype(vs.dtype), vs)
    s = jnp.einsum('btkgd,blkd->btkgl', qr, kw).astype(jnp.float32) * scale
    dpos = qpos[:, None] - kwpos[None, :]
    wmask = (dpos >= 0) & (dpos <= WINDOW) & (kwpos[None, :] >= 0)
    p = masked_softmax(s, wmask[None, :, None, None, :])
    o_win = jnp.einsum('btkgl,blkd->btkgd', p.astype(vw.dtype), vw)
    g = gates.astype(o_cmp.dtype)
    return g[..., 0:1] * o_cmp + g[..., 1:2] * o_slc + g[..., 2:3] * o_win

def nsa_project(h, w_in, pos):
    b, t, _ = h.shape
    z = h @ w_in
    q = z[..., :Q_DIM].reshape(b, t, N_HEADS, HEAD_DIM)
    kv = z[..., Q_DIM:Q_DIM + 6 * KV_DIM].reshape(b, t, 3, 2, N_KV, HEAD_DIM)
    gates = jax.nn.sigmoid(z[..., Q_DIM + 6 * KV_DIM:]).reshape(b, t, N_KV, GROUP, 3)
    qr = rope(q, pos).reshape(b, t, N_KV, GROUP, HEAD_DIM)
    q = q.reshape(b, t, N_KV, GROUP, HEAD_DIM)
    kv_cmp = kv[:, :, 0]
    kv_slc = jnp.stack([rope(kv[:, :, 1, 0], pos), kv[:, :, 1, 1]], axis=2)
    kv_win = jnp.stack([rope(kv[:, :, 2, 0], pos), kv[:, :, 2, 1]], axis=2)
    return q, qr, gates, kv_cmp, kv_slc, kv_win

def nsa_prompt(h, w_in, w_out, cmp_pos, cmp_w1, cmp_w2):
    b, t, _ = h.shape
    q, qr, gates, kv_cmp, kv_slc, kv_win = nsa_project(h, w_in, jnp.arange(t))
    kvc = compress(kv_cmp, cmp_pos, cmp_w1, cmp_w2)
    kc, vc = kvc[:, :, 0], kvc[:, :, 1]
    win_pad = jnp.pad(kv_win, ((0, 0), (WINDOW, 0), (0, 0), (0, 0), (0, 0)))
    bidx = jnp.arange(b)[:, None, None, None]
    hidx = jnp.arange(N_KV)[None, None, :, None]

    def sel_fn(spos):
        r = kv_slc[bidx, spos, :, hidx]
        return r[..., 0, :], r[..., 1, :]

    def block(i):
        s0 = i * Q_BLOCK
        cut = lambda a: lax.dynamic_slice_in_dim(a, s0, Q_BLOCK, axis=1)
        kw = lax.dynamic_slice_in_dim(win_pad, s0, WINDOW + Q_BLOCK, axis=1)
        qpos = s0 + jnp.arange(Q_BLOCK)
        kwpos = s0 - WINDOW + jnp.arange(WINDOW + Q_BLOCK)
        return nsa_attend(cut(q), cut(qr), cut(gates), qpos, kc, vc, sel_fn,
                          kw[:, :, 0], kw[:, :, 1], kwpos)

    o = lax.map(block, jnp.arange(t // Q_BLOCK))
    o = jnp.moveaxis(o, 0, 1).reshape(b, t, Q_DIM)
    wb = min(WINDOW, t)
    return o @ w_out, kv_cmp, kv_slc, kv_win[:, t - wb:]

def nsa_sample(h, cache_cmp, cache_slc, win_state, page_table, w_in, w_out, cmp_pos, cmp_w1, cmp_w2):
    b, t, _ = h.shape
    n_past = page_table.shape[1] * PAGE_SIZE
    pos = n_past + jnp.arange(t)
    q, qr, gates, kv_cmp, kv_slc, kv_win = nsa_project(h, w_in, pos)
    total = n_past + t
    nb = -(-total // BLOCK)
    past = cache_cmp[page_table].reshape((b, n_past) + cache_cmp.shape[2:])
    rows = jnp.concatenate([past, kv_cmp], axis=1)
    rows = jnp.pad(rows, ((0, 0), (0, nb * BLOCK - total), (0, 0), (0, 0), (0, 0)))
    kvc = compress(rows, cmp_pos, cmp_w1, cmp_w2)
    kc, vc = kvc[:, :, 0], kvc[:, :, 1]
    hidx = jnp.arange(N_KV)[None, None, :, None]

    def sel_fn(spos):
        r = gather_paged(cache_slc, page_table, kv_slc, spos, hidx)
        return r[..., 0, :], r[..., 1, :]

    win = jnp.concatenate([win_state, kv_win], axis=1)
    wb = win_state.shape[1]
    kwpos = n_past - wb + jnp.arange(wb + t)
    o = nsa_attend(q, qr, gates, pos, kc, vc, sel_fn, win[:, :, 0], win[:, :, 1], kwpos)
    return o.reshape(b, t, Q_DIM) @ w_out, kv_cmp, kv_slc, win[:, t:]

def dsa_attend(q, qi, wi, qpos, ki, topk, gather_kv):
    n_keys = ki.shape[1]
    sc = jnp.einsum('bthd,bsd->bths', qi, ki).astype(jnp.float32) * IDX_DIM ** -0.5
    score = jnp.einsum('bths,bth->bts', jax.nn.relu(sc), wi.astype(jnp.float32))
    kpos = jnp.arange(n_keys)
    score = jnp.where(kpos[None, None, :] <= qpos[None, :, None], score, NEG)
    _, top_i = lax.top_k(score, topk)
    valid = top_i <= qpos[None, :, None]
    kv = gather_kv(top_i)
    k, v = kv[:, :, :, 0], kv[:, :, :, 1]
    s = jnp.einsum('btkgd,btmkd->btkgm', q, k).astype(jnp.float32) * HEAD_DIM ** -0.5
    p = masked_softmax(s, valid[:, :, None, None, :])
    return jnp.einsum('btkgm,btmkd->btkgd', p.astype(v.dtype), v)

def dsa_project(h, w_in, pos):
    b, t, _ = h.shape
    z = h @ w_in
    q = rope(z[..., :Q_DIM].reshape(b, t, N_HEADS, HEAD_DIM), pos).reshape(b, t, N_KV, GROUP, HEAD_DIM)
    kv = z[..., Q_DIM:Q_DIM + 2 * KV_DIM].reshape(b, t, 2, N_KV, HEAD_DIM)
    kv = jnp.stack([rope(kv[:, :, 0], pos), kv[:, :, 1]], axis=2)
    o1 = Q_DIM + 2 * KV_DIM
    qi = rope(z[..., o1:o1 + N_IDX * IDX_DIM].reshape(b, t, N_IDX, IDX_DIM), pos)
    o2 = o1 + N_IDX * IDX_DIM
    ki = rope(z[..., o2:o2 + IDX_DIM].reshape(b, t, 1, IDX_DIM), pos)[:, :, 0]
    wi = z[..., o2 + IDX_DIM:] * N_IDX ** -0.5
    return q, kv, qi, ki, wi

def dsa_prompt(h, w_in, w_out):
    b, t, _ = h.shape
    q, kv, qi, ki, wi = dsa_project(h, w_in, jnp.arange(t))
    topk = min(DSA_TOPK, t // 4)
    bidx = jnp.arange(b)[:, None, None]

    def gather_kv(idx):
        return kv[bidx, idx]

    def block(i):
        s0 = i * Q_BLOCK
        cut = lambda a: lax.dynamic_slice_in_dim(a, s0, Q_BLOCK, axis=1)
        qpos = s0 + jnp.arange(Q_BLOCK)
        return dsa_attend(cut(q), cut(qi), cut(wi), qpos, ki, topk, gather_kv)

    o = lax.map(block, jnp.arange(t // Q_BLOCK))
    o = jnp.moveaxis(o, 0, 1).reshape(b, t, Q_DIM)
    return o @ w_out, kv, ki

def dsa_sample(h, cache_kv, cache_idx, page_table, w_in, w_out):
    b, t, _ = h.shape
    n_past = page_table.shape[1] * PAGE_SIZE
    pos = n_past + jnp.arange(t)
    q, kv, qi, ki, wi = dsa_project(h, w_in, pos)
    ki_all = jnp.concatenate([cache_idx[page_table].reshape(b, n_past, IDX_DIM), ki], axis=1)
    topk = min(DSA_TOPK, (n_past + t) // 4)

    def gather_kv(idx):
        return gather_paged(cache_kv, page_table, kv, idx)

    o = dsa_attend(q, qi, wi, pos, ki_all, topk, gather_kv)
    return o.reshape(b, t, Q_DIM) @ w_out, kv, ki

def setup_inputs(seed: int = 0) -> dict:
    key = jax.random.key(seed)
    ks = jax.random.split(key, 20)
    n_a = len(range(0, DEPTH, N_MIXERS))
    n_b = len(range(1, DEPTH, N_MIXERS))
    n_pages = PAST_LEN // PAGE_SIZE
    n_used = DEC_BATCH * n_pages
    n_pool = n_used + n_used // 4
    win_buf = min(WINDOW, PAST_LEN)
    f32 = jnp.float32
    nrm = lambda k, shape, sc: jax.random.normal(k, shape, f32) * sc
    page_table = jax.random.permutation(ks[7], n_pool)[:n_used].reshape(DEC_BATCH, n_pages).astype(jnp.int32)
    return {
        'x_prompt': nrm(ks[0], (BATCH, SEQ, D_MODEL), 1.0),
        'x_sample': nrm(ks[1], (DEC_BATCH, DEC_SEQ, D_MODEL), 1.0),
        'cache_nsa_cmp': nrm(ks[2], (n_a, n_pool, PAGE_SIZE, 2, N_KV, HEAD_DIM), 1.0),
        'cache_nsa_slc': nrm(ks[3], (n_a, n_pool, PAGE_SIZE, 2, N_KV, HEAD_DIM), 1.0),
        'state_nsa_win': nrm(ks[4], (n_a, DEC_BATCH, win_buf, 2, N_KV, HEAD_DIM), 1.0),
        'cache_dsa_kv': nrm(ks[5], (n_b, n_pool, PAGE_SIZE, 2, N_KV, HEAD_DIM), 1.0),
        'cache_dsa_idx': nrm(ks[6], (n_b, n_pool, PAGE_SIZE, IDX_DIM), 1.0),
        'page_table': page_table,
        'norm_g': 1.0 + nrm(ks[8], (DEPTH, 3, D_MODEL), 0.01),
        'w_ffn_in': nrm(ks[9], (DEPTH, 2, D_MODEL, 2 * D_FF), D_MODEL ** -0.5),
        'w_ffn_out': nrm(ks[10], (DEPTH, 2, D_FF, D_MODEL), D_FF ** -0.5),
        'w_nsa_in': nrm(ks[11], (n_a, D_MODEL, NSA_COLS), D_MODEL ** -0.5),
        'w_nsa_out': nrm(ks[12], (n_a, Q_DIM, D_MODEL), Q_DIM ** -0.5),
        'nsa_cmp_pos': nrm(ks[13], (n_a, BLOCK, 2, HEAD_DIM), 0.1),
        'nsa_cmp_w1': nrm(ks[14], (n_a, 2, BLOCK, HEAD_DIM, CMP_HIDDEN), (BLOCK * HEAD_DIM) ** -0.5),
        'nsa_cmp_w2': nrm(ks[15], (n_a, 2, CMP_HIDDEN, HEAD_DIM), CMP_HIDDEN ** -0.5),
        'w_dsa_in': nrm(ks[16], (n_b, D_MODEL, DSA_COLS), D_MODEL ** -0.5),
        'w_dsa_out': nrm(ks[17], (n_b, Q_DIM, D_MODEL), Q_DIM ** -0.5),
        'final_norm_g': 1.0 + nrm(ks[18], (D_MODEL,), 0.01),
    }

def reference(x_prompt, x_sample, cache_nsa_cmp, cache_nsa_slc, state_nsa_win, cache_dsa_kv, cache_dsa_idx,
              page_table, norm_g, w_ffn_in, w_ffn_out, w_nsa_in, w_nsa_out, nsa_cmp_pos, nsa_cmp_w1,
              nsa_cmp_w2, w_dsa_in, w_dsa_out, final_norm_g):
    xp, xs = x_prompt, x_sample
    cmp_p, cmp_s, slc_p, slc_s, win_p, win_s = [], [], [], [], [], []
    dkv_p, dkv_s, didx_p, didx_s = [], [], [], []
    for layer in range(DEPTH):
        kind, j = layer % N_MIXERS, layer // N_MIXERS
        xp = xp + 0.5 * swiglu(rmsnorm(xp, norm_g[layer, 0]), w_ffn_in[layer, 0], w_ffn_out[layer, 0])
        xs = xs + 0.5 * swiglu(rmsnorm(xs, norm_g[layer, 0]), w_ffn_in[layer, 0], w_ffn_out[layer, 0])
        hp = rmsnorm(xp, norm_g[layer, 1])
        hs = rmsnorm(xs, norm_g[layer, 1])
        if kind == 0:
            yp, c_p, s_p, w_p = nsa_prompt(hp, w_nsa_in[j], w_nsa_out[j], nsa_cmp_pos[j], nsa_cmp_w1[j], nsa_cmp_w2[j])
            ys, c_s, s_s, w_s = nsa_sample(hs, cache_nsa_cmp[j], cache_nsa_slc[j], state_nsa_win[j], page_table,
                                           w_nsa_in[j], w_nsa_out[j], nsa_cmp_pos[j], nsa_cmp_w1[j], nsa_cmp_w2[j])
            cmp_p.append(c_p); cmp_s.append(c_s); slc_p.append(s_p); slc_s.append(s_s)
            win_p.append(w_p); win_s.append(w_s)
        else:
            yp, kv_p, ki_p = dsa_prompt(hp, w_dsa_in[j], w_dsa_out[j])
            ys, kv_s, ki_s = dsa_sample(hs, cache_dsa_kv[j], cache_dsa_idx[j], page_table, w_dsa_in[j], w_dsa_out[j])
            dkv_p.append(kv_p); dkv_s.append(kv_s); didx_p.append(ki_p); didx_s.append(ki_s)
        xp = xp + yp
        xs = xs + ys
        xp = xp + 0.5 * swiglu(rmsnorm(xp, norm_g[layer, 2]), w_ffn_in[layer, 1], w_ffn_out[layer, 1])
        xs = xs + 0.5 * swiglu(rmsnorm(xs, norm_g[layer, 2]), w_ffn_in[layer, 1], w_ffn_out[layer, 1])
    y_prompt = rmsnorm(xp, final_norm_g)
    y_sample = rmsnorm(xs, final_norm_g)
    return (y_prompt, y_sample, jnp.stack(cmp_p), jnp.stack(cmp_s), jnp.stack(slc_p), jnp.stack(slc_s),
            jnp.stack(win_p), jnp.stack(win_s), jnp.stack(dkv_p), jnp.stack(dkv_s),
            jnp.stack(didx_p), jnp.stack(didx_s))


_drawn_inputs = setup_inputs


def setup_inputs(seed=0):
    import zlib

    import numpy as np

    out = dict(_drawn_inputs(seed))
    spreads = {}
    factors = {}
    for name, (base, spread) in spreads.items():
        noise = np.random.default_rng([zlib.crc32(name.encode()), seed]).standard_normal(out[name].shape)
        drawn = base * np.exp(spread * noise) if base else spread * noise
        out[name] = jnp.asarray(drawn.astype(out[name].dtype))
    for name, factor in factors.items():
        out[name] = (out[name] * factor).astype(out[name].dtype)
    return out
```

```python
from contextlib import ExitStack

import concourse.bass as bass
from concourse import mybir

F32 = mybir.dt.float32
FR = mybir.dt.float32r
BF16 = mybir.dt.bfloat16
I32 = mybir.dt.int32
ACT = mybir.ActivationFunctionType
ALU = mybir.AluOpType
AX = mybir.AxisListType
ds = bass.ds

P = 128
D = 1024
KC = D // P
TP = 512
TS = 8
T = TP + TS
TH = T // 2
NT = 5
DFF = 2816
FH = DFF // P // 2
HEADS = 16
HD = 64
KV = 4
NSA_COLS = 2608
DSA_COLS = 2120
EPS = 1e-6
NEG = -1e30
SCALE = HD ** -0.5
UNIT = FH * P


class Stream:

    def __init__(self):
        self.regions = []
        self.total = 0

    def add(self, name, count, src, cols, per=2):
        self.regions.append((name, self.total, count, src, cols, per))
        self.total += count

    def start(self, name):
        return next(r[1] for r in self.regions if r[0] == name)


class Core:

    def __init__(self, nc, sig, ins, outs, consts, const, views, sem):
        self.nc, self.sig, self.stream, self.const, self.c_const = nc, sig, Stream(), const, consts
        self.h_n, self.norm_n, self.sums, self.stores, self.x_rows = 0, 0, 0, 0, 0
        self.x_prompt, self.x_sample, self.cache_nsa_cmp = ins["x_prompt"], ins["x_sample"], ins["cache_nsa_cmp"]
        self.cache_nsa_slc, self.state_nsa_win, self.cache_dsa_kv = ins["cache_nsa_slc"], ins["state_nsa_win"], ins["cache_dsa_kv"]
        self.cache_dsa_idx, self.page_table, self.norm_g = ins["cache_dsa_idx"], ins["page_table"], ins["norm_g"]
        self.w_ffn_in, self.w_ffn_out, self.w_nsa_in = ins["w_ffn_in"], ins["w_ffn_out"], ins["w_nsa_in"]
        self.w_nsa_out, self.nsa_cmp_pos, self.nsa_cmp_w1 = ins["w_nsa_out"], ins["nsa_cmp_pos"], ins["nsa_cmp_w1"]
        self.nsa_cmp_w2, self.w_dsa_in, self.w_dsa_out = ins["nsa_cmp_w2"], ins["w_dsa_in"], ins["w_dsa_out"]
        self.final_norm_g = ins["final_norm_g"]
        self.y_prompt, self.y_sample, self.nsa_cmp_p = outs["y_prompt"], outs["y_sample"], outs["nsa_cmp_p"]
        self.nsa_cmp_s, self.nsa_slc_p, self.nsa_slc_s = outs["nsa_cmp_s"], outs["nsa_slc_p"], outs["nsa_slc_s"]
        self.nsa_win_p, self.nsa_win_s, self.dsa_kv_p = outs["nsa_win_p"], outs["nsa_win_s"], outs["dsa_kv_p"]
        self.dsa_kv_s, self.dsa_idx_p, self.dsa_idx_s = outs["dsa_kv_s"], outs["dsa_idx_p"], outs["dsa_idx_s"]
        self.ident, self.causal_f, self.ones, self.cos = views["ident"], views["causal_f"], views["ones"], views["cos"]
        self.sin, self.cadd, self.c01, self.hsel = views["sin"], views["cadd"], views["c01"], views["hsel"]
        self.esel, self.hmask, self.bmask, self.rep = views["esel"], views["hmask"], views["bmask"], views["rep"]
        self.esel_t, self.isel, self.imask, self.isel_t = views["esel_t"], views["isel"], views["imask"], views["isel_t"]
        self.landed0, self.landed1, self.lo_done = sem("landed0"), sem("landed1"), sem("lo_done")
        self.hi_done, self.unit_used, self.h_hi_done = sem("hi_done"), sem("unit_used"), sem("h_hi_done")
        self.h_lo_done, self.x_done, self.sq_done = sem("h_lo_done"), sem("x_done"), sem("sq_done")
        self.sum_done, self.stat_ready, self.rms_done = sem("sum_done"), sem("stat_ready"), sem("rms_done")
        self.rs_done, self.gate_read, self.up_read = sem("rs_done"), sem("gate_read"), sem("up_read")
        self.silu_done, self.act_ready, self.a_hi_done = sem("silu_done"), sem("act_ready"), sem("a_hi_done")
        self.a_lo_done, self.start_loaded, self.turned = sem("a_lo_done"), sem("start_loaded"), sem("turned")
        self.sample_turned, self.start_copied, self.row_turned = sem("sample_turned"), sem("start_copied"), sem("row_turned")
        self.row_copied, self.y_done, self.stored = sem("row_copied"), sem("y_done"), sem("stored")
        self.landed = [self.landed0, self.landed1]

    def cols_of(self, u):
        return next(r[4] for r in self.stream.regions if r[1] <= u < r[1] + r[2])


class SampleBuffers:

    def __init__(self, qbd, qz, o_t):
        self.qbd, self.qz, self.o_t = qbd, qz, o_t


def load_units(e, sp, first, last):
    for name, at, count, src, cols, per in e.stream.regions:
        lo, hi = max(first, at), min(last, at + count)
        if lo >= hi:
            continue

        def one(turn, side, u):
            slot = (at + side) % 2
            view, dst = src(turn, side, (lambda v: v) if isinstance(u, int) else sp.snap), e.w_stage[slot][:, 0:cols]
            if not isinstance(u, int) or u >= 2:
                sp.wait_ge(e.lo_done, u - 1)
            sp.dma_start(dst.rearrange("p (k n) -> p k n", k=view.shape[1]), view).then_inc(e.landed[slot], 16)

        k = lo - at
        while k % per and k < hi - at:
            one(k // per, k % per, at + k)
            k += 1
        turns = (hi - at - k) // per
        if turns > 1 and at + k >= 2:
            t0 = k // per
            with sp.Fori(t0, t0 + turns) as q:
                for side in range(per):
                    one(q, side, q * per + (at + side))
            k += per * turns
        while k < hi - at:
            one(k // per, k % per, at + k)
            k += 1


def split_hi(e, act, base, q, cols):
    slot = base % 2
    act.wait_ge(e.landed[slot], q * 16 + 16 * (base // 2 + 1))
    if base >= 2 or not isinstance(q, int):
        act.wait_ge(e.unit_used, q * 2 + (base - 1))
    act.activation(e.w_hi[slot][:, 0:cols], e.w_stage[slot][:, 0:cols], ACT.Copy).then_inc(e.hi_done, 1)


def split_lo(e, dve, base, q, cols):
    slot = base % 2
    dve.wait_ge(e.hi_done, q * 2 + (base + 1))
    dve.tensor_tensor(e.w_lo[slot][:, 0:cols], e.w_stage[slot][:, 0:cols],
                      e.w_hi[slot][:, 0:cols].bitcast(F32), ALU.subtract).then_inc(e.lo_done, 1)


def three_passes(pe, out, w_hi, w_lo, x_hi, x_lo, first, last):
    pe.matmul(out, w_hi, x_hi, start=first, stop=False)
    pe.matmul(out, w_hi, x_lo, start=False, stop=False)
    return pe.matmul(out, w_lo, x_hi, start=False, stop=last)


def warm_up(e, pe, out, count):
    for _ in range(count):
        pe.matmul(out, e.ident_b[:, :], e.causal_b[:, :], start=True, stop=True)



def build_h_act(e, act, norm):
    for k in range(KC):
        act.activation(e.h_hi[:, k, 0:T], e.x[:, k, :], ACT.Copy, scale=e.gain[:, norm * KC + k:norm * KC + k + 1])\
           .then_inc(e.h_hi_done, 1)


def build_h_dve(e, dve, norm, n):
    for k in range(KC):
        dve.wait_ge(e.h_hi_done, KC * n + k + 1)
        dve.scalar_tensor_tensor(e.h_lo[:, k, 0:T], e.x[:, k, :], e.gain[:, norm * KC + k:norm * KC + k + 1],
                                 e.h_hi[:, k, 0:T].bitcast(F32), ALU.mult, ALU.subtract).then_inc(e.h_lo_done, 1)


def square_sum_pool(e, pool, base):
    for i in range(KC):
        pool.wait_ge(e.x_done, base + i + 1)
        pool.wait_ge(e.sum_done, e.sums)
        pool.tensor_tensor(e.sq[:, :], e.x[:, i, :], e.x[:, i, :], ALU.mult).then_inc(e.sq_done, 1)
        pool.wait_ge(e.sq_done, e.sums + 1)
        if i == 0:
            pool.tensor_copy(e.sumsq[:, 0:T], e.sq[:, :]).then_inc(e.sum_done, 1)
        else:
            pool.tensor_tensor(e.sumsq[:, 0:T], e.sumsq[:, 0:T], e.sq[:, :], ALU.add).then_inc(e.sum_done, 1)
        e.sums += 1



def ffn_regions(e, n):
    layer, which = n // 2, n % 2
    w_in = e.w_ffn_in[layer, which].rearrange("(k p) n -> p k n", p=P)
    w_out = e.w_ffn_out[layer, which].rearrange("(f p) n -> p f n", p=P)
    for half in range(2):
        def src_in(pair, side, at, half=half):
            return w_in[:, :, ds(at(pair * P + (side * DFF + half * FH * P)), P)]

        def src_out(pair, side, at, half=half):
            return w_out[:, half * FH:(half + 1) * FH, ds(at(pair * (2 * P) + side * P), P)]

        e.stream.add(f"ffn{n}.in{half}", 2 * FH, src_in, KC * P)
        e.stream.add(f"ffn{n}.out{half}", KC, src_out, FH * P)


def ffn(e, n, norm, x_base):
    nc = e.nc
    in0 = [e.stream.start(f"ffn{n}.in{h}") for h in range(2)]
    out0 = [e.stream.start(f"ffn{n}.out{h}") for h in range(2)]
    end = out0[1] + KC
    f0 = 2 * FH * n
    with ExitStack() as ctx:
        def sb(name, shape, dt=F32):
            return ctx.enter_context(nc.sbuf_tensor(f"{name}_{n}", shape, dt))

        def ps(name, banks):
            return ctx.enter_context(nc.psum_tensor(f"{name}_{n}", [P, banks, 512], F32))
        e.h_hi, e.h_lo = sb("h_hi", [P, KC, T], FR), sb("h_lo", [P, KC, T], FR)
        a_hi, a_lo = sb("a_hi", [P, FH, T], FR), sb("a_lo", [P, FH, T], FR)
        gate_t, up_t, silu_t, act_t = (sb(s, [P, 2, TH]) for s in ("gate_t", "up_t", "silu_t", "act_t"))
        gate_ps, up_ps = ps("gate_ps", 2), ps("up_ps", 2)
        y_ps = [ps("y_ps0", 2), ps("y_ps1", 2)]
        rs2 = e.rs[:, :].rearrange("p (a t) -> p a t", a=2)
        hn = e.h_n
        sums = e.sums

        block = ctx.enter_context(nc.Block())

        @block.sync
        def _(sp):
            load_units(e, sp, in0[0] + 2, min(end + 2, e.stream.total))

        @block.gpsimd
        def _(pool):
            square_sum_pool(e, pool, x_base + KC)

        @block.tensor
        def _(pe):
            def in_unit(base, q, f, side, first_unit):
                slot = (base + side) % 2
                pe.wait_ge(e.lo_done, q * 2 + (base + side + 1))
                bank = (gate_ps, up_ps)[side]
                if not first_unit:
                    pe.wait_ge((e.gate_read, e.up_read)[side], f)
                for k in range(KC):
                    if first_unit and side == 0:
                        pe.wait_ge(e.h_lo_done, KC * hn + k + 1)
                    for half in range(2):
                        t = slice(half * TH, (half + 1) * TH)
                        m = three_passes(pe, bank[:, half, 0:TH], e.w_hi[slot][:, k * P:(k + 1) * P],
                                         e.w_lo[slot][:, k * P:(k + 1) * P], e.h_hi[:, k, t], e.h_lo[:, k, t],
                                         k == 0, k == KC - 1)
                m.then_inc(e.unit_used, 1)

            def statistics():
                pe.wait_ge(e.sum_done, sums)
                for half in range(2):
                    m = pe.matmul(y_ps[1][:, half, 0:TH], e.ones[:, :], e.sumsq[:, half * TH:(half + 1) * TH],
                                  start=True, stop=True)
                m.then_inc(e.stat_ready, 1)

            def out_unit(half, q, side, first):
                base = out0[half]
                slot = (base + side) % 2
                pe.wait_ge(e.lo_done, q * 2 + (base + side + 1))
                if not (first and half == 0):
                    pe.wait_ge(e.x_done, q * 2 + (x_base + KC * half + side - 1))
                for f in range(FH):
                    if first and side == 0:
                        pe.wait_ge(e.a_lo_done, f0 + half * FH + f + 2)
                    for th in range(2):
                        t = slice(th * TH, (th + 1) * TH)
                        m = three_passes(pe, y_ps[side][:, th, 0:TH], e.w_hi[slot][:, f * P:(f + 1) * P],
                                         e.w_lo[slot][:, f * P:(f + 1) * P], a_hi[:, f, t], a_lo[:, f, t],
                                         f == 0, f == FH - 1)
                m.then_inc(e.unit_used, 1)

            for half in range(2):
                for side in range(2):
                    in_unit(in0[half], 0, f0 + half * FH, side, half == 0)
                    if half == 0 and side == 0:
                        statistics()
                with pe.Fori(1, FH) as q:
                    for side in range(2):
                        in_unit(in0[half], q, q + (f0 + half * FH), side, False)
                if half == 0:
                    pe.wait_ge(e.rms_done, e.norm_n + 1)
                for side in range(2):
                    out_unit(half, 0, side, True)
                with pe.Fori(1, KC // 2) as q:
                    for side in range(2):
                        out_unit(half, q, side, False)

        @block.scalar
        def _(act):
            def a_hi_of(f, j):
                act.wait_ge(e.act_ready, f + 1)
                act.activation(a_hi[:, j, :] if isinstance(j, int) else a_hi[:, ds(j, 1), :],
                               act_t[:, :, :], ACT.Copy).then_inc(e.a_hi_done, 1)

            def silu_of(f, first):
                act.wait_ge(e.gate_read, f + 1)
                if not first:
                    act.wait_ge(e.act_ready, f)
                act.activation(silu_t[:, :, :], gate_t[:, :, :], ACT.Silu).then_inc(e.silu_done, 1)

            build_h_act(e, act, norm)
            for half in range(2):
                b = in0[half]
                F = f0 + half * FH
                split_hi(e, act, b + 1, 0, KC * P)
                split_hi(e, act, b + 2, 0, KC * P)
                if half == 0:
                    act.wait_ge(e.stat_ready, e.norm_n + 1)
                    act.activation(e.rms[:, :].rearrange("p (a t) -> p a t", a=2), y_ps[1][:, :, 0:TH], ACT.Sqrt,
                                   bias=e.eps[:, :], scale=1.0 / D).then_inc(e.rms_done, 1)
                silu_of(F, half == 0)
                if half == 1:
                    act.wait_ge(e.unit_used, out0[0] + KC)

                with act.Fori(1, FH - 1) as q:
                    split_hi(e, act, b + 1, q, KC * P)
                    a_hi_of(q + (F - 1), q - 1)
                    split_hi(e, act, b + 2, q, KC * P)
                    silu_of(q + F, False)
                split_hi(e, act, b + 2 * FH - 1, 0, KC * P)
                a_hi_of(F + FH - 2, FH - 2)
                split_hi(e, act, out0[half], 0, FH * P)
                silu_of(F + FH - 1, False)
                a_hi_of(F + FH - 1, FH - 1)
                split_hi(e, act, out0[half] + 1, 0, FH * P)
                with act.Fori(1, KC // 2) as q:
                    for side in range(2):
                        split_hi(e, act, out0[half] + side, q, FH * P)
                if half == 0:
                    split_hi(e, act, in0[1], 0, KC * P)
                elif end < e.stream.total:
                    split_hi(e, act, end, 0, e.cols_of(end))

        @block.vector
        def _(dve):
            def strip_of(b, q, f, j):
                dve.wait_ge(e.unit_used, q * 2 + (b + 2))
                dve.tensor_tensor(up_t[:, :, :], up_ps[:, :, 0:TH], rs2, ALU.mult).then_inc(e.up_read, 1)
                dve.wait_ge(e.up_read, f + 1)
                dve.wait_ge(e.silu_done, f + 1)
                dve.wait_ge(e.a_lo_done, f + 1)
                dve.tensor_tensor(act_t[:, :, :], up_t[:, :, :], silu_t[:, :, :], ALU.mult).then_inc(e.act_ready, 1)
                dve.wait_ge(e.a_hi_done, f + 1)
                dst, hi = (a_lo[:, j, :], a_hi[:, j, :]) if isinstance(j, int) else (a_lo[:, ds(j, 1), :], a_hi[:, ds(j, 1), :])
                dve.tensor_tensor(dst, act_t[:, :, :].rearrange("p a t -> p (a t)"), hi.bitcast(F32), ALU.subtract).then_inc(e.a_lo_done, 1)

            def gate_of(b, q, f, first):
                dve.wait_ge(e.unit_used, q * 2 + (b + 1))
                if not first:
                    dve.wait_ge(e.silu_done, f)
                dve.tensor_tensor(gate_t[:, :, :], gate_ps[:, :, 0:TH], rs2, ALU.mult).then_inc(e.gate_read, 1)

            def x_of(half, u, side, q, i):
                dve.wait_ge(e.unit_used, u)
                xi = e.x[:, i, :] if isinstance(i, int) else e.x[:, ds(i, 1), :]
                if isinstance(i, int):
                    xi = xi.rearrange("p (a t) -> p a t", a=2)
                else:
                    xi = xi.rearrange("p o (a t) -> p (o a) t", a=2)
                dve.scalar_tensor_tensor(xi, y_ps[side][:, :, 0:TH], 0.5, xi, ALU.mult, ALU.add).then_inc(e.x_done, 1)

            build_h_dve(e, dve, norm, hn)
            for half in range(2):
                b = in0[half]
                F = f0 + half * FH
                split_lo(e, dve, b + 1, 0, KC * P)
                split_lo(e, dve, b + 2, 0, KC * P)
                if half == 0:
                    dve.wait_ge(e.rms_done, e.norm_n + 1)
                    dve.reciprocal(e.rs[:, :], e.rms[:, :]).then_inc(e.rs_done, 1)
                    dve.wait_ge(e.rs_done, e.norm_n + 1)
                gate_of(b, 0, F, half == 0)
                with dve.Fori(1, FH - 1) as q:
                    split_lo(e, dve, b + 1, q, KC * P)
                    strip_of(b, q - 1, q + (F - 1), q - 1)
                    split_lo(e, dve, b + 2, q, KC * P)
                    gate_of(b, q, q + F, False)
                split_lo(e, dve, b + 2 * FH - 1, 0, KC * P)
                strip_of(b + 2 * (FH - 2), 0, F + FH - 2, FH - 2)
                split_lo(e, dve, out0[half], 0, FH * P)
                gate_of(b + 2 * (FH - 1), 0, F + FH - 1, False)
                strip_of(b + 2 * (FH - 1), 0, F + FH - 1, FH - 1)
                o = out0[half]
                split_lo(e, dve, o + 1, 0, FH * P)
                with dve.Fori(1, KC // 2) as q:
                    split_lo(e, dve, o, q, FH * P)
                    x_of(half, q * 2 + (o - 1), 0, q, q * 2 - 2)
                    split_lo(e, dve, o + 1, q, FH * P)
                    x_of(half, q * 2 + o, 1, q, q * 2 - 1)
                if half == 0:
                    split_lo(e, dve, in0[1], 0, KC * P)
                elif end < e.stream.total:
                    split_lo(e, dve, end, 0, e.cols_of(end))
                x_of(half, o + KC - 1, 0, 0, KC - 2)
                x_of(half, o + KC, 1, 0, KC - 1)
    e.h_n += 1
    e.norm_n += 1



class Signal:

    def __init__(self, sem):
        self.sem, self.base = sem, 0

    def wait(self, eng, n):
        eng.wait_ge(self.sem, n + self.base)


class Chain:

    def __init__(self, eng, mark):
        self.eng, self.mark, self.n = eng, mark, 0

    def __call__(self, ins):
        ins.then_inc(self.mark.sem, 1)
        self.n += 1
        self.mark.wait(self.eng, self.n)


def projection_regions(e, name, w, cols, groups):
    view = w.rearrange("(k p) n -> p k n", p=P)

    def src(group, side, at):
        return view[:, 2 * side:2 * side + 2, ds(at(group * 512), 512)]

    e.stream.add(f"{name}.in", 4 * groups, src, 1024, 4)
    e.stream.add(f"{name}.rest", 1, lambda pair, side, at: view[:, :, groups * 512:cols], KC * (cols - groups * 512))


def out_regions(e, name, w):
    view = w.rearrange("(k p) n -> p k n", p=P)
    e.stream.add(f"{name}.out", KC, lambda pair, side, at: view[:, :, ds(at(pair * (2 * P) + side * P), P)], KC * P)


def projection(e, name, norm, z, groups, cols):
    nc = e.nc
    u0, u1 = e.stream.start(f"{name}.in"), e.stream.start(f"{name}.rest")
    rest = cols - 512 * groups
    n_norm, hn, sums = e.norm_n, e.h_n, e.sums
    with ExitStack() as ctx:
        e.h_hi = ctx.enter_context(nc.sbuf_tensor(f"{name}_h_hi", [P, KC, NT * P], FR))
        e.h_lo = ctx.enter_context(nc.sbuf_tensor(f"{name}_h_lo", [P, KC, NT * P], FR))
        banks = [ctx.enter_context(nc.psum_tensor(f"{name}_z_ps{t}", [P, 512], F32)) for t in range(NT)]
        stat_ps = ctx.enter_context(nc.psum_tensor(f"{name}_stat_ps", [P, 512], F32))
        rest_ps = ctx.enter_context(nc.psum_tensor(f"{name}_rest_ps", [P, 512], F32))
        z_ready, z_act, z_dve, pads = e.sig("z_ready", "z_read_act", "z_read_dve", "h_padded")
        block = ctx.enter_context(nc.Block())

        @block.sync
        def _(sp):
            load_units(e, sp, u0 + 2, u1 + 3)

        @block.gpsimd
        def _(pool):
            for h in (e.h_hi, e.h_lo):
                pool.memset(h[:, :, T:NT * P].bitcast(F32), 0.0).then_inc(pads.sem, 1)

        @block.tensor
        def _(pe):
            def unit(g, side, first):
                u = u0 + side
                slot = u % 2
                pe.wait_ge(e.lo_done, g * 4 + (u + 1))
                for t in range(NT):
                    tok = slice(t * P, (t + 1) * P)
                    if side == 0 and not first:
                        if t % 2 == 0:
                            z_act.wait(pe, g * 3 + (t // 2 - 2))
                        else:
                            z_dve.wait(pe, g * 2 + (t // 2 - 1))
                    for kk in range(2):
                        k = 2 * side + kk
                        if first and t == 0:
                            pe.wait_ge(e.h_lo_done, KC * hn + k + 1)
                        w = slice(kk * 512, (kk + 1) * 512)
                        m = three_passes(pe, banks[t][:, :], e.h_hi[:, k, tok], e.h_lo[:, k, tok],
                                         e.w_hi[slot][:, w], e.w_lo[slot][:, w], k == 0, k == KC - 1)
                    if side == 3 and t < NT - 1:
                        m.then_inc(z_ready.sem, 1)
                m.then_inc(e.unit_used, 1)

            pads.wait(pe, 2)
            for side in range(4):
                unit(0, side, True)
                if side == 0:
                    pe.wait_ge(e.sum_done, sums)
                    for t in range(NT):
                        m = pe.matmul(stat_ps[:, t:t + 1], e.sumsq[:, t * P:(t + 1) * P], e.ones[:, 0:1],
                                      start=True, stop=True)
                    m.then_inc(e.stat_ready, 1)
            with pe.Fori(1, groups) as g:
                for side in range(4):
                    unit(g, side, False)
            pe.wait_ge(e.lo_done, u1 + 1)
            for t in range(NT):
                tok = slice(t * P, (t + 1) * P)
                for k in range(KC):
                    w = slice(k * rest, (k + 1) * rest)
                    m = three_passes(pe, rest_ps[:, t * rest:(t + 1) * rest], e.h_hi[:, k, tok], e.h_lo[:, k, tok],
                                     e.w_hi[u1 % 2][:, w], e.w_lo[u1 % 2][:, w], k == 0, k == KC - 1)
            m.then_inc(e.unit_used, 1)

        def out_of(g, t):
            if isinstance(g, int) and g < 2:
                return z[:, t, g * 512:(g + 1) * 512].rearrange("p (g a d) -> p a g d", g=4, a=2)
            return z[:, t, ds(g * 512, 512)]

        def in_of(g, t):
            if isinstance(g, int) and g < 2:
                return banks[t][:, :].rearrange("p (a g d) -> p a g d", g=4, a=2)
            return banks[t][:, :]

        @block.scalar
        def _(act):
            def evacuate(g, t):
                if t == NT - 1:
                    act.wait_ge(e.unit_used, g * 4 + (u0 + 4))
                else:
                    z_ready.wait(act, g * 4 + (t + 1))
                act.activation(out_of(g, t), in_of(g, t), ACT.Copy, scale=e.rs_col[:, t:t + 1]).then_inc(z_act.sem, 1)

            build_h_act(e, act, norm)
            for side in range(3):
                split_hi(e, act, u0 + side + 1, 0, 1024)
                if side == 0:
                    act.wait_ge(e.stat_ready, n_norm + 1)
                    act.activation(e.rms_col[:, :], stat_ps[:, 0:NT], ACT.Sqrt, bias=e.eps[:, :], scale=1.0 / D)\
                       .then_inc(e.rms_done, 1)
            act.wait_ge(e.rs_done, n_norm + 1)

            def group(g):
                split_hi4(e, act, u0, g, 0)
                for t in (0, 2, 4):
                    evacuate(g - 1, t)
                for side in range(1, 4):
                    split_hi4(e, act, u0, g, side)
            group(1)
            group(2)
            with act.Fori(3, groups) as g:
                group(g)
            split_hi(e, act, u1, 0, KC * rest)
            for t in (0, 2, 4):
                evacuate(groups - 1, t)
            split_hi(e, act, u1 + 1, 0, e.cols_of(u1 + 1))

        @block.vector
        def _(dve):
            def evacuate(g, t):
                z_ready.wait(dve, g * 4 + (t + 1))
                dve.tensor_scalar(out_of(g, t), in_of(g, t), e.rs_col[:, t:t + 1], None, ALU.mult)\
                   .then_inc(z_dve.sem, 1)

            build_h_dve(e, dve, norm, hn)
            for side in range(3):
                split_lo(e, dve, u0 + side + 1, 0, 1024)
                if side == 0:
                    dve.wait_ge(e.rms_done, n_norm + 1)
                    dve.reciprocal(e.rs_col[:, :], e.rms_col[:, :]).then_inc(e.rs_done, 1)
            dve.wait_ge(e.rs_done, n_norm + 1)

            def group(g):
                split_lo4(e, dve, u0, g, 0)
                for t in (1, 3):
                    evacuate(g - 1, t)
                for side in range(1, 4):
                    split_lo4(e, dve, u0, g, side)
            group(1)
            group(2)
            with dve.Fori(3, groups) as g:
                group(g)
            split_lo(e, dve, u1, 0, KC * rest)
            for t in (1, 3):
                evacuate(groups - 1, t)
            split_lo(e, dve, u1 + 1, 0, e.cols_of(u1 + 1))
            dve.wait_ge(e.unit_used, u1 + 1)
            dve.tensor_tensor(z[:, :, groups * 512:cols], rest_ps[:, 0:NT * rest].rearrange("p (t n) -> p t n", t=NT),
                              e.rs_col[:, :].unsqueeze(2).to_broadcast([P, NT, rest]), ALU.mult).then_inc(z_dve.sem, 1)
    z_ready.base += 4 * groups
    z_act.base += 3 * groups
    z_dve.base += 2 * groups + 1
    pads.base += 2
    e.h_n += 1
    e.norm_n += 1


def split_hi4(e, act, base, g, side):
    slot = (base + side) % 2
    act.wait_ge(e.landed[slot], g * 32 + 16 * ((base + side) // 2 + 1))
    act.wait_ge(e.unit_used, g * 4 + (base + side - 1))
    act.activation(e.w_hi[slot][:, 0:1024], e.w_stage[slot][:, 0:1024], ACT.Copy).then_inc(e.hi_done, 1)


def split_lo4(e, dve, base, g, side):
    slot = (base + side) % 2
    dve.wait_ge(e.hi_done, g * 4 + (base + side + 1))
    dve.tensor_tensor(e.w_lo[slot][:, 0:1024], e.w_stage[slot][:, 0:1024],
                      e.w_hi[slot][:, 0:1024].bitcast(F32), ALU.subtract).then_inc(e.lo_done, 1)


def rope(chain, eng, x, heads, cos, sin, t_cos, t_sin):
    v = x.rearrange("p (h d) -> p h d", d=HD)
    both = v[:, :, 0:16].rearrange("p h (a j) -> p h a j", a=2)
    shape = [P, heads, 2, 8]
    c4, s4 = (s.unsqueeze(1).unsqueeze(1).to_broadcast(shape) for s in (cos, sin))
    tc = t_cos[:, 0:heads * 16].rearrange("p (h a j) -> p h a j", a=2, j=8)
    ts_ = t_sin[:, 0:heads * 16].rearrange("p (h a j) -> p h a j", a=2, j=8)
    chain(eng.tensor_tensor(tc, both, c4, ALU.mult))
    chain(eng.tensor_tensor(ts_, both, s4, ALU.mult))
    chain(eng.tensor_tensor(v[:, :, 0:8], tc[:, :, 0, :], ts_[:, :, 1, :], ALU.subtract))
    chain(eng.tensor_tensor(v[:, :, 8:16], tc[:, :, 1, :], ts_[:, :, 0, :], ALU.add))


def turn_stage(e, name, z, jobs, q_parts, k_parts, stores):
    nc = e.nc
    q_steps, k_steps = 4 * NT * len(q_parts), 4 * NT * len(k_parts)
    n_raw = sum(job[3] == "raw" for job in jobs)
    with ExitStack() as ctx:
        t_c = [ctx.enter_context(nc.sbuf_tensor(f"{name}_rope{i}", [P, 256], F32)) for i in range(4)]
        ps = [ctx.enter_context(nc.psum_tensor(f"{name}_turn_ps{i}", [P, 512], F32)) for i in range(6)]
        q_rot, k_rot, turned, read_act, read_dve = e.sig("q_rotated", "k_rotated", "qk_turned", "turn_read_act",
                                                         "turn_read_dve")
        block = ctx.enter_context(nc.Block())

        @block.tensor
        def _(pe):
            for i, (src, _, _, need) in enumerate(jobs):
                if i >= 3:
                    (read_act if (i - 3) % 2 else read_dve).wait(pe, (i - 3) // 2 + 1)
                if need == "k":
                    k_rot.wait(pe, k_steps)
                if need == "q":
                    q_rot.wait(pe, q_steps)
                b = 2 * (i % 3)
                for t in range(NT):
                    n = src(t).shape[1]
                    dst = ps[b][0:n, t * P:(t + 1) * P] if t < NT - 1 else ps[b + 1][0:n, 0:P]
                    m = pe.transpose(dst, src(t), e.ident[:, :])
                m.then_inc(turned.sem, 1)

        def copy_out(eng, i, copy, read):
            _, dst, scale, _ = jobs[i]
            turned.wait(eng, i + 1)
            b = 2 * (i % 3)
            n = jobs[i][0](0).shape[1]
            for at in range(0, P, n):
                copy(dst[at:at + n, 0:TP], ps[b][0:n, :], scale)
                ins = copy(dst[at:at + n, TP:T], ps[b + 1][0:n, 0:TS], scale)
            ins.then_inc(read.sem, 1)

        @block.scalar
        def _(act):
            for i in range(1, len(jobs), 2):
                copy_out(act, i, lambda o, x, s: act.activation(o, x, ACT.Copy, scale=s), read_act)

        @block.vector
        def _(dve):
            for i in range(0, len(jobs), 2):
                if i == n_raw:
                    chain = Chain(dve, q_rot)
                    turned.wait(dve, n_raw) if n_raw else None
                    for t in range(NT):
                        for col, heads in q_parts:
                            rope(chain, dve, z[:, t, col:col + heads * HD], heads, e.cos[:, t, :], e.sin[:, t, :],
                                 t_c[0], t_c[1])
                copy_out(dve, i, lambda o, x, s: dve.tensor_scalar(o, x, s, None, ALU.mult), read_dve)

        @block.gpsimd
        def _(pool):
            chain = Chain(pool, k_rot)
            for t in range(NT):
                for col, heads in k_parts:
                    rope(chain, pool, z[:, t, col:col + heads * HD], heads, e.cos[:, t, :], e.sin[:, t, :],
                         t_c[2], t_c[3])

        @block.sync
        def _(sp):
            k_rot.wait(sp, k_steps)
            for dst, src in stores:
                sp.dma_start(dst, src).then_inc(e.stored, 16)
                e.stores += 1
            sp.wait_ge(e.stored, 16 * e.stores)
    for s, n in ((q_rot, q_steps), (k_rot, k_steps), (turned, len(jobs)), (read_act, len(jobs) // 2),
                 (read_dve, (len(jobs) + 1) // 2)):
        s.base += n


ORDER = (0, 1, 2, 3)
AHEAD = 3


def attention(e, name, qt, kt, v_of, bias, gate, o, accumulate):
    nc = e.nc
    with ExitStack() as ctx:
        def sb(n, shape, dt=F32):
            return ctx.enter_context(nc.sbuf_tensor(f"{name}_{n}", shape, dt))

        def psb(n):
            return ctx.enter_context(nc.psum_tensor(f"{name}_{n}", [P, 512], F32))
        qs = [sb(f"qs{c}", [P, TP]) for c in range(2)]
        probs, probs_t = [sb(f"p{i}", [P, TP]) for i in range(4)], [sb(f"pt{i}", [P, TP]) for i in range(2)]
        neg_max, sums, weight = sb("neg_max", [P, 2, 8]), sb("sums", [P, 2, 8]), sb("weight", [P, 8])
        part = sb("part", [P, 2, 8, HD])
        s_ps, t_ps = [psb(f"s_ps{i}") for i in range(4)], [psb(f"t_ps{i}") for i in range(2)]
        o_ps = [psb(f"o_ps{c}") for c in range(2)]
        q_here, s_ready, max_done, p_ready, t_ready, even_copied, odd_copied, pv_done, o_read, o_chain, o_added = e.sig(
            "q_staged", "scores_ready", "max_done", "probs_ready", "probs_turned", "even_probs_copied",
            "odd_probs_copied", "pv_done", "o_read", "o_chain", "o_added")
        links = 2 if gate else 1
        items = [(c, par, i) for c in range(2) for par in range(2) for i in ORDER]
        M = len(items)
        block = ctx.enter_context(nc.Block())

        def width_of(m):
            return (items[m % M][2] + 1) * P

        def column_of(m):
            return 4 * items[m % M][1] + items[m % M][2]

        def copied(eng, g, m):
            (odd_copied if m % 2 else even_copied).wait(eng, g * (M // 2) + (m // 2 + 1))

        def copy(eng, g, m, do):
            t_ready.wait(eng, g * M + (m + 1))
            if not first(g) or m >= 2:
                pv_done.wait(eng, g * M + (m - 1))
            do(probs_t[m % 2][:, 0:width_of(m)], t_ps[m % 2][:, 0:width_of(m)])\
                .then_inc((odd_copied if m % 2 else even_copied).sem, 1)

        def loop(eng, body):
            body(0, False)
            with eng.Fori(1, 3) as g:
                body(g, False)
            body(3, True)

        def first(g):
            return isinstance(g, int) and g == 0

        @block.gpsimd
        def _(pool):
            def add(g, c, back):
                o_read.wait(pool, g * 2 + (c + 1 - 2 * back))
                for par in range(2):
                    dst = o[:, :, ds(g * HD + (8 * c + 4 * par - back) * HD, HD)]
                    ins = pool.tensor_tensor(dst, dst, part[:, c, 4 * par:4 * par + 4, :], ALU.add)
                ins.then_inc(o_added.sem, 1)

            def body(g, last):
                for c in range(2):
                    if not first(g):
                        s_ready.wait(pool, g * M + (8 * c + 8 - M))
                    src = qt[:, 4 * c + g, 0:TP] if isinstance(g, int) else qt[:, ds(g + 4 * c, 1), 0:TP]
                    pool.tensor_copy(qs[c][:, :], src).then_inc(q_here.sem, 1)
                    if accumulate and not first(g):
                        add(g, c, 1)
                if accumulate and last:
                    for c in range(2):
                        add(g, c, 0)
            loop(pool, body)

        @block.tensor
        def _(pe):
            def scores(g, m):
                c, par, i = items[m % M]
                rows, width = slice(par * HD, (par + 1) * HD), (i + 1) * P
                if m % 8 == 0:
                    q_here.wait(pe, g * 2 + (m // 8 + 1))
                if not first(g) or m >= 4:
                    p_ready.wait(pe, g * M + (m - 3))
                bank = s_ps[m % 4]
                pe.matmul(bank[:, 0:width], qs[c][rows, i * P:(i + 1) * P], kt[rows, c, 0:width], start=True, stop=False)
                if bias is None:
                    mm = pe.matmul(bank[:, i * P:width], e.ident_b[:, :], e.causal_b[:, :], start=False, stop=True)
                else:
                    mm = pe.matmul(bank[:, 0:width], e.ident_b[:, :], bias[:, i, 0:width], start=False, stop=True)
                mm.then_inc(s_ready.sem, 1)

            def turn(g, m):
                p_ready.wait(pe, g * M + (m + 1))
                if not first(g) or m >= 2:
                    copied(pe, g, m - 2)
                for kc in range(width_of(m) // P):
                    mm = pe.transpose(t_ps[m % 2][:, kc * P:(kc + 1) * P], probs[m % 4][:, kc * P:(kc + 1) * P], e.ident[:, :])
                mm.then_inc(t_ready.sem, 1)

            def values(g, m):
                c, par, i = items[m % M]
                copied(pe, g, m)
                if m % 8 == 0 and not first(g):
                    o_read.wait(pe, g * 2 + (c - 1))
                at = column_of(m)
                for kc in range(i + 1):
                    mm = pe.matmul(o_ps[c][:, at * HD:(at + 1) * HD], probs_t[m % 2][:, kc * P:(kc + 1) * P],
                                   v_of(kc, 2 * c + par), start=kc == 0, stop=kc == i)
                mm.then_inc(pv_done.sem, 1)

            def body(g, last):
                if first(g):
                    warm_up(e, pe, o_ps[0][:, 0:P], 64)
                    for m in range(AHEAD):
                        scores(g, m)
                for m in range(M):
                    if m + AHEAD < M or not last:
                        scores(g, m + AHEAD)
                    turn(g, m)
                    if m >= 1 or not first(g):
                        values(g, m - 1)
                if last:
                    values(g, M - 1)
            loop(pe, body)

        @block.scalar
        def _(act):
            def exp(g, m):
                c, at, width = m // 8 % 2, column_of(m), width_of(m)
                max_done.wait(act, g * M + (m + 1))
                if not first(g) or m >= 4:
                    t_ready.wait(act, g * M + (m - 3))
                act.activation(probs[m % 4][:, 0:width], s_ps[m % 4][:, 0:width], ACT.Exp,
                               bias=neg_max[:, c, at:at + 1], accum_out=sums[:, c, at:at + 1]).then_inc(p_ready.sem, 1)

            def body(g, last):
                if first(g):
                    for m in range(AHEAD - 1):
                        exp(g, m)
                for m in range(M):
                    if m + AHEAD - 1 < M or not last:
                        exp(g, m + AHEAD - 1)
                    if m % 2:
                        copy(act, g, m, lambda dst, src: act.activation(dst, src, ACT.Copy))
            loop(act, body)

        @block.vector
        def _(dve):
            def maximum(g, m):
                at = column_of(m)
                s_ready.wait(dve, g * M + (m + 1))
                dve.tensor_reduce(neg_max[:, m // 8 % 2, at:at + 1], s_ps[m % 4][:, 0:width_of(m)], AX.X, ALU.max,
                                  negate=True).then_inc(max_done.sem, 1)

            def output(g, c, back):
                k = [0]

                def link(ins):
                    ins.then_inc(o_chain.sem, 1)
                    k[0] += 1
                    o_chain.wait(dve, g * (2 * links) + ((c - 2 * back) * links + k[0]))
                p_ready.wait(dve, g * M + (8 * c + 8 - M * back))
                link(dve.reciprocal(weight[:, :], sums[:, c, :]))
                if gate is not None:
                    gates, branch = gate
                    for par in range(2):
                        col = g * 3 + (24 * c + 12 * par + branch - 3 * back)
                        w = weight[:, 4 * par:4 * par + 4].unsqueeze(2)
                        ins = dve.tensor_tensor(w, w, gates[:, 0:4, ds(col, 1)], ALU.mult)
                    link(ins)
                pv_done.wait(dve, g * M + (8 * c + 8 - M * back))
                src = o_ps[c][:, :].rearrange("p (m d) -> p m d", d=HD)
                w = weight[:, :].unsqueeze(2)
                if accumulate:
                    if not first(g) and not (isinstance(g, int) and g * 2 + c - 2 * back < 2):
                        o_added.wait(dve, g * 2 + (c - 1 - 2 * back))
                    dve.tensor_tensor(part[:, c, :, :], src, w.to_broadcast([P, 8, HD]), ALU.mult).then_inc(o_read.sem, 1)
                else:
                    for par in range(2):
                        ins = dve.tensor_tensor(o[:, :, ds(g * HD + (8 * c + 4 * par - back) * HD, HD)],
                                                src[:, 4 * par:4 * par + 4, :],
                                                w[:, 4 * par:4 * par + 4, :].to_broadcast([P, 4, HD]), ALU.mult)
                    ins.then_inc(o_read.sem, 1)
                o_read.wait(dve, g * 2 + (c + 1 - 2 * back))
                assert k[0] == links, (k, links)

            def body(g, last):
                if first(g):
                    for m in range(AHEAD):
                        maximum(g, m)
                for m in range(M):
                    if m + AHEAD < M or not last:
                        maximum(g, m + AHEAD)
                    if m % 2 == 0:
                        copy(dve, g, m, dve.tensor_copy)
                    if m == 2 and not first(g):
                        output(g, 1, 1)
                    if m == 10:
                        output(g, 0, 0)
                if last:
                    output(g, 1, 0)
            loop(dve, body)
    for s, n in ((q_here, 8), (s_ready, 64), (max_done, 64), (p_ready, 64), (t_ready, 64), (even_copied, 32),
                 (odd_copied, 32), (pv_done, 64), (o_read, 8), (o_chain, 8 * links), (o_added, 8 if accumulate else 0)):
        s.base += n


def out_projection(e, name, o, o_sample, x_base):
    nc = e.nc
    u0 = e.stream.start(f"{name}.out")
    with ExitStack() as ctx:
        ot_hi = ctx.enter_context(nc.sbuf_tensor(f"{name}_ot_hi", [P, KC, T], FR))
        ot_lo = ctx.enter_context(nc.sbuf_tensor(f"{name}_ot_lo", [P, KC, T], FR))
        t_ps = [ctx.enter_context(nc.psum_tensor(f"{name}_ot_ps{i}", [P, 512], F32)) for i in range(2)]
        y_ps = [ctx.enter_context(nc.psum_tensor(f"{name}_y_ps{i}", [P, 2, 512], F32)) for i in range(2)]
        turned, hi_done, lo_done = e.sig("o_turned", "o_hi_done", "o_lo_done")
        block = ctx.enter_context(nc.Block())

        @block.sync
        def _(sp):
            load_units(e, sp, u0 + 2, min(u0 + KC + 2, e.stream.total))

        @block.gpsimd
        def _(pool):
            square_sum_pool(e, pool, x_base)

        @block.tensor
        def _(pe):
            for j in range(KC):
                if j >= 2:
                    lo_done.wait(pe, j - 1)
                for i in range(4):
                    m = pe.transpose(t_ps[j % 2][:, i * P:(i + 1) * P], o[:, i, j * P:(j + 1) * P], e.ident[:, :])
                m.then_inc(turned.sem, 1)

            def unit(q, side, first):
                slot = (u0 + side) % 2
                pe.wait_ge(e.lo_done, q * 2 + (u0 + side + 1))
                if not first:
                    pe.wait_ge(e.x_done, q * 2 + (x_base + side - 1))
                for k in range(KC):
                    if first and side == 0:
                        lo_done.wait(pe, k + 1 if k < KC - 1 else KC)
                        if k == 0:
                            lo_done.wait(pe, KC + 1)
                    for th in range(2):
                        t = slice(th * TH, (th + 1) * TH)
                        m = three_passes(pe, y_ps[side][:, th, 0:TH], e.w_hi[slot][:, k * P:(k + 1) * P],
                                         e.w_lo[slot][:, k * P:(k + 1) * P], ot_hi[:, k, t], ot_lo[:, k, t],
                                         k == 0, k == KC - 1)
                m.then_inc(e.unit_used, 1)

            for side in range(2):
                unit(0, side, True)
            with pe.Fori(1, KC // 2) as q:
                for side in range(2):
                    unit(q, side, False)

        @block.scalar
        def _(act):
            for j in range(KC):
                turned.wait(act, j + 1)
                act.activation(ot_hi[:, j, 0:TP], t_ps[j % 2][:, :], ACT.Copy).then_inc(hi_done.sem, 1)
            act.activation(ot_hi[:, :, TP:T], o_sample[:, :, :], ACT.Copy).then_inc(hi_done.sem, 1)
            split_hi(e, act, u0 + 1, 0, KC * P)
            with act.Fori(1, KC // 2) as q:
                for side in range(2):
                    split_hi(e, act, u0 + side, q, KC * P)
            if u0 + KC < e.stream.total:
                split_hi(e, act, u0 + KC, 0, e.cols_of(u0 + KC))

        @block.vector
        def _(dve):
            for j in range(KC):
                hi_done.wait(dve, j + 1)
                dve.tensor_tensor(ot_lo[:, j, 0:TP], t_ps[j % 2][:, :], ot_hi[:, j, 0:TP].bitcast(F32), ALU.subtract)\
                   .then_inc(lo_done.sem, 1)
            hi_done.wait(dve, KC + 1)
            dve.tensor_tensor(ot_lo[:, :, TP:T], o_sample[:, :, :], ot_hi[:, :, TP:T].bitcast(F32), ALU.subtract)\
               .then_inc(lo_done.sem, 1)
            split_lo(e, dve, u0 + 1, 0, KC * P)

            def x_of(u, side, i):
                dve.wait_ge(e.unit_used, u)
                if isinstance(i, int):
                    xi = e.x[:, i, :].rearrange("p (a t) -> p a t", a=2)
                else:
                    xi = e.x[:, ds(i, 1), :].rearrange("p o (a t) -> p (o a) t", a=2)
                dve.tensor_tensor(xi, y_ps[side][:, :, 0:TH], xi, ALU.add).then_inc(e.x_done, 1)

            with dve.Fori(1, KC // 2) as q:
                split_lo(e, dve, u0, q, KC * P)
                x_of(q * 2 + (u0 - 1), 0, q * 2 - 2)
                split_lo(e, dve, u0 + 1, q, KC * P)
                x_of(q * 2 + u0, 1, q * 2 - 1)
            if u0 + KC < e.stream.total:
                split_lo(e, dve, u0 + KC, 0, e.cols_of(u0 + KC))
            x_of(u0 + KC - 1, 0, KC - 2)
            x_of(u0 + KC, 1, KC - 1)
    turned.base += KC
    hi_done.base += KC + 1
    lo_done.base += KC + 1
    e.x_rows += KC


def compress(e, z, kc_t, vc_prompt, vc_sample):
    nc = e.nc
    NB, PB = 41, 8
    LG = 8
    with ExitStack() as ctx:
        def sb(n, shape, dt=F32):
            return ctx.enter_context(nc.sbuf_tensor(f"cmp_{n}", shape, dt))

        def psb(n, shape=(P, 512)):
            return ctx.enter_context(nc.psum_tensor(f"cmp_{n}", list(shape), F32))
        kt = sb("kt", [P, 2, 2, NB, 64])
        w1 = [[sb(f"w1_{s}{par}", [P, LG * P]) for par in range(2)] for s in range(2)]
        w2 = sb("w2", [P, 2, HD])
        pages = [sb(f"page{i}", [P, 512]) for i in range(4)]
        pos_rows = sb("pos_rows", [64, 2, 2, HD])
        bias = sb("bias", [P, 4])
        hidden = [sb(f"hidden{i}", [P, 2, NB - 1]) for i in range(4)]
        t_ps = [psb(f"t_ps{i}") for i in range(2)]
        pre_ps = [psb(f"pre_ps{i}") for i in range(4)]
        k_ps, v_ps = psb("k_ps"), psb("v_ps")
        zeroed, w1_in0, w1_in1, w1_used, pos_in, page_in0, page_in1, page_in2, page_in3, turned, kt_done, bias_done, \
            hid_done, small_done = e.sig(
                "cmp_zeroed", "cmp_w1_landed0", "cmp_w1_landed1", "cmp_w1_used", "cmp_pos_landed", "cmp_page_landed0",
                "cmp_page_landed1", "cmp_page_landed2", "cmp_page_landed3", "cmp_turned", "cmp_kt_done",
                "cmp_bias_done", "cmp_hidden_done", "cmp_small_done")
        w1_in, page_in = (w1_in0, w1_in1), (page_in0, page_in1, page_in2, page_in3)
        block = ctx.enter_context(nc.Block())
        TURNS = 22

        @block.gpsimd
        def _(pool):
            for s in range(2):
                for par in range(2):
                    rows = slice((1 - par) * HD, (2 - par) * HD)
                    pool.memset(w1[s][par][rows, :], 0.0).then_inc(zeroed.sem, 1)

        @block.sync
        def _(sp):
            sp.dma_start(pos_rows[:, :, 0, :], e.nsa_cmp_pos[0]).then_inc(pos_in.sem, 16)
            sp.dma_start(pos_rows[:, :, 1, :], e.nsa_cmp_pos[0]).then_inc(pos_in.sem, 16)
            sp.dma_start(w2[:, :, :], e.nsa_cmp_w2[0].rearrange("c h d -> h c d")).then_inc(pos_in.sem, 16)
            for i in range(16):
                page = sp.value_load(e.table[0:1, i:i + 1], min_val=0, max_val=e.cache_nsa_cmp.shape[1] - 1)
                if i >= 4:
                    turned.wait(sp, 6 + i - 3)
                sp.dma_start(pages[i % 4][:, :], e.cache_nsa_cmp[0, ds(page, 1)].rearrange("o p c k d -> (o p) (c k d)"))\
                  .then_inc(page_in[i % 4].sem, 16)

        @block.scalar
        def _(act):
            w1v = e.nsa_cmp_w1[0].rearrange("c l d h -> c d l h")
            for i in range(16):
                c, lg = i // 8, i % 8
                if i >= 2:
                    w1_used.wait(act, i - 1)
                for par in range(2):
                    act.dma_start(w1[i % 2][par][par * HD:(par + 1) * HD, :].rearrange("p (l h) -> p l h", l=LG),
                                  w1v[c, :, lg * LG:(lg + 1) * LG, :]).then_inc(w1_in[i % 2].sem, 16)
            for i in range(4):
                w1_used.wait(act, 8 * (i // 2 + 1))
                bias_done.wait(act, i + 1)
                act.activation(hidden[i][:, :, :], pre_ps[i][:, 0:2 * NB].rearrange("p (c n) -> p c n", c=2)[:, :, 0:NB - 1],
                               ACT.Gelu_apprx_tanh, bias=bias[:, i:i + 1]).then_inc(hid_done.sem, 1)

        @block.tensor
        def _(pe):
            n = 0
            for c in range(2):
                for chunk in range(2):
                    if n >= 2:
                        kt_done.wait(pe, n - 1)
                    for t in range(4):
                        col = 1024 + c * 256 + chunk * P
                        m = pe.transpose(t_ps[n % 2][:, t * P:(t + 1) * P], z[:, t, col:col + P], e.ident[:, :])
                    m.then_inc(turned.sem, 1)
                    n += 1
            pos_in.wait(pe, 48)
            for c in range(2):
                kt_done.wait(pe, n - 1)
                pe.transpose(t_ps[n % 2][:, 0:64], pos_rows[:, c, :, :].rearrange("p a d -> p (a d)"), e.ident[0:64, 0:64])\
                  .then_inc(turned.sem, 1)
                n += 1
            for i in range(16):
                kt_done.wait(pe, n - 1)
                page_in[i % 4].wait(pe, 16 * (i // 4 + 1))
                for j in range(4):
                    m = pe.transpose(t_ps[n % 2][:, j * P:(j + 1) * P], pages[i % 4][:, j * P:(j + 1) * P], e.ident[:, :])
                m.then_inc(turned.sem, 1)
                n += 1
            kt_done.wait(pe, TURNS)
            zeroed.wait(pe, 4)
            for c in range(2):
                def group(q, side, first=False, last=False):
                    w1_in[side].wait(pe, q * 32 + 32 * (4 * c + 1))
                    for l in range(LG):
                        for par in range(2):
                            at = q * (2 * LG) + (side * LG + l)
                            m = pe.matmul(pre_ps[2 * c + par][:, 0:2 * NB], w1[side][par][:, l * P:(l + 1) * P],
                                          kt[:, c, :, :, ds(at, 1)], start=first and side == 0 and l == 0,
                                          stop=last and side == 1 and l == LG - 1)
                    m.then_inc(w1_used.sem, 1)
                for side in range(2):
                    group(0, side, first=True)
                with pe.Fori(1, 3) as q:
                    for side in range(2):
                        group(q, side)
                for side in range(2):
                    group(3, side, last=True)
            w2_k, w2_v = w2[:, 0, :], w2[:, 1, :]
            for par in range(2):
                hid_done.wait(pe, par + 1)
                m = pe.matmul(k_ps[par * HD:(par + 1) * HD, 0:2 * (NB - 1)], w2_k, hidden[par][:, :, :].rearrange("p c n -> p (c n)"),
                              start=True, stop=True)
            m.then_inc(small_done.sem, 1)
            for chunk in range(2):
                for par in range(2):
                    hid_done.wait(pe, 3 + par)
                    kv = 2 * chunk + par
                    pe.matmul(v_ps[0:PB, kv * HD:(kv + 1) * HD], hidden[2 + par][:, chunk, 0:PB], w2_v, start=True, stop=True)
            for chunk in range(2):
                for par in range(2):
                    kv = 2 * chunk + par
                    m = pe.matmul(v_ps[0:32, 256 + kv * HD:256 + (kv + 1) * HD], hidden[2 + par][:, chunk, PB:NB - 1], w2_v,
                                  start=True, stop=True)
            m.then_inc(small_done.sem, 1)

        @block.vector
        def _(dve):
            n = 0
            for c in range(2):
                for chunk in range(2):
                    turned.wait(dve, n + 1)
                    dve.tensor_copy(kt[:, c, chunk, 0:PB, :].rearrange("p n l -> p (n l)"), t_ps[n % 2][:, :])\
                       .then_inc(kt_done.sem, 1)
                    n += 1
            for c in range(2):
                turned.wait(dve, n + 1)
                dve.tensor_copy(kt[:, c, :, NB - 1, :], t_ps[n % 2][:, 0:64].unsqueeze(1).to_broadcast([P, 2, 64]))\
                   .then_inc(kt_done.sem, 1)
                n += 1
            for i in range(16):
                turned.wait(dve, n + 1)
                dst = kt[:, :, :, PB + 2 * i:PB + 2 * i + 2, :].rearrange("p c k n l -> p (c k) (n l)")
                dve.tensor_copy(dst, t_ps[n % 2][:, :].rearrange("p (j s) -> p j s", j=4)).then_inc(kt_done.sem, 1)
                n += 1
            for i in range(4):
                w1_used.wait(dve, 8 * (i // 2 + 1))
                dve.tensor_copy(bias[:, i:i + 1], pre_ps[i][:, NB - 1:NB]).then_inc(bias_done.sem, 1)
            small_done.wait(dve, 1)
            dve.tensor_copy(kc_t[:, :, :].rearrange("p c n -> p (c n)"), k_ps[:, 0:2 * (NB - 1)])
            small_done.wait(dve, 2)
            dve.tensor_copy(vc_prompt[0:PB, :], v_ps[0:PB, 0:256])
            dve.tensor_copy(vc_sample[0:32, :], v_ps[0:32, 256:512])


def compressed_attention(e, qt_raw, kc_t, vc_prompt, gates, o):
    nc = e.nc
    with ExitStack() as ctx:
        def sb(n, shape, dt=F32):
            return ctx.enter_context(nc.sbuf_tensor(f"ca_{n}", shape, dt))

        def psb(n):
            return ctx.enter_context(nc.psum_tensor(f"ca_{n}", [P, 512], F32))
        kc_bd, v_bd = sb("kc_bd", [P, 2, 2, 8]), sb("v_bd", [P, HEADS, HD])
        s_sb = [sb(f"s{i}", [P, HEADS, 8]) for i in range(4)]
        m_sb, r_sb, p_t = sb("m", [P, HEADS]), sb("r", [P, HEADS]), [sb(f"pt{i}", [P, P]) for i in range(2)]
        s_ps, t_ps, v_ps = [psb("s_ps0"), psb("s_ps1")], psb("t_ps"), psb("v_ps")
        o_ps = [psb(f"o_ps{i}") for i in range(4)]
        step, s_ready, v_ready, e_done, p_done, turned, t_copied, o_ready, o_copied, zeroed = e.sig(
            "ca_step", "ca_scores", "ca_values_spread", "ca_exp_done", "ca_probs_done", "ca_turned", "ca_turn_copied",
            "ca_out_ready", "ca_out_copied", "ca_keys_spread")
        block = ctx.enter_context(nc.Block())

        @block.gpsimd
        def _(pool):
            chain = Chain(pool, zeroed)
            chain(pool.memset(kc_bd[:, :, :, :], 0.0))
            for par in range(2):
                rows = slice(par * HD, (par + 1) * HD)
                chain(pool.tensor_copy(kc_bd[rows, :, par, :], kc_t[rows, :, 0:8]))

        @block.tensor
        def _(pe):
            pe.matmul(v_ps[:, 0:256], e.rep[0:8, :], vc_prompt[0:8, :], start=True, stop=True).then_inc(v_ready.sem, 1)
            zeroed.wait(pe, 3)

            def scores(i):
                if i >= 2:
                    e_done.wait(pe, i - 1)
                for j in range(8):
                    m = pe.matmul(s_ps[i % 2][:, j * 16:(j + 1) * 16], qt_raw[:, j, i * P:(i + 1) * P],
                                  kc_bd[:, j // 4, :, :].rearrange("p a n -> p (a n)"), start=True, stop=True)
                m.then_inc(s_ready.sem, 1)
            scores(0)
            scores(1)
            for i in range(4):
                p_done.wait(pe, i + 1)
                if i >= 1:
                    t_copied.wait(pe, i)
                pe.transpose(t_ps[:, 0:P], s_sb[i][:, :, :].rearrange("p h n -> p (h n)"), e.ident[:, :]).then_inc(turned.sem, 1)
                if i + 2 < 4:
                    scores(i + 2)
                t_copied.wait(pe, i + 1)
                for half in range(2):
                    b = 2 * (i % 2) + half
                    if i >= 2:
                        o_copied.wait(pe, 2 * (i - 2) + half + 1)
                    pe.matmul(o_ps[b][:, :], p_t[i % 2][:, :], v_bd[:, 8 * half:8 * half + 8, :].rearrange("p h d -> p (h d)"),
                              start=True, stop=True).then_inc(o_ready.sem, 1)

        @block.scalar
        def _(act):
            for i in range(4):
                step.wait(act, 4 + 11 * i + 3)
                act.activation(s_sb[i][:, :, :], s_sb[i][:, :, :], ACT.Exp).then_inc(e_done.sem, 1)

        @block.vector
        def _(dve):
            chain = Chain(dve, step)
            v_ready.wait(dve, 1)
            for kv in range(KV):
                chain(dve.tensor_tensor(v_bd[:, 4 * kv:4 * kv + 4, :],
                                        v_ps[:, kv * HD:(kv + 1) * HD].unsqueeze(1).to_broadcast([P, 4, HD]),
                                        e.hsel[:, 4 * kv:4 * kv + 4].unsqueeze(2).to_broadcast([P, 4, HD]), ALU.mult))
            for i in range(4):
                s = s_sb[i]
                s_ready.wait(dve, i + 1)
                chain(dve.tensor_tensor(s[:, :, :], s_ps[i % 2][:, 0:P].rearrange("p (h n) -> p h n", n=8),
                                        e.cadd[:, i, :].unsqueeze(1).to_broadcast([P, HEADS, 8]), ALU.add))
                chain(dve.tensor_reduce(m_sb[:, :], s[:, :, :], AX.X, ALU.max))
                chain(dve.tensor_tensor(s[:, :, :], s[:, :, :], m_sb[:, :].unsqueeze(2).to_broadcast([P, HEADS, 8]),
                                        ALU.subtract))
                e_done.wait(dve, i + 1)
                chain(dve.tensor_tensor(s[:, :, :], s[:, :, :], e.c01[:, i, :].unsqueeze(1).to_broadcast([P, HEADS, 8]),
                                        ALU.mult))
                chain(dve.tensor_reduce(r_sb[:, :], s[:, :, :], AX.X, ALU.add))
                chain(dve.tensor_scalar(r_sb[:, :], r_sb[:, :], 1e-30, None, ALU.max))
                chain(dve.reciprocal(r_sb[:, :], r_sb[:, :]))
                g_view = gates[:, i, :].rearrange("p (c a g r) -> p c g a r", c=2, a=2, g=4, r=3)
                for c in range(2):
                    chain(dve.tensor_tensor(r_sb[:, 8 * c:8 * c + 8].rearrange("p (g a) -> p g a", a=2),
                                            r_sb[:, 8 * c:8 * c + 8].rearrange("p (g a) -> p g a", a=2),
                                            g_view[:, c, :, :, 0], ALU.mult))
                chain(dve.tensor_tensor(s[:, :, :], s[:, :, :], r_sb[:, :].unsqueeze(2).to_broadcast([P, HEADS, 8]), ALU.mult))
                dve.memset(e.start_mark[:, :], 0.0).then_inc(p_done.sem, 1)
                turned.wait(dve, i + 1)
                chain(dve.tensor_copy(p_t[i % 2][:, :], t_ps[:, 0:P]))
                dve.memset(e.start_mark2[:, :], 0.0).then_inc(t_copied.sem, 1)
                for half in range(2):
                    o_ready.wait(dve, 2 * i + half + 1)
                    dve.tensor_copy(o[:, i, half * 512:(half + 1) * 512], o_ps[2 * (i % 2) + half][:, :])\
                       .then_inc(o_copied.sem, 1)


def sample_setup(e, qt_raw, qt, sb_):
    nc = e.nc
    spread, = e.sig("sample_q_spread")
    block_ctx = ExitStack()
    with block_ctx:
        block = block_ctx.enter_context(nc.Block())

        @block.vector
        def _(dve):
            dve.memset(sb_.qbd[:, :], 0.0)
            if qt_raw is not None:
                dve.memset(sb_.qz[:, :], 0.0)
            dve.memset(e.start_mark[:, :], 0.0).then_inc(spread.sem, 1)
            spread.wait(dve, 1)
            for c in range(2):
                for par in range(2):
                    rows, at = slice(par * HD, (par + 1) * HD), 8 * c + 4 * par
                    src = qt[rows, 4 * c:4 * c + 4, TP:T].rearrange("p g b -> p b g")
                    dst = sb_.qbd[rows, 0:2176].rearrange("p (b s) -> p b s", s=272)[:, :, c * P + at:c * P + at + 4]
                    dve.tensor_copy(dst, src)
                    if qt_raw is not None:
                        src = qt_raw[rows, 4 * c:4 * c + 4, TP:T].rearrange("p g b -> p b g")
                        dst = sb_.qz[rows, c * P:(c + 1) * P].rearrange("p (b h) -> p b h", h=16)[:, :, at:at + 4]
                        dve.tensor_copy(dst, src)
    spread.base += 1


def sample_attention(e, name, sb_, rows_of, kt_new, v_new, gate_w, first, bias=None, table=None):
    nc = e.nc
    with ExitStack() as ctx:
        def sb(n, shape, dt=F32):
            return ctx.enter_context(nc.sbuf_tensor(f"{name}_{n}", shape, dt))

        def psb(n):
            return ctx.enter_context(nc.psum_tensor(f"{name}_{n}", [P, 512], F32))
        rows, kt = sb("rows", [P, 16, 512]), sb("kt", [P, 2, 2, 256])
        prob, p_new, neg_max, r = sb("prob", [P, 257]), sb("p_new", [P, TS]), sb("neg_max", [P, 1]), sb("r", [P, 1])
        p_t, p_nt = sb("p_t", [P, 2, P]), sb("p_nt", [TS, P])
        k_ps = [psb(f"k_ps{i}") for i in range(2)]
        s_ps, t_ps, o_ps = psb("s_ps"), psb("t_ps"), [psb(f"o_ps{i}") for i in range(2)]
        landed = e.sig(*[f"sample_rows_landed{i}" for i in range(4)])
        turned, copied, s_ready, used, step, exp_done, p_ready, p_turned, p_copied, o_ready = e.sig(
            "sample_k_turned", "sample_k_copied", "sample_scores", "sample_k_used", "sample_step", "sample_exp_done",
            "sample_probs", "sample_probs_turned", "sample_probs_copied", "sample_out_ready")
        block = ctx.enter_context(nc.Block())

        @block.sync
        def _(sp):
            for i in range(16):
                page = None
                if table is not None:
                    page = sp.value_load(table[0:1, i:i + 1], min_val=0, max_val=e.cache_nsa_slc.shape[1] - 1)
                if i >= 4:
                    landed[i % 4].wait(sp, 16 * (i // 4))
                sp.dma_start(rows[:, i, :], rows_of(i, page)).then_inc(landed[i % 4].sem, 16)

        def score(pe, b):
            copied.wait(pe, b + 1)
            for c in range(2):
                m = pe.matmul(s_ps[:, 0:256], sb_.qbd[:, b * 256 + c * P:b * 256 + (c + 1) * P], kt[:, b % 2, c, :],
                              start=b == 0 and c == 0, stop=b == TS - 1 and c == 1 and bias is None)
            m.then_inc(used.sem, 1)

        @block.tensor
        def _(pe):
            for b in range(TS):
                if b >= 2:
                    copied.wait(pe, b - 1)
                for half in range(2):
                    i = 2 * b + half
                    landed[i % 4].wait(pe, 16 * (i // 4 + 1))
                    for c in range(2):
                        m = pe.transpose(k_ps[b % 2][:, c * 256 + half * P:c * 256 + (half + 1) * P],
                                         rows[:, i, c * P:(c + 1) * P], e.ident[:, :])
                m.then_inc(turned.sem, 1)
                if b >= 1:
                    score(pe, b - 1)
            score(pe, TS - 1)
            if bias is not None:
                pe.matmul(s_ps[:, 0:256], bias[0], bias[1][:, 0:256], start=False, stop=True)
            for b in range(TS):
                for c in range(2):
                    m = pe.matmul(s_ps[:, 256:257], sb_.qbd[:, b * 256 + c * P:b * 256 + (c + 1) * P],
                                  kt_new[:, c, b:b + 1], start=b == 0 and c == 0, stop=b == TS - 1 and c == 1 and bias is None)
            if bias is not None:
                m = pe.matmul(s_ps[:, 256:257], bias[0], bias[1][:, 256:257], start=False, stop=True)
            m.then_inc(s_ready.sem, 1)
            p_ready.wait(pe, 1)
            for half in range(2):
                pe.transpose(t_ps[:, half * P:(half + 1) * P], prob[:, half * P:(half + 1) * P], e.ident[:, :])
            pe.transpose(t_ps[0:TS, 256:256 + P], p_new[:, :], e.ident[:, :]).then_inc(p_turned.sem, 1)
            p_copied.wait(pe, 1)
            for c in range(2):
                for i in range(16):
                    b, half = i // 2, i % 2
                    pe.matmul(o_ps[c][:, b * 16:(b + 1) * 16], rows[:, i, 256 + c * P:256 + (c + 1) * P],
                              p_t[:, half, b * 16:(b + 1) * 16], start=i == 0, stop=False, skip_group_check=True)
                m = pe.matmul(o_ps[c][:, 0:P], v_new[:, c * P:(c + 1) * P], p_nt[:, :], start=False, stop=True,
                              skip_group_check=True)
            m.then_inc(o_ready.sem, 1)

        @block.scalar
        def _(act):
            step.wait(act, 1)
            act.activation(prob[:, :], s_ps[:, 0:257], ACT.Exp, bias=neg_max[:, :], accum_out=r[:, :]).then_inc(exp_done.sem, 1)

        @block.vector
        def _(dve):
            for b in range(TS):
                turned.wait(dve, b + 1)
                if b >= 2:
                    used.wait(dve, b - 1)
                dve.tensor_copy(kt[:, b % 2, :, :].rearrange("p c s -> p (c s)"), k_ps[b % 2][:, :]).then_inc(copied.sem, 1)
            chain = Chain(dve, step)
            s_ready.wait(dve, 1)
            chain(dve.tensor_reduce(neg_max[:, :], s_ps[:, 0:257], AX.X, ALU.max, negate=True))
            exp_done.wait(dve, 1)
            chain(dve.reciprocal(r[:, :], r[:, :]))
            if gate_w is not None:
                chain(dve.tensor_tensor(r[:, :], r[:, :], gate_w, ALU.mult))
            chain(dve.tensor_scalar(prob[:, :], prob[:, :], r[:, :], None, ALU.mult))
            dve.tensor_scalar(p_new[:, :], e.esel[:, :], prob[:, 256:257], None, ALU.mult).then_inc(p_ready.sem, 1)
            p_turned.wait(dve, 1)
            dve.tensor_copy(p_t[:, :, :].rearrange("p a k -> p (a k)"), t_ps[:, 0:256])
            dve.tensor_copy(p_nt[:, :], t_ps[0:TS, 256:256 + P]).then_inc(p_copied.sem, 1)
            o_ready.wait(dve, 1)
            for c in range(2):
                if first:
                    dve.tensor_copy(sb_.o_t[:, c, :], o_ps[c][:, 0:P])
                else:
                    dve.tensor_tensor(sb_.o_t[:, c, :], o_ps[c][:, 0:P], sb_.o_t[:, c, :], ALU.add)
    for s in landed:
        s.base += 64
    for s, n in ((turned, 8), (copied, 8), (s_ready, 1), (used, 8), (step, 3 + (gate_w is not None)), (exp_done, 1),
                 (p_ready, 1), (p_turned, 1), (p_copied, 1), (o_ready, 1)):
        s.base += n


def sample_compressed(e, sb_, kc_t, vc_sample, gate_w):
    nc = e.nc
    with ExitStack() as ctx:
        s, m, r = (ctx.enter_context(nc.sbuf_tensor(f"sc_{n}", shape, F32)) for n, shape in
                   (("s", [P, 32]), ("m", [P, 1]), ("r", [P, 1])))
        p_t = ctx.enter_context(nc.sbuf_tensor("sc_pt", [32, P], F32))
        s_ps, t_ps, o_ps = (ctx.enter_context(nc.psum_tensor(f"sc_{n}", [P, 512], F32)) for n in ("s_ps", "t_ps", "o_ps"))
        step, exp_done, pe_step = e.sig("sc_step", "sc_exp_done", "sc_turned")
        block = ctx.enter_context(nc.Block())

        @block.tensor
        def _(pe):
            for c in range(2):
                mm = pe.matmul(s_ps[:, 0:32], sb_.qz[:, c * P:(c + 1) * P], kc_t[:, c, 8:40], start=c == 0, stop=c == 1)
            mm.then_inc(pe_step.sem, 1)
            step.wait(pe, 5)
            pe.transpose(t_ps[0:32, 0:P], s[:, :], e.ident[:, :]).then_inc(pe_step.sem, 1)
            step.wait(pe, 6)
            for c in range(2):
                mm = pe.matmul(o_ps[:, c * P:(c + 1) * P], vc_sample[0:32, c * P:(c + 1) * P], p_t[:, :], start=True, stop=True)
            mm.then_inc(pe_step.sem, 1)

        @block.scalar
        def _(act):
            step.wait(act, 2)
            act.activation(s[:, :], s[:, :], ACT.Exp, bias=m[:, :], accum_out=r[:, :]).then_inc(exp_done.sem, 1)

        @block.vector
        def _(dve):
            chain = Chain(dve, step)
            pe_step.wait(dve, 1)
            chain(dve.tensor_tensor(s[:, :], s_ps[:, 0:32], e.bmask[:, :], ALU.add))
            chain(dve.tensor_reduce(m[:, :], s[:, :], AX.X, ALU.max, negate=True))
            exp_done.wait(dve, 1)
            chain(dve.reciprocal(r[:, :], r[:, :]))
            chain(dve.tensor_tensor(r[:, :], r[:, :], gate_w, ALU.mult))
            chain(dve.tensor_scalar(s[:, :], s[:, :], r[:, :], None, ALU.mult))
            pe_step.wait(dve, 2)
            chain(dve.tensor_copy(p_t[:, :], t_ps[0:32, 0:P]))
            pe_step.wait(dve, 3)
            chain(dve.tensor_tensor(sb_.o_t[:, :, :].rearrange("p c n -> p (c n)"), o_ps[:, 0:256],
                                    sb_.o_t[:, :, :].rearrange("p c n -> p (c n)"), ALU.add))
    step.base += 7
    exp_done.base += 1
    pe_step.base += 3


def sample_finish(e, sb_, o_sample):
    nc = e.nc
    with ExitStack() as ctx:
        block = ctx.enter_context(nc.Block())

        @block.vector
        def _(dve):
            v = sb_.o_t[:, :, :].rearrange("p c (b h) -> p c h b", h=16)
            for c in range(2):
                for par in range(2):
                    for odd in range(2):
                        at, tile = 8 * c + 4 * par + odd, 4 * c + 2 * par
                        dve.tensor_copy(o_sample[odd * HD:(odd + 1) * HD, tile:tile + 2, :],
                                        v[par * HD:(par + 1) * HD, c, at:at + 3:2, :])


def nsa_regions(e):
    projection_regions(e, "nsa", e.w_nsa_in[0], NSA_COLS, 5)
    out_regions(e, "nsa", e.w_nsa_out[0])


def nsa(e):
    nc = e.nc
    with ExitStack() as mix:
        def sb(n, shape, dt=F32, ctx=mix):
            return ctx.enter_context(nc.sbuf_tensor(f"nsa_{n}", shape, dt))
        z = sb("z", [P, NT, NSA_COLS])
        o, o_sample = sb("o", [P, 4, D]), sb("o_sample", [P, KC, TS])
        gates, kc_t = sb("gates", [P, NT, 3 * HEADS]), sb("kc_t", [P, 2, 40])
        vc_prompt, vc_sample = sb("vc_prompt", [8, 256]), sb("vc_sample", [32, 256])
        kn = [sb(f"k_new{i}", [P, 2, TS]) for i in range(2)]
        g_bh = sb("g_bh", [P, 3])
        projection(e, "nsa", 1, z, 5, NSA_COLS)
        gates_done, g_copied, g_spread = e.sig("gates_done", "gates_masked", "gates_spread")
        with ExitStack() as ctx:
            g_ps = ctx.enter_context(nc.psum_tensor("g_ps", [P, 512], F32))
            g_m = ctx.enter_context(nc.sbuf_tensor("g_m", [P, 3, HEADS], F32))
            block = ctx.enter_context(nc.Block())

            @block.sync
            def _(sp):
                out = e.nsa_cmp_p[0, 0].rearrange("(t p) c k d -> p t (c k d)", p=P)
                for t in range(4):
                    sp.dma_start(out[:, t, :], z[:, t, 1024:1536]).then_inc(e.stored, 16)
                sp.dma_start(e.nsa_cmp_s[0].rearrange("b s c k d -> (b s) (c k d)"), z[0:TS, 4, 1024:1536]).then_inc(e.stored, 16)
                sp.dma_start(e.nsa_win_s[0, :, 0:255], e.state_nsa_win[0, :, 1:256]).then_inc(e.stored, 16)
                e.stores += 6

            @block.scalar
            def _(act):
                act.activation(gates[:, :, :], z[:, :, 2560:NSA_COLS], ACT.Sigmoid).then_inc(gates_done.sem, 1)

            @block.tensor
            def _(pe):
                gates_done.wait(pe, 1)
                pe.matmul(g_ps[:, 0:48], e.esel_t[0:TS, :], gates[0:TS, 4, :], start=True, stop=True).then_inc(g_spread.sem, 1)

            @block.vector
            def _(dve):
                g_spread.wait(dve, 1)
                dve.tensor_tensor(g_m[:, :, :], g_ps[:, 0:48].rearrange("p (h r) -> p r h", r=3),
                                  e.hmask[:, :].unsqueeze(1).to_broadcast([P, 3, HEADS]), ALU.mult).then_inc(g_copied.sem, 1)
                g_copied.wait(dve, 1)
                dve.tensor_reduce(g_bh[:, :], g_m[:, :, :], AX.X, ALU.add)
        compress(e, z, kc_t, vc_prompt, vc_sample)
        sb_ = SampleBuffers(sb("qbd", [P, 2304]), sb("qz", [P, 256]), sb("o_t", [P, 2, P]))
        with ExitStack() as turns:
            qt_raw, qt = sb("qt_raw", [P, 8, T], ctx=turns), sb("qt", [P, 8, T], ctx=turns)
            kts = [sb(f"kt{i}", [P, 2, T], ctx=turns) for i in range(2)]
            k_cols = (1536, 2048)
            jobs = [(lambda t, j=j: z[:, t, j * P:(j + 1) * P], qt_raw[:, j, :], SCALE, "raw") for j in range(8)]
            jobs += [(lambda t, c=c, i=i: z[:, t, k_cols[i] + c * P:k_cols[i] + (c + 1) * P], kts[i][:, c, :], 1.0, "k")
                     for i in range(2) for c in range(2)]
            jobs += [(lambda t, j=j: z[:, t, j * P:(j + 1) * P], qt[:, j, :], SCALE, "q") for j in range(8)]
            stores = []
            for i, (out_p, out_s) in enumerate(((e.nsa_slc_p, e.nsa_slc_s), (e.nsa_win_p, None))):
                v = out_p[0, 0].rearrange("(t p) c k d -> p t (c k d)", p=P)
                stores += [(v[:, t, :], z[:, t, k_cols[i]:k_cols[i] + 512]) for t in range(4)]
                if out_s is not None:
                    stores.append((out_s[0].rearrange("b s c k d -> (b s) (c k d)"), z[0:TS, 4, k_cols[i]:k_cols[i] + 512]))
                else:
                    stores.append((e.nsa_win_s[0, :, 255].rearrange("b c k d -> b (c k d)"), z[0:TS, 4, k_cols[i]:k_cols[i] + 512]))
            turn_stage(e, "nsa", z, jobs, [(0, HEADS)], [(c, KV) for c in k_cols], stores)
            compressed_attention(e, qt_raw, kc_t, vc_prompt, gates, o)
            for i in range(2):
                attention(e, ("slc", "win")[i], qt, kts[i], lambda kc, kv, i=i: z[:, kc, k_cols[i] + 256 + kv * HD:k_cols[i] + 256 + (kv + 1) * HD],
                          None, (gates, 1 + i), o, True)
            with ExitStack() as ctx:
                block = ctx.enter_context(nc.Block())

                @block.vector
                def _(dve):
                    for i in range(2):
                        dve.tensor_copy(kn[i][:, :, :], kts[i][:, :, TP:T])
            sample_setup(e, qt_raw, qt, sb_)
        sample_attention(e, "sslc", sb_, lambda i, page: e.cache_nsa_slc[0, ds(page, 1)].rearrange("o p c k d -> (o p) (c k d)"),
                         kn[0], z[0:TS, 4, 1792:2048], g_bh[:, 1:2], True, table=e.table)
        sample_attention(e, "swin", sb_, lambda i, page: e.state_nsa_win[0, i // 2, (i % 2) * P:(i % 2 + 1) * P].rearrange("p c k d -> p (c k d)"),
                         kn[1], z[0:TS, 4, 2304:2560], g_bh[:, 2:3], False)
        sample_compressed(e, sb_, kc_t, vc_sample, g_bh[:, 0:1])
        sample_finish(e, sb_, o_sample)
        out_projection(e, "nsa", o, o_sample, e.x_rows)



N_IDX = 8
TOPK = P
TOPK_S = 64
TAKEN = -3.0e38
IDX_SCALE = N_IDX ** -0.5


def index_prompt(e, z, qi_t, ki_t, wi, bias):
    nc = e.nc
    with ExitStack() as ctx:
        def sb(n, shape, dt=F32):
            return ctx.enter_context(nc.sbuf_tensor(f"ix_{n}", shape, dt))
        relu, score, top = [sb(f"relu{i}", [P, TP]) for i in range(2)], sb("score", [P, 4, TP]), sb("top", [P, 8])
        ps = [ctx.enter_context(nc.psum_tensor(f"ix_ps{i}", [P, 512], F32)) for i in range(2)]
        s_ready, r_done, summed, step = e.sig("ix_scores", "ix_relu_done", "ix_summed", "ix_step")
        items = [(i, h) for i in range(1, 4) for h in range(N_IDX)]
        block = ctx.enter_context(nc.Block())

        @block.tensor
        def _(pe):
            for n, (i, h) in enumerate(items):
                if n >= 2:
                    r_done.wait(pe, n - 1)
                rows = slice((h % 2) * HD, (h % 2 + 1) * HD)
                pe.matmul(ps[n % 2][:, 0:(i + 1) * P], qi_t[rows, h // 2, i * P:(i + 1) * P], ki_t[rows, 0, 0:(i + 1) * P],
                          start=True, stop=True).then_inc(s_ready.sem, 1)

        @block.scalar
        def _(act):
            for n, (i, h) in enumerate(items):
                s_ready.wait(act, n + 1)
                if n >= 2:
                    summed.wait(act, n - 1)
                act.activation(relu[n % 2][:, 0:(i + 1) * P], ps[n % 2][:, 0:(i + 1) * P], ACT.Relu).then_inc(r_done.sem, 1)

        @block.vector
        def _(dve):
            chain = Chain(dve, step)
            chain(dve.tensor_scalar(wi[:, :, :], z[:, :, 2112:2120], IDX_SCALE, None, ALU.mult))
            chain(dve.tensor_copy(bias[:, 0, 0:P], e.causal_b[:, :]))
            for i in range(1, 4):
                width = (i + 1) * P
                s = score[:, i, 0:width]
                for h in range(N_IDX):
                    n = (i - 1) * N_IDX + h
                    r_done.wait(dve, n + 1)
                    if h == 0:
                        dve.tensor_scalar(s, relu[n % 2][:, 0:width], wi[:, i, 0:1], None, ALU.mult).then_inc(summed.sem, 1)
                    else:
                        dve.scalar_tensor_tensor(s, relu[n % 2][:, 0:width], wi[:, i, h:h + 1], s, ALU.mult, ALU.add)\
                           .then_inc(summed.sem, 1)
                    summed.wait(dve, n + 1)
                chain(dve.tensor_tensor(score[:, i, i * P:width], score[:, i, i * P:width], e.causal_f[:, :], ALU.add))
                for _ in range(TOPK // 8):
                    chain(dve.max(top[:, :], s))
                    chain(dve.match_replace(s, top[:, :], s, TAKEN))
                chain(dve.tensor_scalar(bias[:, i, 0:width], s, TAKEN / 2, NEG, ALU.is_gt, ALU.mult))
                chain(dve.tensor_tensor(bias[:, i, i * P:width], bias[:, i, i * P:width], e.causal_b[:, :], ALU.add))
    s_ready.base += len(items)
    r_done.base += len(items)
    summed.base += len(items)
    step.base += 2 + 3 * (3 + 2 * TOPK // 8)


def index_sample(e, qi_t, ki_t, wi, bias_s):
    nc = e.nc
    with ExitStack() as ctx:
        def sb(n, shape, dt=F32):
            return ctx.enter_context(nc.sbuf_tensor(f"is_{n}", shape, dt))
        rows, kt = sb("rows", [P, 16, HD]), sb("kt", [HD, TS, 256])
        qz, w_m, w_col, w_bd = sb("qz", [HD, 8 * 72]), sb("w_m", [64, 8]), sb("w_col", [64, 1]), sb("w_bd", [64, TS])
        relu, s, top = sb("relu", [64, 257]), sb("s", [TS, 257]), sb("top", [TS, 8])
        k_ps = [ctx.enter_context(nc.psum_tensor(f"is_k_ps{i}", [P, 512], F32)) for i in range(2)]
        s_ps, w_ps, o_ps = (ctx.enter_context(nc.psum_tensor(f"is_{n}", [P, 512], F32)) for n in ("s_ps", "w_ps", "o_ps"))
        landed = e.sig(*[f"sample_rows_landed{i}" for i in range(4)])
        turned, copied, ready, step, relu_done, summed = e.sig("is_turned", "is_copied", "is_ready", "is_step", "is_relu",
                                                               "is_summed")
        block = ctx.enter_context(nc.Block())

        @block.sync
        def _(sp):
            for i in range(16):
                page = sp.value_load(e.table[0:1, i:i + 1], min_val=0, max_val=e.cache_dsa_idx.shape[1] - 1)
                if i >= 4:
                    landed[i % 4].wait(sp, 16 * (i // 4))
                sp.dma_start(rows[:, i, :], e.cache_dsa_idx[0, ds(page, 1)].rearrange("o p d -> (o p) d"))\
                  .then_inc(landed[i % 4].sem, 16)

        @block.tensor
        def _(pe):
            pe.matmul(w_ps[0:64, 0:8], e.isel_t[0:TS, :], wi[0:TS, 4, :], start=True, stop=True).then_inc(turned.sem, 1)
            for n in range(4):
                if n >= 2:
                    copied.wait(pe, n - 1)
                for k in range(4):
                    i = 4 * n + k
                    landed[i % 4].wait(pe, 16 * (i // 4 + 1))
                    m = pe.transpose(k_ps[n % 2][0:HD, k * P:(k + 1) * P], rows[:, i, :], e.ident[:, :])
                m.then_inc(turned.sem, 1)
            copied.wait(pe, 4)
            step.wait(pe, 6)
            for b in range(TS):
                pe.matmul(s_ps[0:64, 0:256], qz[:, b * 64:(b + 1) * 64], kt[:, b, :], start=b == 0, stop=b == TS - 1)
            for b in range(TS):
                m = pe.matmul(s_ps[0:64, 256:257], qz[:, b * 64:(b + 1) * 64], ki_t[0:HD, 0, TP + b:TP + b + 1],
                              start=b == 0, stop=b == TS - 1)
            m.then_inc(ready.sem, 1)
            relu_done.wait(pe, 1)
            pe.matmul(o_ps[0:TS, 0:257], w_bd[:, :], relu[:, :], start=True, stop=True).then_inc(summed.sem, 1)

        @block.scalar
        def _(act):
            ready.wait(act, 1)
            act.activation(relu[:, :], s_ps[0:64, 0:257], ACT.Relu).then_inc(relu_done.sem, 1)

        @block.vector
        def _(dve):
            chain = Chain(dve, step)
            turned.wait(dve, 1)
            chain(dve.tensor_tensor(w_m[:, :], w_ps[0:64, 0:8], e.imask[0:64, :], ALU.mult))
            chain(dve.tensor_reduce(w_col[:, :], w_m[:, :], AX.X, ALU.add))
            chain(dve.tensor_scalar(w_bd[:, :], e.isel[0:64, :], w_col[:, :], None, ALU.mult))
            chain(dve.memset(qz[:, :], 0.0))
            for par in range(2):
                chain(dve.tensor_copy(qz[:, :].rearrange("p (b s) -> p b s", s=72)[:, :, par:8:2],
                                      qi_t[par * HD:(par + 1) * HD, :, TP:T].rearrange("p h b -> p b h")))
            for n in range(4):
                turned.wait(dve, n + 2)
                dve.tensor_copy(kt[:, 2 * n:2 * n + 2, :].rearrange("p b s -> p (b s)"), k_ps[n % 2][0:HD, :]).then_inc(copied.sem, 1)
            summed.wait(dve, 1)
            chain(dve.tensor_copy(s[:, :], o_ps[0:TS, 0:257]))
            for _ in range(TOPK_S // 8):
                chain(dve.max(top[:, :], s[:, :]))
                chain(dve.match_replace(s[:, :], top[:, :], s[:, :], TAKEN))
            chain(dve.tensor_scalar(bias_s[:, :], s[:, :], TAKEN / 2, NEG, ALU.is_gt, ALU.mult))
    for sig in landed:
        sig.base += 64
    for sig, n in ((turned, 5), (copied, 4), (ready, 1), (step, 8 + 2 * TOPK_S // 8), (relu_done, 1), (summed, 1)):
        sig.base += n


def dsa_regions(e):
    projection_regions(e, "dsa", e.w_dsa_in[0], DSA_COLS, 4)
    out_regions(e, "dsa", e.w_dsa_out[0])


def dsa(e):
    nc = e.nc
    with ExitStack() as mix:
        def sb(n, shape, dt=F32, ctx=mix):
            return ctx.enter_context(nc.sbuf_tensor(f"dsa_{n}", shape, dt))
        z = sb("z", [P, NT, DSA_COLS])
        o, o_sample, kn = sb("o", [P, 4, D]), sb("o_sample", [P, KC, TS]), sb("k_new", [P, 2, TS])
        bias_s = sb("bias_s", [TS, 257])
        sb_ = SampleBuffers(sb("qbd", [P, 2304]), None, sb("o_t", [P, 2, P]))
        projection(e, "dsa", 4, z, 4, DSA_COLS)
        with ExitStack() as turns:
            qt, kt = sb("qt", [P, 8, T], ctx=turns), sb("kt", [P, 2, T], ctx=turns)
            qi_t, ki_t = sb("qi_t", [P, 4, T], ctx=turns), sb("ki_t", [P, 1, T], ctx=turns)
            wi, bias = sb("wi", [P, NT, N_IDX], ctx=turns), sb("bias", [P, 4, TP], BF16, ctx=turns)
            jobs = [(lambda t, c=c: z[:, t, 1024 + c * P:1024 + (c + 1) * P], kt[:, c, :], 1.0, "k") for c in range(2)]
            jobs.append((lambda t: z[:, t, 2048:2112], ki_t[:, 0, :], 1.0, "k"))
            jobs += [(lambda t, j=j: z[:, t, 1536 + j * P:1536 + (j + 1) * P], qi_t[:, j, :], SCALE, "q") for j in range(4)]
            jobs += [(lambda t, j=j: z[:, t, j * P:(j + 1) * P], qt[:, j, :], SCALE, "q") for j in range(8)]
            kv, ix = (x[0, 0].rearrange(r, p=P) for x, r in ((e.dsa_kv_p, "(t p) c k d -> p t (c k d)"),
                                                             (e.dsa_idx_p, "(t p) d -> p t d")))
            stores = [(kv[:, t, :], z[:, t, 1024:1536]) for t in range(4)] + [(ix, z[:, 0:4, 2048:2112])]
            stores += [(e.dsa_kv_s[0].rearrange("b s c k d -> (b s) (c k d)"), z[0:TS, 4, 1024:1536]),
                       (e.dsa_idx_s[0].rearrange("b s d -> (b s) d"), z[0:TS, 4, 2048:2112])]
            turn_stage(e, "dsa", z, jobs, [(1536, N_IDX), (0, HEADS)], [(1024, KV), (2048, 1)], stores)
            index_prompt(e, z, qi_t, ki_t, wi, bias)
            attention(e, "dsa_att", qt, kt, lambda kc, kv: z[:, kc, 1280 + kv * HD:1280 + (kv + 1) * HD], bias, None, o, False)
            index_sample(e, qi_t, ki_t, wi, bias_s)
            with ExitStack() as ctx:
                block = ctx.enter_context(nc.Block())

                @block.vector
                def _(dve):
                    dve.tensor_copy(kn[:, :, :], kt[:, :, TP:T])
            sample_setup(e, None, qt, sb_)
        sample_attention(e, "sdsa", sb_, lambda i, page: e.cache_dsa_kv[0, ds(page, 1)].rearrange("o p c k d -> (o p) (c k d)"),
                         kn, z[0:TS, 4, 1280:1536], None, True, bias=(e.esel_t[0:TS, :], bias_s), table=e.table)
        sample_finish(e, sb_, o_sample)
        out_projection(e, "dsa", o, o_sample, e.x_rows)


def start_stage(e):
    nc = e.nc
    with ExitStack() as ctx:
        rows = ctx.enter_context(nc.sbuf_tensor("x_rows", [P, NT, D], F32))
        gain_rows = ctx.enter_context(nc.sbuf_tensor("gain_rows", [7 * KC, P], F32))
        xt_ps = [ctx.enter_context(nc.psum_tensor(f"xt_ps{i}", [P, 512], F32)) for i in range(4)]
        block = ctx.enter_context(nc.Block())
        loads = [
            (e.const[:, :], e.c_const), (e.table[:, :], e.page_table.rearrange("(o b) n -> o (b n)", o=1)),
            (gain_rows[0:6 * KC, :], e.norm_g.rearrange("l s (k p) -> (l s k) p", p=P)),
            (gain_rows[6 * KC:7 * KC, :], e.final_norm_g.rearrange("(k p) -> k p", p=P)),
            (rows[:, 0:4, :], e.x_prompt[0].rearrange("(t p) d -> p t d", p=P)),
            (rows[0:TS, 4, :], e.x_sample.rearrange("b s d -> (b s) d")),
        ]

        @block.sync
        def _(sp):
            for dst, src in loads:
                sp.dma_start(dst, src).then_inc(e.start_loaded, 16)
            load_units(e, sp, 0, min(2, e.stream.total))

        @block.gpsimd
        def _(pool):
            pool.memset(e.sumsq[:, :], 1.0).then_inc(e.sum_done, 1)
            pool.memset(e.eps[:, :], EPS).then_inc(e.sq_done, 1)
            e.sums = 1
            pool.wait_ge(e.sq_done, 1)
            square_sum_pool(e, pool, 0)

        @block.tensor
        def _(pe):
            pe.wait_ge(e.start_loaded, 16 * len(loads))
            pe.transpose(xt_ps[2][:, 0:7 * KC], gain_rows[:, :], e.ident[0:7 * KC, 0:7 * KC])
            for k in range(KC):
                m = pe.transpose(xt_ps[3][:, k * TS:(k + 1) * TS], rows[0:TS, 4, k * P:(k + 1) * P], e.ident[0:TS, 0:TS])
            m.then_inc(e.turned, 1)
            for k in range(KC):
                if k >= 2:
                    pe.wait_ge(e.x_done, k - 1)
                for t in range(4):
                    m = pe.transpose(xt_ps[k % 2][:, t * P:(t + 1) * P], rows[:, t, k * P:(k + 1) * P], e.ident[:, :])
                m.then_inc(e.turned, 1)

        @block.scalar
        def _(act):
            act.wait_ge(e.turned, 1)
            act.activation(e.x[:, :, TP:T], xt_ps[3][:, 0:KC * TS].rearrange("p (k t) -> p k t", k=KC), ACT.Copy)\
               .then_inc(e.sample_turned, 1)
            split_hi(e, act, 0, 0, e.cols_of(0))

        @block.vector
        def _(dve):
            dve.wait_ge(e.turned, 1)
            dve.memset(e.start_mark[:, :], 0.0).then_inc(e.a_lo_done, 1)
            dve.tensor_copy(e.gain[:, :], xt_ps[2][:, 0:7 * KC]).then_inc(e.start_copied, 1)
            dve.tensor_copy(e.ident_b[:, :], e.ident[:, :]).then_inc(e.start_copied, 1)
            dve.tensor_copy(e.causal_b[:, :], e.causal_f[:, :]).then_inc(e.start_copied, 1)
            dve.wait_ge(e.sample_turned, 1)
            for k in range(KC):
                dve.wait_ge(e.turned, k + 2)
                dve.tensor_copy(e.x[:, k, 0:TP], xt_ps[k % 2][:, :]).then_inc(e.x_done, 1)
            split_lo(e, dve, 0, 0, e.cols_of(0))
    e.x_rows += KC


def final_stage(e):
    nc = e.nc
    norm = 6
    with ExitStack() as ctx:
        y = ctx.enter_context(nc.sbuf_tensor("y", [P, KC, T], F32))
        rows = ctx.enter_context(nc.sbuf_tensor("y_rows", [P, NT, D], F32))
        stat_ps = ctx.enter_context(nc.psum_tensor("stat_ps", [P, 2, 512], F32))
        row_ps = [ctx.enter_context(nc.psum_tensor(f"row_ps{i}", [P, 512], F32)) for i in range(4)]
        block = ctx.enter_context(nc.Block())
        n = e.norm_n

        @block.tensor
        def _(pe):
            for half in range(2):
                m = pe.matmul(stat_ps[:, half, 0:TH], e.ones[:, :], e.sumsq[:, half * TH:(half + 1) * TH],
                              start=True, stop=True)
            m.then_inc(e.stat_ready, 1)
            for t in range(NT):
                m_rows = P if t < 4 else TS
                for half in range(2):
                    i = 2 * t + half
                    if i >= 4:
                        pe.wait_ge(e.row_copied, i - 3)
                    pe.wait_ge(e.y_done, 4 * (half + 1))
                    for k in range(4):
                        kk = 4 * half + k
                        m = pe.transpose(row_ps[i % 4][0:m_rows, k * P:(k + 1) * P],
                                         y[:, kk, t * P:t * P + m_rows], e.ident[:, :])
                    m.then_inc(e.row_turned, 1)

        @block.scalar
        def _(act):
            act.wait_ge(e.stat_ready, n + 1)
            act.activation(e.rms[:, :].rearrange("p (a t) -> p a t", a=2), stat_ps[:, :, 0:TH], ACT.Sqrt,
                           bias=e.eps[:, :], scale=1.0 / D).then_inc(e.rms_done, 1)

        @block.vector
        def _(dve):
            dve.wait_ge(e.rms_done, n + 1)
            dve.reciprocal(e.rs[:, :], e.rms[:, :]).then_inc(e.rs_done, 1)
            dve.wait_ge(e.rs_done, n + 1)
            for k in range(KC):
                dve.scalar_tensor_tensor(y[:, k, :], e.x[:, k, :], e.gain[:, norm * KC + k:norm * KC + k + 1],
                                         e.rs[:, :], ALU.mult, ALU.mult).then_inc(e.y_done, 1)
            for i in range(2 * NT):
                m_rows = P if i < 8 else TS
                dve.wait_ge(e.row_turned, i + 1)
                dve.tensor_copy(rows[0:m_rows, i // 2, (i % 2) * 512:(i % 2 + 1) * 512],
                                row_ps[i % 4][0:m_rows, :]).then_inc(e.row_copied, 1)

        @block.sync
        def _(sp):
            yp = e.y_prompt[0].rearrange("(t p) d -> p t d", p=P)
            for t in range(4):
                sp.wait_ge(e.row_copied, 2 * t + 2)
                sp.dma_start(yp[:, t, :], rows[:, t, :]).then_inc(e.stored, 16)
                e.stores += 1
            sp.wait_ge(e.row_copied, 2 * NT)
            sp.dma_start(e.y_sample.rearrange("b s d -> (b s) d"), rows[0:TS, 4, :]).then_inc(e.stored, 16)
            e.stores += 1
            sp.wait_ge(e.stored, 16 * e.stores)


CONSTS = (("ident", P), ("causal_f", P), ("ones", P), ("cos", NT * 8), ("sin", NT * 8), ("cadd", 32), ("c01", 32),
          ("hsel", HEADS), ("esel", TS), ("hmask", HEADS), ("bmask", 32), ("rep", P), ("esel_t", P),
          ("isel", TS), ("imask", 8), ("isel_t", 64))


def constants():
    import numpy as np
    i = np.arange(P)
    pos = np.full(NT * P, 256, np.int32)
    pos[0:TP] = np.arange(TP)
    inv = np.float32(500000.0) ** (-np.arange(8, dtype=np.float32) * np.float32(2.0) / np.float32(16))
    ang = pos.astype(np.float32)[:, None] * inv[None, :]
    seen = ((np.arange(8) + 1) * 64 - 1)[None, :] <= np.arange(TP)[:, None]

    def tiles(a):
        return a.reshape(-1, P, 8).transpose(1, 0, 2).reshape(P, -1)
    j, par, n = i // 16, i // 8 % 2, i % 8
    head = 8 * (j // 4) + 4 * par + j % 4
    rep = np.zeros((P, P), np.float32)
    rep[n, i] = 1
    esel_t = np.zeros((P, P), np.float32)
    esel_t[i // 16, i] = 1
    parts = {
        "ident": np.eye(P), "causal_f": np.where(i[None, :] <= i[:, None], 0, NEG), "ones": np.ones((P, P)),
        "cos": tiles(np.cos(ang)), "sin": tiles(np.sin(ang)), "cadd": tiles(np.where(seen, 0, NEG)),
        "c01": tiles(seen), "hsel": head[:, None] == np.arange(16), "esel": i[:, None] // 16 == np.arange(8),
        "hmask": i[:, None] % 16 == np.arange(16), "bmask": np.where(i[:, None] // 16 == np.arange(32) // 4, 0, NEG),
        "rep": rep, "esel_t": esel_t, "isel": i[:, None] // 8 == np.arange(8), "imask": i[:, None] % 8 == np.arange(8),
        "isel_t": i[:, None] == np.arange(64) // 8,
    }
    return {"c_const": np.concatenate([np.asarray(parts[c], np.float32) for c, _ in CONSTS], axis=1)}


OUTS = {
    "y_prompt": (1, TP, D), "y_sample": (TS, 1, D),
    "nsa_cmp_p": (1, 1, TP, 2, KV, HD), "nsa_cmp_s": (1, TS, 1, 2, KV, HD),
    "nsa_slc_p": (1, 1, TP, 2, KV, HD), "nsa_slc_s": (1, TS, 1, 2, KV, HD),
    "nsa_win_p": (1, 1, TP, 2, KV, HD), "nsa_win_s": (1, TS, 256, 2, KV, HD),
    "dsa_kv_p": (1, 1, TP, 2, KV, HD), "dsa_kv_s": (1, TS, 1, 2, KV, HD),
    "dsa_idx_p": (1, 1, TP, HD), "dsa_idx_s": (1, TS, 1, HD),
}


def build(nc, ins, outs, plan=None):
    c_const = ins["c_const"]
    plan = plan or ["ffn0", "nsa", "ffn1", "ffn2", "dsa", "ffn3"]
    with ExitStack() as ctx:
        def sb(name, shape, dt=F32):
            return ctx.enter_context(nc.sbuf_tensor(name, shape, dt))
        signals = {}

        def sig(*names):
            for name in names:
                if name not in signals:
                    signals[name] = Signal(ctx.enter_context(nc.semaphore(name)))
            return [signals[name] for name in names]
        const, views, at = sb("const", [P, sum(n for _, n in CONSTS)]), {}, 0
        for name, n in CONSTS:
            views[name] = const[:, at:at + n]
            at += n
        for name, n in (("cos", NT), ("sin", NT), ("cadd", 4), ("c01", 4)):
            views[name] = views[name].rearrange("p (t n) -> p t n", t=n)
        e = Core(nc, sig, ins, outs, c_const, const, views, lambda name: ctx.enter_context(nc.semaphore(name)))
        for step in plan:
            if step.startswith("ffn"):
                ffn_regions(e, int(step[3:]))
            elif step == "nsa":
                nsa_regions(e)
            else:
                dsa_regions(e)
        e.x = sb("x", [P, KC, T])
        e.w_stage = [sb(f"w_stage{i}", [P, UNIT]) for i in range(2)]
        e.w_hi = [sb(f"w_hi{i}", [P, UNIT], FR) for i in range(2)]
        e.w_lo = [sb(f"w_lo{i}", [P, UNIT], FR) for i in range(2)]
        e.table = sb("table", [1, 2 * TS], I32)
        e.ident_b, e.causal_b = sb("ident_b", [P, P], BF16), sb("causal_b", [P, P], BF16)
        e.gain = sb("gain", [P, 7 * KC])
        e.sq, e.sumsq = sb("sq", [P, T]), sb("sumsq", [P, NT * P])
        e.rms, e.rs = sb("rms", [P, T]), sb("rs", [P, T])
        e.eps, e.start_mark, e.start_mark2 = sb("eps", [P, 1]), sb("start_mark", [P, 1]), sb("start_mark2", [P, 1])
        e.rms_col, e.rs_col = sb("rms_col", [P, NT]), sb("rs_col", [P, NT])
        start_stage(e)
        for step in plan:
            if step.startswith("ffn"):
                n = int(step[3:])
                ffn(e, n, 3 * (n // 2) + 2 * (n % 2), e.x_rows)
                e.x_rows += 2 * KC
            elif step == "nsa":
                nsa(e)
            else:
                dsa(e)
        final_stage(e)



INS = ("x_prompt", "x_sample", "cache_nsa_cmp", "cache_nsa_slc", "state_nsa_win", "cache_dsa_kv", "cache_dsa_idx",
       "page_table", "norm_g", "w_ffn_in", "w_ffn_out", "w_nsa_in", "w_nsa_out", "nsa_cmp_pos", "nsa_cmp_w1",
       "nsa_cmp_w2", "w_dsa_in", "w_dsa_out", "final_norm_g")


def kernel(**inputs):
    import numpy as np
    import concourse.bacc as bacc
    from concourse.bass_utils import run_bass_kernel_spmd

    nc = bacc.Bacc("TRN2", target_bir_lowering=False, num_devices=1)
    arrays, ins = {}, {}
    for name in INS:
        arrays[name] = np.ascontiguousarray(inputs[name])
    arrays.update(constants())
    for name, a in arrays.items():
        ins[name] = nc.dram_tensor(name, a.shape, mybir.dt.from_np(a.dtype), kind="ExternalInput").ap()
    outs = {name: nc.dram_tensor(name, shape, F32, kind="ExternalOutput").ap() for name, shape in OUTS.items()}
    build(nc, ins, outs)
    r = run_bass_kernel_spmd(nc, [arrays], core_ids=[0])
    return tuple(r.results[0][name] for name in OUTS)
```

```python
from contextlib import ExitStack

import concourse.bass as bass
from concourse import mybir

F32 = mybir.dt.float32
FR = mybir.dt.float32r
BF16 = mybir.dt.bfloat16
I32 = mybir.dt.int32
ACT = mybir.ActivationFunctionType
ALU = mybir.AluOpType
AX = mybir.AxisListType
ds = bass.ds

P = 128
D = 1024
KC = D // P
TP = 512
TS = 8
T = TP + TS
TH = T // 2
NT = 5
DFF = 2816
FH = DFF // P // 2
HEADS = 16
HD = 64
KV = 4
NSA_COLS = 2608
DSA_COLS = 2120
EPS = 1e-6
NEG = -1e30
SCALE = HD ** -0.5
UNIT = FH * P


class Stream:

    def __init__(self):
        self.regions = []
        self.total = 0

    def add(self, name, count, src, cols, per=2):
        self.regions.append((name, self.total, count, src, cols, per))
        self.total += count

    def start(self, name):
        return next(r[1] for r in self.regions if r[0] == name)


class Core:

    def __init__(self, nc, sig, ins, outs, consts, const, views, sem):
        self.nc, self.sig, self.stream, self.const, self.c_const = nc, sig, Stream(), const, consts
        self.h_n, self.norm_n, self.sums, self.stores, self.x_rows = 0, 0, 0, 0, 0
        self.x_prompt, self.x_sample, self.cache_nsa_cmp = ins["x_prompt"], ins["x_sample"], ins["cache_nsa_cmp"]
        self.cache_nsa_slc, self.state_nsa_win, self.cache_dsa_kv = ins["cache_nsa_slc"], ins["state_nsa_win"], ins["cache_dsa_kv"]
        self.cache_dsa_idx, self.page_table, self.norm_g = ins["cache_dsa_idx"], ins["page_table"], ins["norm_g"]
        self.w_ffn_in, self.w_ffn_out, self.w_nsa_in = ins["w_ffn_in"], ins["w_ffn_out"], ins["w_nsa_in"]
        self.w_nsa_out, self.nsa_cmp_pos, self.nsa_cmp_w1 = ins["w_nsa_out"], ins["nsa_cmp_pos"], ins["nsa_cmp_w1"]
        self.nsa_cmp_w2, self.w_dsa_in, self.w_dsa_out = ins["nsa_cmp_w2"], ins["w_dsa_in"], ins["w_dsa_out"]
        self.final_norm_g = ins["final_norm_g"]
        self.y_prompt, self.y_sample, self.nsa_cmp_p = outs["y_prompt"], outs["y_sample"], outs["nsa_cmp_p"]
        self.nsa_cmp_s, self.nsa_slc_p, self.nsa_slc_s = outs["nsa_cmp_s"], outs["nsa_slc_p"], outs["nsa_slc_s"]
        self.nsa_win_p, self.nsa_win_s, self.dsa_kv_p = outs["nsa_win_p"], outs["nsa_win_s"], outs["dsa_kv_p"]
        self.dsa_kv_s, self.dsa_idx_p, self.dsa_idx_s = outs["dsa_kv_s"], outs["dsa_idx_p"], outs["dsa_idx_s"]
        self.ident, self.causal_f, self.ones, self.cos = views["ident"], views["causal_f"], views["ones"], views["cos"]
        self.sin, self.cadd, self.c01, self.hsel = views["sin"], views["cadd"], views["c01"], views["hsel"]
        self.esel, self.hmask, self.bmask, self.rep = views["esel"], views["hmask"], views["bmask"], views["rep"]
        self.esel_t, self.isel, self.imask, self.isel_t = views["esel_t"], views["isel"], views["imask"], views["isel_t"]
        self.landed0, self.landed1, self.lo_done = sem("landed0"), sem("landed1"), sem("lo_done")
        self.hi_done, self.unit_used, self.h_hi_done = sem("hi_done"), sem("unit_used"), sem("h_hi_done")
        self.h_lo_done, self.x_done, self.sq_done = sem("h_lo_done"), sem("x_done"), sem("sq_done")
        self.sum_done, self.stat_ready, self.rms_done = sem("sum_done"), sem("stat_ready"), sem("rms_done")
        self.rs_done, self.gate_read, self.up_read = sem("rs_done"), sem("gate_read"), sem("up_read")
        self.silu_done, self.act_ready, self.a_hi_done = sem("silu_done"), sem("act_ready"), sem("a_hi_done")
        self.a_lo_done, self.start_loaded, self.turned = sem("a_lo_done"), sem("start_loaded"), sem("turned")
        self.sample_turned, self.start_copied, self.row_turned = sem("sample_turned"), sem("start_copied"), sem("row_turned")
        self.row_copied, self.y_done, self.stored = sem("row_copied"), sem("y_done"), sem("stored")
        self.start_squared, self.start_added = sem("start_squared"), sem("start_added")
        self.landed = [self.landed0, self.landed1]

    def cols_of(self, u):
        return next(r[4] for r in self.stream.regions if r[1] <= u < r[1] + r[2])


class SampleBuffers:

    def __init__(self, qbd, qz, o_rows):
        self.qbd, self.qz, self.o_rows = qbd, qz, o_rows


def load_units(e, sp, first, last):
    for name, at, count, src, cols, per in e.stream.regions:
        lo, hi = max(first, at), min(last, at + count)
        if lo >= hi:
            continue

        def one(turn, side, u):
            slot = (at + side) % 2
            view, dst = src(turn, side, (lambda v: v) if isinstance(u, int) else sp.snap), e.w_stage[slot][:, 0:cols]
            if not isinstance(u, int) or u >= 2:
                sp.wait_ge(e.lo_done, u - 1)
            sp.dma_start(dst.rearrange("p (k n) -> p k n", k=view.shape[1]), view).then_inc(e.landed[slot], 16)

        k = lo - at
        while k % per and k < hi - at:
            one(k // per, k % per, at + k)
            k += 1
        turns = (hi - at - k) // per
        if turns > 1 and at + k >= 2:
            t0 = k // per
            with sp.Fori(t0, t0 + turns) as q:
                for side in range(per):
                    one(q, side, q * per + (at + side))
            k += per * turns
        while k < hi - at:
            one(k // per, k % per, at + k)
            k += 1


def split_hi(e, act, base, q, cols):
    slot = base % 2
    act.wait_ge(e.landed[slot], q * 16 + 16 * (base // 2 + 1))
    if base >= 2 or not isinstance(q, int):
        act.wait_ge(e.unit_used, q * 2 + (base - 1))
    act.activation(e.w_hi[slot][:, 0:cols], e.w_stage[slot][:, 0:cols], ACT.Copy).then_inc(e.hi_done, 1)


def split_lo(e, dve, base, q, cols):
    slot = base % 2
    dve.wait_ge(e.hi_done, q * 2 + (base + 1))
    dve.tensor_tensor(e.w_lo[slot][:, 0:cols], e.w_stage[slot][:, 0:cols],
                      e.w_hi[slot][:, 0:cols].bitcast(F32), ALU.subtract).then_inc(e.lo_done, 1)


def three_passes(pe, out, w_hi, w_lo, x_hi, x_lo, first, last):
    pe.matmul(out, w_hi, x_hi, start=first, stop=False)
    pe.matmul(out, w_hi, x_lo, start=False, stop=False)
    return pe.matmul(out, w_lo, x_hi, start=False, stop=last)


def warm_up(e, pe, out, count):
    for _ in range(count):
        pe.matmul(out, e.ident_b[:, :], e.causal_b[:, :], start=True, stop=True)



def build_h_act(e, act, norm):
    for k in range(KC):
        act.activation(e.h_hi[:, k, 0:T], e.x[:, k, :], ACT.Copy, scale=e.gain[:, norm * KC + k:norm * KC + k + 1])\
           .then_inc(e.h_hi_done, 1)


def build_h_dve(e, dve, norm, n):
    for k in range(KC):
        dve.wait_ge(e.h_hi_done, KC * n + k + 1)
        dve.scalar_tensor_tensor(e.h_lo[:, k, 0:T], e.x[:, k, :], e.gain[:, norm * KC + k:norm * KC + k + 1],
                                 e.h_hi[:, k, 0:T].bitcast(F32), ALU.mult, ALU.subtract).then_inc(e.h_lo_done, 1)


def square_sum_pool(e, pool, base):
    for i in range(KC):
        pool.wait_ge(e.x_done, base + i + 1)
        pool.wait_ge(e.sum_done, e.sums)
        pool.tensor_tensor(e.sq[:, :], e.x[:, i, :], e.x[:, i, :], ALU.mult).then_inc(e.sq_done, 1)
        pool.wait_ge(e.sq_done, e.sums + 1)
        if i == 0:
            pool.tensor_copy(e.sumsq[:, 0:T], e.sq[:, :]).then_inc(e.sum_done, 1)
        else:
            pool.tensor_tensor(e.sumsq[:, 0:T], e.sumsq[:, 0:T], e.sq[:, :], ALU.add).then_inc(e.sum_done, 1)
        e.sums += 1



def ffn_regions(e, n):
    layer, which = n // 2, n % 2
    w_in = e.w_ffn_in[layer, which].rearrange("(k p) n -> p k n", p=P)
    w_out = e.w_ffn_out[layer, which].rearrange("(f p) n -> p f n", p=P)
    for half in range(2):
        def src_in(pair, side, at, half=half):
            return w_in[:, :, ds(at(pair * P + (side * DFF + half * FH * P)), P)]

        def src_out(pair, side, at, half=half):
            return w_out[:, half * FH:(half + 1) * FH, ds(at(pair * (2 * P) + side * P), P)]

        e.stream.add(f"ffn{n}.in{half}", 2 * FH, src_in, KC * P)
        e.stream.add(f"ffn{n}.out{half}", KC, src_out, FH * P)


def ffn(e, n, norm, x_base):
    nc = e.nc
    in0 = [e.stream.start(f"ffn{n}.in{h}") for h in range(2)]
    out0 = [e.stream.start(f"ffn{n}.out{h}") for h in range(2)]
    end = out0[1] + KC
    f0 = 2 * FH * n
    with ExitStack() as ctx:
        def sb(name, shape, dt=F32):
            return ctx.enter_context(nc.sbuf_tensor(f"{name}_{n}", shape, dt))

        def ps(name, banks):
            return ctx.enter_context(nc.psum_tensor(f"{name}_{n}", [P, banks, 512], F32))
        e.h_hi, e.h_lo = sb("h_hi", [P, KC, T], FR), sb("h_lo", [P, KC, T], FR)
        a_hi, a_lo = sb("a_hi", [P, FH, T], FR), sb("a_lo", [P, FH, T], FR)
        gate_t, up_t, silu_t, act_t = (sb(s, [P, 2, TH]) for s in ("gate_t", "up_t", "silu_t", "act_t"))
        gate_ps, up_ps = ps("gate_ps", 2), ps("up_ps", 2)
        y_ps = [ps("y_ps0", 2), ps("y_ps1", 2)]
        rs2 = e.rs[:, :].rearrange("p (a t) -> p a t", a=2)
        hn = e.h_n
        at_start = n == 0
        start_sq = (e.sq[:, :], e.rs[:, :])
        sums = e.sums

        block = ctx.enter_context(nc.Block())

        @block.sync
        def _(sp):
            load_units(e, sp, in0[0] + 2, min(end + 2, e.stream.total))

        @block.gpsimd
        def _(pool):
            if at_start:
                for k in range(KC):
                    if k >= 2:
                        pool.wait_ge(e.start_added, k - 1)
                    pool.tensor_tensor(start_sq[k % 2], e.x[:, k, :], e.x[:, k, :], ALU.mult).then_inc(e.start_squared, 1)
                pool.wait_ge(e.start_added, KC)
            square_sum_pool(e, pool, x_base + KC)

        @block.tensor
        def _(pe):
            def in_unit(base, q, f, side, first_unit):
                slot = (base + side) % 2
                pe.wait_ge(e.lo_done, q * 2 + (base + side + 1))
                bank = (gate_ps, up_ps)[side]
                if not first_unit:
                    pe.wait_ge((e.gate_read, e.up_read)[side], f)
                for k in range(KC):
                    if first_unit and side == 0:
                        pe.wait_ge(e.h_lo_done, KC * hn + k + 1)
                    for half in range(2):
                        t = slice(half * TH, (half + 1) * TH)
                        m = three_passes(pe, bank[:, half, 0:TH], e.w_hi[slot][:, k * P:(k + 1) * P],
                                         e.w_lo[slot][:, k * P:(k + 1) * P], e.h_hi[:, k, t], e.h_lo[:, k, t],
                                         k == 0, k == KC - 1)
                m.then_inc(e.unit_used, 1)

            def statistics():
                pe.wait_ge(e.sum_done, sums)
                if at_start:
                    pe.wait_ge(e.start_added, KC)
                for half in range(2):
                    m = pe.matmul(y_ps[1][:, half, 0:TH], e.ones[:, :], e.sumsq[:, half * TH:(half + 1) * TH],
                                  start=True, stop=True)
                m.then_inc(e.stat_ready, 1)

            def out_unit(half, q, side, first):
                base = out0[half]
                slot = (base + side) % 2
                pe.wait_ge(e.lo_done, q * 2 + (base + side + 1))
                if not (first and half == 0):
                    pe.wait_ge(e.x_done, q * 2 + (x_base + KC * half + side - 1))
                for f in range(FH):
                    if first and side == 0:
                        pe.wait_ge(e.a_lo_done, f0 + half * FH + f + 2)
                    for th in range(2):
                        t = slice(th * TH, (th + 1) * TH)
                        m = three_passes(pe, y_ps[side][:, th, 0:TH], e.w_hi[slot][:, f * P:(f + 1) * P],
                                         e.w_lo[slot][:, f * P:(f + 1) * P], a_hi[:, f, t], a_lo[:, f, t],
                                         f == 0, f == FH - 1)
                m.then_inc(e.unit_used, 1)

            for half in range(2):
                for side in range(2):
                    in_unit(in0[half], 0, f0 + half * FH, side, half == 0)
                    if half == 0 and side == at_start:
                        statistics()
                with pe.Fori(1, FH) as q:
                    for side in range(2):
                        in_unit(in0[half], q, q + (f0 + half * FH), side, False)
                if half == 0:
                    pe.wait_ge(e.rms_done, e.norm_n + 1)
                for side in range(2):
                    out_unit(half, 0, side, True)
                with pe.Fori(1, KC // 2) as q:
                    for side in range(2):
                        out_unit(half, q, side, False)

        @block.scalar
        def _(act):
            def a_hi_of(f, j):
                act.wait_ge(e.act_ready, f + 1)
                act.activation(a_hi[:, j, :] if isinstance(j, int) else a_hi[:, ds(j, 1), :],
                               act_t[:, :, :], ACT.Copy).then_inc(e.a_hi_done, 1)

            def silu_of(f, first):
                act.wait_ge(e.gate_read, f + 1)
                if not first:
                    act.wait_ge(e.act_ready, f)
                act.activation(silu_t[:, :, :], gate_t[:, :, :], ACT.Silu).then_inc(e.silu_done, 1)

            build_h_act(e, act, norm)
            for half in range(2):
                b = in0[half]
                F = f0 + half * FH
                split_hi(e, act, b + 1, 0, KC * P)
                split_hi(e, act, b + 2, 0, KC * P)
                if half == 0:
                    act.wait_ge(e.stat_ready, e.norm_n + 1)
                    act.activation(e.rms[:, :].rearrange("p (a t) -> p a t", a=2), y_ps[1][:, :, 0:TH], ACT.Sqrt,
                                   bias=e.eps[:, :], scale=1.0 / D).then_inc(e.rms_done, 1)
                silu_of(F, half == 0)
                if half == 1:
                    act.wait_ge(e.unit_used, out0[0] + KC)

                with act.Fori(1, FH - 1) as q:
                    split_hi(e, act, b + 1, q, KC * P)
                    a_hi_of(q + (F - 1), q - 1)
                    split_hi(e, act, b + 2, q, KC * P)
                    silu_of(q + F, False)
                split_hi(e, act, b + 2 * FH - 1, 0, KC * P)
                a_hi_of(F + FH - 2, FH - 2)
                split_hi(e, act, out0[half], 0, FH * P)
                silu_of(F + FH - 1, False)
                a_hi_of(F + FH - 1, FH - 1)
                split_hi(e, act, out0[half] + 1, 0, FH * P)
                with act.Fori(1, KC // 2) as q:
                    for side in range(2):
                        split_hi(e, act, out0[half] + side, q, FH * P)
                if half == 0:
                    split_hi(e, act, in0[1], 0, KC * P)
                elif end < e.stream.total:
                    split_hi(e, act, end, 0, e.cols_of(end))

        @block.vector
        def _(dve):
            def strip_of(b, q, f, j):
                dve.wait_ge(e.unit_used, q * 2 + (b + 2))
                dve.tensor_tensor(up_t[:, :, :], up_ps[:, :, 0:TH], rs2, ALU.mult).then_inc(e.up_read, 1)
                dve.wait_ge(e.up_read, f + 1)
                dve.wait_ge(e.silu_done, f + 1)
                dve.wait_ge(e.a_lo_done, f + 1)
                dve.tensor_tensor(act_t[:, :, :], up_t[:, :, :], silu_t[:, :, :], ALU.mult).then_inc(e.act_ready, 1)
                dve.wait_ge(e.a_hi_done, f + 1)
                dst, hi = (a_lo[:, j, :], a_hi[:, j, :]) if isinstance(j, int) else (a_lo[:, ds(j, 1), :], a_hi[:, ds(j, 1), :])
                dve.tensor_tensor(dst, act_t[:, :, :].rearrange("p a t -> p (a t)"), hi.bitcast(F32), ALU.subtract).then_inc(e.a_lo_done, 1)

            def gate_of(b, q, f, first):
                dve.wait_ge(e.unit_used, q * 2 + (b + 1))
                if not first:
                    dve.wait_ge(e.silu_done, f)
                dve.tensor_tensor(gate_t[:, :, :], gate_ps[:, :, 0:TH], rs2, ALU.mult).then_inc(e.gate_read, 1)

            def x_of(half, u, side, q, i):
                dve.wait_ge(e.unit_used, u)
                xi = e.x[:, i, :] if isinstance(i, int) else e.x[:, ds(i, 1), :]
                if isinstance(i, int):
                    xi = xi.rearrange("p (a t) -> p a t", a=2)
                else:
                    xi = xi.rearrange("p o (a t) -> p (o a) t", a=2)
                dve.scalar_tensor_tensor(xi, y_ps[side][:, :, 0:TH], 0.5, xi, ALU.mult, ALU.add).then_inc(e.x_done, 1)

            build_h_dve(e, dve, norm, hn)
            for half in range(2):
                b = in0[half]
                F = f0 + half * FH
                split_lo(e, dve, b + 1, 0, KC * P)
                if half == 0 and at_start:
                    for k in range(KC):
                        dve.wait_ge(e.start_squared, k + 1)
                        if k == 0:
                            ins = dve.tensor_copy(e.sumsq[:, 0:T], start_sq[0])
                        else:
                            dve.wait_ge(e.start_added, k)
                            ins = dve.tensor_tensor(e.sumsq[:, 0:T], e.sumsq[:, 0:T], start_sq[k % 2], ALU.add)
                        ins.then_inc(e.start_added, 1)
                split_lo(e, dve, b + 2, 0, KC * P)
                if half == 0:
                    dve.wait_ge(e.rms_done, e.norm_n + 1)
                    dve.reciprocal(e.rs[:, :], e.rms[:, :]).then_inc(e.rs_done, 1)
                    dve.wait_ge(e.rs_done, e.norm_n + 1)
                gate_of(b, 0, F, half == 0)
                with dve.Fori(1, FH - 1) as q:
                    split_lo(e, dve, b + 1, q, KC * P)
                    strip_of(b, q - 1, q + (F - 1), q - 1)
                    split_lo(e, dve, b + 2, q, KC * P)
                    gate_of(b, q, q + F, False)
                split_lo(e, dve, b + 2 * FH - 1, 0, KC * P)
                strip_of(b + 2 * (FH - 2), 0, F + FH - 2, FH - 2)
                split_lo(e, dve, out0[half], 0, FH * P)
                gate_of(b + 2 * (FH - 1), 0, F + FH - 1, False)
                strip_of(b + 2 * (FH - 1), 0, F + FH - 1, FH - 1)
                o = out0[half]
                split_lo(e, dve, o + 1, 0, FH * P)
                with dve.Fori(1, KC // 2) as q:
                    split_lo(e, dve, o, q, FH * P)
                    x_of(half, q * 2 + (o - 1), 0, q, q * 2 - 2)
                    split_lo(e, dve, o + 1, q, FH * P)
                    x_of(half, q * 2 + o, 1, q, q * 2 - 1)
                if half == 0:
                    split_lo(e, dve, in0[1], 0, KC * P)
                elif end < e.stream.total:
                    split_lo(e, dve, end, 0, e.cols_of(end))
                x_of(half, o + KC - 1, 0, 0, KC - 2)
                x_of(half, o + KC, 1, 0, KC - 1)
    e.h_n += 1
    e.norm_n += 1



class Signal:

    def __init__(self, sem):
        self.sem, self.base = sem, 0

    def wait(self, eng, n):
        eng.wait_ge(self.sem, n + self.base)


class Chain:

    def __init__(self, eng, mark):
        self.eng, self.mark, self.n = eng, mark, 0

    def __call__(self, ins):
        ins.then_inc(self.mark.sem, 1)
        self.n += 1
        self.mark.wait(self.eng, self.n)


def projection_regions(e, name, w, cols, groups):
    view = w.rearrange("(k p) n -> p k n", p=P)

    def src(group, side, at):
        return view[:, 2 * side:2 * side + 2, ds(at(group * 512), 512)]

    e.stream.add(f"{name}.in", 4 * groups, src, 1024, 4)
    e.stream.add(f"{name}.rest", 1, lambda pair, side, at: view[:, :, groups * 512:cols], KC * (cols - groups * 512))


def out_regions(e, name, w):
    view = w.rearrange("(k p) n -> p k n", p=P)
    e.stream.add(f"{name}.out", KC, lambda pair, side, at: view[:, :, ds(at(pair * (2 * P) + side * P), P)], KC * P)


def projection(e, name, norm, z, groups, cols):
    nc = e.nc
    u0, u1 = e.stream.start(f"{name}.in"), e.stream.start(f"{name}.rest")
    rest = cols - 512 * groups
    n_norm, hn, sums = e.norm_n, e.h_n, e.sums
    with ExitStack() as ctx:
        e.h_hi = ctx.enter_context(nc.sbuf_tensor(f"{name}_h_hi", [P, KC, NT * P], FR))
        e.h_lo = ctx.enter_context(nc.sbuf_tensor(f"{name}_h_lo", [P, KC, NT * P], FR))
        banks = [ctx.enter_context(nc.psum_tensor(f"{name}_z_ps{t}", [P, 512], F32)) for t in range(NT)]
        stat_ps = ctx.enter_context(nc.psum_tensor(f"{name}_stat_ps", [P, 512], F32))
        rest_ps = ctx.enter_context(nc.psum_tensor(f"{name}_rest_ps", [P, 2, 512], F32))
        rest_copied, rest_turned = e.sig("rest_copied", "rest_turned")
        z_ready, z_act, z_dve, pads = e.sig("z_ready", "z_read_act", "z_read_dve", "h_padded")
        block = ctx.enter_context(nc.Block())

        @block.sync
        def _(sp):
            load_units(e, sp, u0 + 2, u1 + 3)

        @block.gpsimd
        def _(pool):
            for h in (e.h_hi, e.h_lo):
                pool.memset(h[:, :, T:NT * P].bitcast(F32), 0.0).then_inc(pads.sem, 1)
            pool.memset(z[:, NT - 1, groups * 512:cols], 0.0).then_inc(pads.sem, 1)

        @block.tensor
        def _(pe):
            def unit(g, side, first):
                u = u0 + side
                slot = u % 2
                pe.wait_ge(e.lo_done, g * 4 + (u + 1))
                for t in range(NT):
                    tok = slice(t * P, (t + 1) * P)
                    if side == 0 and not first:
                        if t % 2 == 0:
                            z_act.wait(pe, g * 3 + (t // 2 - 2))
                        else:
                            z_dve.wait(pe, g * 2 + (t // 2 - 1))
                    for kk in range(2):
                        k = 2 * side + kk
                        if first and t == 0:
                            pe.wait_ge(e.h_lo_done, KC * hn + k + 1)
                        w = slice(kk * 512, (kk + 1) * 512)
                        m = three_passes(pe, banks[t][:, :], e.h_hi[:, k, tok], e.h_lo[:, k, tok],
                                         e.w_hi[slot][:, w], e.w_lo[slot][:, w], k == 0, k == KC - 1)
                    if side == 3 and t < NT - 1:
                        m.then_inc(z_ready.sem, 1)
                m.then_inc(e.unit_used, 1)

            pads.wait(pe, 2)
            for side in range(4):
                unit(0, side, True)
                if side == 0:
                    pe.wait_ge(e.sum_done, sums)
                    for t in range(NT):
                        m = pe.matmul(stat_ps[:, t:t + 1], e.sumsq[:, t * P:(t + 1) * P], e.ones[:, 0:1],
                                      start=True, stop=True)
                    m.then_inc(e.stat_ready, 1)
            with pe.Fori(1, groups) as g:
                for side in range(4):
                    unit(g, side, False)
            pe.wait_ge(e.lo_done, u1 + 1)
            for k in range(KC):
                w = slice(k * rest, (k + 1) * rest)
                for half in range(2):
                    t = slice(half * TH, (half + 1) * TH)
                    m = three_passes(pe, rest_ps[0:rest, half, 0:TH], e.w_hi[u1 % 2][:, w], e.w_lo[u1 % 2][:, w],
                                     e.h_hi[:, k, t], e.h_lo[:, k, t], k == 0, k == KC - 1)
            m.then_inc(e.unit_used, 1)
            rest_copied.wait(pe, 1)
            pe.wait_ge(e.rms_done, n_norm + 1)
            for t in range(NT):
                n = P if t < NT - 1 else TS
                m = pe.transpose(stat_ps[0:n, t * rest:(t + 1) * rest], e.sq[0:rest, t * P:t * P + n],
                                 e.ident[0:rest, 0:rest])
            m.then_inc(rest_turned.sem, 1)

        def out_of(g, t):
            if isinstance(g, int) and g < 2:
                return z[:, t, g * 512:(g + 1) * 512].rearrange("p (g a d) -> p a g d", g=4, a=2)
            return z[:, t, ds(g * 512, 512)]

        def in_of(g, t):
            if isinstance(g, int) and g < 2:
                return banks[t][:, :].rearrange("p (a g d) -> p a g d", g=4, a=2)
            return banks[t][:, :]

        @block.scalar
        def _(act):
            def evacuate(g, t):
                if t == NT - 1:
                    act.wait_ge(e.unit_used, g * 4 + (u0 + 4))
                else:
                    z_ready.wait(act, g * 4 + (t + 1))
                act.activation(out_of(g, t), in_of(g, t), ACT.Copy, scale=e.rs_col[:, t:t + 1]).then_inc(z_act.sem, 1)

            build_h_act(e, act, norm)
            for side in range(3):
                split_hi(e, act, u0 + side + 1, 0, 1024)
                if side == 0:
                    act.wait_ge(e.stat_ready, n_norm + 1)
                    act.activation(e.rms_col[:, :], stat_ps[:, 0:NT], ACT.Sqrt, bias=e.eps[:, :], scale=1.0 / D)\
                       .then_inc(e.rms_done, 1)
            act.wait_ge(e.rs_done, n_norm + 1)

            def group(g):
                split_hi4(e, act, u0, g, 0)
                for t in (0, 2, 4):
                    evacuate(g - 1, t)
                for side in range(1, 4):
                    split_hi4(e, act, u0, g, side)
            group(1)
            group(2)
            with act.Fori(3, groups) as g:
                group(g)
            split_hi(e, act, u1, 0, KC * rest)
            for t in (0, 2, 4):
                evacuate(groups - 1, t)
            split_hi(e, act, u1 + 1, 0, e.cols_of(u1 + 1))

        @block.vector
        def _(dve):
            def evacuate(g, t):
                z_ready.wait(dve, g * 4 + (t + 1))
                dve.tensor_scalar(out_of(g, t), in_of(g, t), e.rs_col[:, t:t + 1], None, ALU.mult)\
                   .then_inc(z_dve.sem, 1)

            build_h_dve(e, dve, norm, hn)
            for side in range(3):
                split_lo(e, dve, u0 + side + 1, 0, 1024)
                if side == 0:
                    dve.wait_ge(e.rms_done, n_norm + 1)
                    dve.reciprocal(e.rs_col[:, :], e.rms_col[:, :]).then_inc(e.rs_done, 1)
            dve.wait_ge(e.rs_done, n_norm + 1)

            def group(g):
                split_lo4(e, dve, u0, g, 0)
                for t in (1, 3):
                    evacuate(g - 1, t)
                for side in range(1, 4):
                    split_lo4(e, dve, u0, g, side)
            group(1)
            group(2)
            with dve.Fori(3, groups) as g:
                group(g)
            split_lo(e, dve, u1, 0, KC * rest)
            for t in (1, 3):
                evacuate(groups - 1, t)
            split_lo(e, dve, u1 + 1, 0, e.cols_of(u1 + 1))
            dve.wait_ge(e.unit_used, u1 + 1)
            dve.tensor_copy(e.sq[0:rest, :].rearrange("p (a t) -> p a t", a=2), rest_ps[0:rest, :, 0:TH])\
                .then_inc(rest_copied.sem, 1)
            rest_turned.wait(dve, 1)
            pads.wait(dve, 3)
            dve.tensor_tensor(z[:, 0:4, groups * 512:cols], stat_ps[:, 0:4 * rest].rearrange("p (t n) -> p t n", t=4),
                              e.rs_col[:, 0:4].unsqueeze(2).to_broadcast([P, 4, rest]), ALU.mult)
            dve.tensor_scalar(z[0:TS, 4, groups * 512:cols], stat_ps[0:TS, 4 * rest:5 * rest], e.rs_col[0:TS, 4:5], None, ALU.mult)
    z_ready.base += 4 * groups
    z_act.base += 3 * groups
    z_dve.base += 2 * groups
    pads.base += 3
    rest_copied.base += 1
    rest_turned.base += 1
    e.h_n += 1
    e.norm_n += 1


def split_hi4(e, act, base, g, side):
    slot = (base + side) % 2
    act.wait_ge(e.landed[slot], g * 32 + 16 * ((base + side) // 2 + 1))
    act.wait_ge(e.unit_used, g * 4 + (base + side - 1))
    act.activation(e.w_hi[slot][:, 0:1024], e.w_stage[slot][:, 0:1024], ACT.Copy).then_inc(e.hi_done, 1)


def split_lo4(e, dve, base, g, side):
    slot = (base + side) % 2
    dve.wait_ge(e.hi_done, g * 4 + (base + side + 1))
    dve.tensor_tensor(e.w_lo[slot][:, 0:1024], e.w_stage[slot][:, 0:1024],
                      e.w_hi[slot][:, 0:1024].bitcast(F32), ALU.subtract).then_inc(e.lo_done, 1)


def rope(chain, eng, x, heads, cos, sin, t_cos, t_sin):
    v = x.rearrange("p t (h d) -> p t h d", d=HD)
    both = v[:, :, :, 0:16]
    shape = [P, NT, heads, 16]
    c4, s4 = (s.unsqueeze(2).to_broadcast(shape) for s in (cos, sin))
    tc, ts_ = (s[:, 0:NT * heads * 16].rearrange("p (t h j) -> p t h j", t=NT, j=16) for s in (t_cos, t_sin))
    chain(eng.tensor_tensor(tc, both, c4, ALU.mult))
    chain(eng.tensor_tensor(ts_, both, s4, ALU.mult))
    chain(eng.tensor_tensor(v[:, :, :, 0:8], tc[:, :, :, 0:8], ts_[:, :, :, 8:16], ALU.subtract))
    chain(eng.tensor_tensor(v[:, :, :, 8:16], tc[:, :, :, 8:16], ts_[:, :, :, 0:8], ALU.add))


def turn_stage(e, name, z, jobs, q_parts, k_parts, stores):
    nc = e.nc
    q_steps, k_steps = 4 * len(q_parts), 4 * len(k_parts)
    n_raw = sum(job[3] == "raw" for job in jobs)
    with ExitStack() as ctx:
        t_c = [ctx.enter_context(nc.sbuf_tensor(f"{name}_rope{i}", [P, NT * 16 * n], F32))
               for i, n in enumerate((HEADS, HEADS, KV, KV))]
        ps = [ctx.enter_context(nc.psum_tensor(f"{name}_turn_ps{i}", [P, 512], F32)) for i in range(6)]
        q_rot, k_rot, turned, read_act, read_dve = e.sig("q_rotated", "k_rotated", "qk_turned", "turn_read_act",
                                                         "turn_read_dve")
        block = ctx.enter_context(nc.Block())

        @block.tensor
        def _(pe):
            for i, (src, _, _, need) in enumerate(jobs):
                if i >= 3:
                    (read_act if (i - 3) % 2 else read_dve).wait(pe, (i - 3) // 2 + 1)
                if need == "k":
                    k_rot.wait(pe, k_steps)
                if need == "q":
                    q_rot.wait(pe, q_steps)
                b = 2 * (i % 3)
                for t in range(NT):
                    n = src(t).shape[1]
                    dst = ps[b][0:n, t * P:(t + 1) * P] if t < NT - 1 else ps[b + 1][0:n, 0:P]
                    m = pe.transpose(dst, src(t), e.ident[:, :])
                m.then_inc(turned.sem, 1)

        def copy_out(eng, i, copy, read):
            _, dst, scale, _ = jobs[i]
            turned.wait(eng, i + 1)
            b = 2 * (i % 3)
            n = jobs[i][0](0).shape[1]
            for at in range(0, P, n):
                copy(dst[at:at + n, 0:TP], ps[b][0:n, :], scale)
                ins = copy(dst[at:at + n, TP:T], ps[b + 1][0:n, 0:TS], scale)
            ins.then_inc(read.sem, 1)

        @block.scalar
        def _(act):
            for i in range(1, len(jobs), 2):
                copy_out(act, i, lambda o, x, s: act.activation(o, x, ACT.Copy, scale=s), read_act)

        @block.vector
        def _(dve):
            for i in range(0, len(jobs), 2):
                if i == n_raw:
                    chain = Chain(dve, q_rot)
                    turned.wait(dve, n_raw) if n_raw else None
                    for col, heads in q_parts:
                        rope(chain, dve, z[:, :, col:col + heads * HD], heads, e.cos, e.sin, t_c[0], t_c[1])
                copy_out(dve, i, lambda o, x, s: dve.tensor_scalar(o, x, s, None, ALU.mult), read_dve)

        @block.gpsimd
        def _(pool):
            chain = Chain(pool, k_rot)
            for col, heads in k_parts:
                rope(chain, pool, z[:, :, col:col + heads * HD], heads, e.cos, e.sin, t_c[2], t_c[3])

        @block.sync
        def _(sp):
            k_rot.wait(sp, k_steps)
            for dst, src in stores:
                sp.dma_start(dst, src).then_inc(e.stored, 16)
                e.stores += 1
    for s, n in ((q_rot, q_steps), (k_rot, k_steps), (turned, len(jobs)), (read_act, len(jobs) // 2),
                 (read_dve, (len(jobs) + 1) // 2)):
        s.base += n


ORDER = (0, 1, 2, 3)
AHEAD = 3


def attention(e, name, qt, kt, v_of, bias, gate, o, accumulate, prefetch):
    nc = e.nc
    with ExitStack() as ctx:
        def sb(n, shape, dt=F32):
            return ctx.enter_context(nc.sbuf_tensor(f"{name}_{n}", shape, dt))

        def psb(n):
            return ctx.enter_context(nc.psum_tensor(f"{name}_{n}", [P, 512], F32))
        qs = [sb(f"qs{c}", [P, TP]) for c in range(2)]
        probs, probs_t = [sb(f"p{i}", [P, TP]) for i in range(4)], [sb(f"pt{i}", [P, TP]) for i in range(2)]
        neg_max, sums, weight = sb("neg_max", [P, 2, 8]), sb("sums", [P, 2, 8]), sb("weight", [P, 8])
        part = sb("part", [P, 2, 8, HD])
        s_ps, t_ps = [psb(f"s_ps{i}") for i in range(4)], [psb(f"t_ps{i}") for i in range(2)]
        o_ps = [psb(f"o_ps{c}") for c in range(2)]
        q_here, s_ready, max_done, p_ready, t_ready, even_copied, odd_copied, pv_done, o_read, o_chain, o_added = e.sig(
            "q_staged", "scores_ready", "max_done", "probs_ready", "probs_turned", "even_probs_copied",
            "odd_probs_copied", "pv_done", "o_read", "o_chain", "o_added")
        links = 2 if gate else 1
        items = [(c, par, i) for c in range(2) for par in range(2) for i in ORDER]
        M = len(items)
        block = ctx.enter_context(nc.Block())

        def width_of(m):
            return (items[m % M][2] + 1) * P

        def column_of(m):
            return 4 * items[m % M][1] + items[m % M][2]

        def copied(eng, g, m):
            (odd_copied if m % 2 else even_copied).wait(eng, g * (M // 2) + (m // 2 + 1))

        def copy(eng, g, m, do):
            t_ready.wait(eng, g * M + (m + 1))
            if not first(g) or m >= 2:
                pv_done.wait(eng, g * M + (m - 1))
            do(probs_t[m % 2][:, 0:width_of(m)], t_ps[m % 2][:, 0:width_of(m)])\
                .then_inc((odd_copied if m % 2 else even_copied).sem, 1)

        def loop(eng, body):
            body(0, False)
            with eng.Fori(1, 3) as g:
                body(g, False)
            body(3, True)

        def first(g):
            return isinstance(g, int) and g == 0

        @block.sync
        def _(sp):
            prefetch(sp)

        @block.gpsimd
        def _(pool):
            def add(g, c, back):
                o_read.wait(pool, g * 2 + (c + 1 - 2 * back))
                for par in range(2):
                    dst = o[:, :, ds(g * HD + (8 * c + 4 * par - back) * HD, HD)]
                    ins = pool.tensor_tensor(dst, dst, part[:, c, 4 * par:4 * par + 4, :], ALU.add)
                ins.then_inc(o_added.sem, 1)

            def body(g, last):
                for c in range(2):
                    if not first(g):
                        s_ready.wait(pool, g * M + (8 * c + 8 - M))
                    src = qt[:, 4 * c + g, 0:TP] if isinstance(g, int) else qt[:, ds(g + 4 * c, 1), 0:TP]
                    pool.tensor_copy(qs[c][:, :], src).then_inc(q_here.sem, 1)
                    if accumulate and not first(g):
                        add(g, c, 1)
                if accumulate and last:
                    for c in range(2):
                        add(g, c, 0)

            if accumulate:
                pool.memset(part[:, :, :, :], 0.0).then_inc(o_added.sem, 1)
            loop(pool, body)

        @block.tensor
        def _(pe):
            def scores(g, m):
                c, par, i = items[m % M]
                rows, width = slice(par * HD, (par + 1) * HD), (i + 1) * P
                if m % 8 == 0:
                    q_here.wait(pe, g * 2 + (m // 8 + 1))
                if not first(g) or m >= 4:
                    p_ready.wait(pe, g * M + (m - 3))
                bank = s_ps[m % 4]
                pe.matmul(bank[:, 0:width], qs[c][rows, i * P:(i + 1) * P], kt[rows, c, 0:width], start=True, stop=False)
                if bias is None:
                    mm = pe.matmul(bank[:, i * P:width], e.ident_b[:, :], e.causal_b[:, :], start=False, stop=True)
                else:
                    mm = pe.matmul(bank[:, 0:width], e.ident_b[:, :], bias[:, i, 0:width], start=False, stop=True)
                mm.then_inc(s_ready.sem, 1)

            def turn(g, m):
                p_ready.wait(pe, g * M + (m + 1))
                if not first(g) or m >= 2:
                    copied(pe, g, m - 2)
                for kc in range(width_of(m) // P):
                    mm = pe.transpose(t_ps[m % 2][:, kc * P:(kc + 1) * P], probs[m % 4][:, kc * P:(kc + 1) * P], e.ident[:, :])
                mm.then_inc(t_ready.sem, 1)

            def values(g, m):
                c, par, i = items[m % M]
                copied(pe, g, m)
                if m % 8 == 0 and not first(g):
                    o_read.wait(pe, g * 2 + (c - 1))
                at = column_of(m)
                for kc in range(i + 1):
                    mm = pe.matmul(o_ps[c][:, at * HD:(at + 1) * HD], probs_t[m % 2][:, kc * P:(kc + 1) * P],
                                   v_of(kc, 2 * c + par), start=kc == 0, stop=kc == i)
                mm.then_inc(pv_done.sem, 1)

            def body(g, last):
                if first(g):
                    warm_up(e, pe, o_ps[0][:, 0:P], 64)
                    for m in range(AHEAD):
                        scores(g, m)
                for m in range(M):
                    if m + AHEAD < M or not last:
                        scores(g, m + AHEAD)
                    turn(g, m)
                    if m >= 1 or not first(g):
                        values(g, m - 1)
                if last:
                    values(g, M - 1)
            loop(pe, body)

        @block.scalar
        def _(act):
            def exp(g, m):
                c, at, width = m // 8 % 2, column_of(m), width_of(m)
                max_done.wait(act, g * M + (m + 1))
                if not first(g) or m >= 4:
                    t_ready.wait(act, g * M + (m - 3))
                act.activation(probs[m % 4][:, 0:width], s_ps[m % 4][:, 0:width], ACT.Exp,
                               bias=neg_max[:, c, at:at + 1], accum_out=sums[:, c, at:at + 1]).then_inc(p_ready.sem, 1)

            def body(g, last):
                if first(g):
                    for m in range(AHEAD - 1):
                        exp(g, m)
                for m in range(M):
                    if m + AHEAD - 1 < M or not last:
                        exp(g, m + AHEAD - 1)
                    if m % 2:
                        copy(act, g, m, lambda dst, src: act.activation(dst, src, ACT.Copy))
            loop(act, body)

        @block.vector
        def _(dve):
            def maximum(g, m):
                at = column_of(m)
                s_ready.wait(dve, g * M + (m + 1))
                dve.tensor_reduce(neg_max[:, m // 8 % 2, at:at + 1], s_ps[m % 4][:, 0:width_of(m)], AX.X, ALU.max,
                                  negate=True).then_inc(max_done.sem, 1)

            def output(g, c, back):
                k = [0]

                def link(ins):
                    ins.then_inc(o_chain.sem, 1)
                    k[0] += 1
                    o_chain.wait(dve, g * (2 * links) + ((c - 2 * back) * links + k[0]))
                p_ready.wait(dve, g * M + (8 * c + 8 - M * back))
                link(dve.reciprocal(weight[:, :], sums[:, c, :]))
                if gate is not None:
                    gates, branch = gate
                    for par in range(2):
                        col = g * 3 + (24 * c + 12 * par + branch - 3 * back)
                        w = weight[:, 4 * par:4 * par + 4].unsqueeze(2)
                        ins = dve.tensor_tensor(w, w, gates[:, 0:4, ds(col, 1)], ALU.mult)
                    link(ins)
                pv_done.wait(dve, g * M + (8 * c + 8 - M * back))
                src = o_ps[c][:, :].rearrange("p (m d) -> p m d", d=HD)
                w = weight[:, :].unsqueeze(2)
                if accumulate:
                    turn = g * 2 + (c - 2 * back)
                    o_added.wait(dve, max(turn, 1) if isinstance(turn, int) else turn)
                    dve.tensor_tensor(part[:, c, :, :], src, w.to_broadcast([P, 8, HD]), ALU.mult).then_inc(o_read.sem, 1)
                else:
                    for par in range(2):
                        ins = dve.tensor_tensor(o[:, :, ds(g * HD + (8 * c + 4 * par - back) * HD, HD)],
                                                src[:, 4 * par:4 * par + 4, :],
                                                w[:, 4 * par:4 * par + 4, :].to_broadcast([P, 4, HD]), ALU.mult)
                    ins.then_inc(o_read.sem, 1)
                o_read.wait(dve, g * 2 + (c + 1 - 2 * back))
                assert k[0] == links, (k, links)

            def body(g, last):
                if first(g):
                    for m in range(AHEAD):
                        maximum(g, m)
                for m in range(M):
                    if m + AHEAD < M or not last:
                        maximum(g, m + AHEAD)
                    if m % 2 == 0:
                        copy(dve, g, m, dve.tensor_copy)
                    if m == 2 and not first(g):
                        output(g, 1, 1)
                    if m == 10:
                        output(g, 0, 0)
                if last:
                    output(g, 1, 0)
            loop(dve, body)
    for s, n in ((q_here, 8), (s_ready, 64), (max_done, 64), (p_ready, 64), (t_ready, 64), (even_copied, 32),
                 (odd_copied, 32), (pv_done, 64), (o_read, 8), (o_chain, 8 * links), (o_added, 9 if accumulate else 0)):
        s.base += n


def out_projection(e, name, o, o_sample, x_base):
    nc = e.nc
    u0 = e.stream.start(f"{name}.out")
    with ExitStack() as ctx:
        ot_hi = ctx.enter_context(nc.sbuf_tensor(f"{name}_ot_hi", [P, KC, T], FR))
        ot_lo = ctx.enter_context(nc.sbuf_tensor(f"{name}_ot_lo", [P, KC, T], FR))
        t_ps = [ctx.enter_context(nc.psum_tensor(f"{name}_ot_ps{i}", [P, 512], F32)) for i in range(2)]
        y_ps = [ctx.enter_context(nc.psum_tensor(f"{name}_y_ps{i}", [P, 2, 512], F32)) for i in range(2)]
        turned, hi_done, lo_done = e.sig("o_turned", "o_hi_done", "o_lo_done")
        block = ctx.enter_context(nc.Block())

        @block.sync
        def _(sp):
            load_units(e, sp, u0 + 2, min(u0 + KC + 2, e.stream.total))

        @block.gpsimd
        def _(pool):
            square_sum_pool(e, pool, x_base)

        @block.tensor
        def _(pe):
            for j in range(KC):
                if j >= 2:
                    lo_done.wait(pe, j - 1)
                for i in range(4):
                    m = pe.transpose(t_ps[j % 2][:, i * P:(i + 1) * P], o[:, i, j * P:(j + 1) * P], e.ident[:, :])
                m.then_inc(turned.sem, 1)

            def unit(q, side, first):
                slot = (u0 + side) % 2
                pe.wait_ge(e.lo_done, q * 2 + (u0 + side + 1))
                if not first:
                    pe.wait_ge(e.x_done, q * 2 + (x_base + side - 1))
                for k in range(KC):
                    if first and side == 0:
                        lo_done.wait(pe, k + 1 if k < KC - 1 else KC)
                        if k == 0:
                            lo_done.wait(pe, KC + 1)
                    for th in range(2):
                        t = slice(th * TH, (th + 1) * TH)
                        m = three_passes(pe, y_ps[side][:, th, 0:TH], e.w_hi[slot][:, k * P:(k + 1) * P],
                                         e.w_lo[slot][:, k * P:(k + 1) * P], ot_hi[:, k, t], ot_lo[:, k, t],
                                         k == 0, k == KC - 1)
                m.then_inc(e.unit_used, 1)

            for side in range(2):
                unit(0, side, True)
            with pe.Fori(1, KC // 2) as q:
                for side in range(2):
                    unit(q, side, False)

        @block.scalar
        def _(act):
            for j in range(KC):
                turned.wait(act, j + 1)
                act.activation(ot_hi[:, j, 0:TP], t_ps[j % 2][:, :], ACT.Copy).then_inc(hi_done.sem, 1)
            act.activation(ot_hi[:, :, TP:T], o_sample[:, :, :], ACT.Copy).then_inc(hi_done.sem, 1)
            split_hi(e, act, u0 + 1, 0, KC * P)
            with act.Fori(1, KC // 2) as q:
                for side in range(2):
                    split_hi(e, act, u0 + side, q, KC * P)
            if u0 + KC < e.stream.total:
                split_hi(e, act, u0 + KC, 0, e.cols_of(u0 + KC))

        @block.vector
        def _(dve):
            for j in range(KC):
                hi_done.wait(dve, j + 1)
                dve.tensor_tensor(ot_lo[:, j, 0:TP], t_ps[j % 2][:, :], ot_hi[:, j, 0:TP].bitcast(F32), ALU.subtract)\
                   .then_inc(lo_done.sem, 1)
            hi_done.wait(dve, KC + 1)
            dve.tensor_tensor(ot_lo[:, :, TP:T], o_sample[:, :, :], ot_hi[:, :, TP:T].bitcast(F32), ALU.subtract)\
               .then_inc(lo_done.sem, 1)
            split_lo(e, dve, u0 + 1, 0, KC * P)

            def x_of(u, side, i):
                dve.wait_ge(e.unit_used, u)
                if isinstance(i, int):
                    xi = e.x[:, i, :].rearrange("p (a t) -> p a t", a=2)
                else:
                    xi = e.x[:, ds(i, 1), :].rearrange("p o (a t) -> p (o a) t", a=2)
                dve.tensor_tensor(xi, y_ps[side][:, :, 0:TH], xi, ALU.add).then_inc(e.x_done, 1)

            with dve.Fori(1, KC // 2) as q:
                split_lo(e, dve, u0, q, KC * P)
                x_of(q * 2 + (u0 - 1), 0, q * 2 - 2)
                split_lo(e, dve, u0 + 1, q, KC * P)
                x_of(q * 2 + u0, 1, q * 2 - 1)
            if u0 + KC < e.stream.total:
                split_lo(e, dve, u0 + KC, 0, e.cols_of(u0 + KC))
            x_of(u0 + KC - 1, 0, KC - 2)
            x_of(u0 + KC, 1, KC - 1)
    turned.base += KC
    hi_done.base += KC + 1
    lo_done.base += KC + 1
    e.x_rows += KC


def compress(e, z, kc_t, vc_prompt, vc_sample):
    nc = e.nc
    NB, PB = 41, 8
    PAIRS = 32
    LG, W1_SLOTS = 8, 4
    UNITS = 2 * PAIRS // LG
    with ExitStack() as ctx:
        def sb(n, shape, dt=F32):
            return ctx.enter_context(nc.sbuf_tensor(f"cmp_{n}", shape, dt))

        def psb(n, shape=(P, 512)):
            return ctx.enter_context(nc.psum_tensor(f"cmp_{n}", list(shape), F32))
        kt = sb("kt", [P, 2, KV, NB, PAIRS])
        w1 = [sb(f"w1_{s}", [P, LG * P]) for s in range(W1_SLOTS)]
        w2 = sb("w2", [P, 2, HD])
        pages = [sb(f"page{i}", [P, 512]) for i in range(4)]
        pos_rows = sb("pos_rows", [64, 2, 2, HD])
        bias = sb("bias", [P, 2])
        hidden = [sb(f"hidden{c}", [P, KV, NB - 1]) for c in range(2)]
        t_ps = [psb(f"t_ps{i}") for i in range(4)]
        pre_ps = [psb(f"pre_ps{c}") for c in range(2)]
        k_ps, v_ps = psb("k_ps"), psb("v_ps")
        w1_in0, w1_in1, w1_in2, w1_in3, w1_used, pos_in, page_in0, page_in1, page_in2, page_in3, turned, even_done, \
            odd_done, bias_done, hid_done, small_done = e.sig(
                "cmp_w1_landed0", "cmp_w1_landed1", "cmp_w1_landed2", "cmp_w1_landed3", "cmp_w1_used",
                "cmp_pos_landed", "cmp_page_landed0", "cmp_page_landed1", "cmp_page_landed2", "cmp_page_landed3",
                "cmp_turned", "cmp_even_done", "cmp_odd_done", "cmp_bias_done", "cmp_hidden_done", "cmp_small_done")
        w1_in, page_in = (w1_in0, w1_in1, w1_in2, w1_in3), (page_in0, page_in1, page_in2, page_in3)
        block = ctx.enter_context(nc.Block())
        TURNS = 22

        def emptied(eng, n):
            (odd_done if n % 2 else even_done).wait(eng, n // 2 + 1)

        def load_w1(eng, u):
            c, lg = u // (UNITS // 2), u % (UNITS // 2)
            if u >= W1_SLOTS:
                w1_used.wait(eng, u - W1_SLOTS + 1)
            view = e.nsa_cmp_w1[0, c].rearrange("(l a) d h -> (a d) l h", a=2)
            eng.dma_start(w1[u % W1_SLOTS][:, :].rearrange("p (l h) -> p l h", l=LG),
                          view[:, lg * LG:(lg + 1) * LG, :]).then_inc(w1_in[u % W1_SLOTS].sem, 16)

        @block.sync
        def _(sp):
            sp.dma_start(pos_rows[:, :, 0, :], e.nsa_cmp_pos[0]).then_inc(pos_in.sem, 16)
            sp.dma_start(pos_rows[:, :, 1, :], e.nsa_cmp_pos[0]).then_inc(pos_in.sem, 16)
            sp.dma_start(w2[:, :, :], e.nsa_cmp_w2[0].rearrange("c h d -> h c d")).then_inc(pos_in.sem, 16)
            for i in range(16):
                page = sp.value_load(e.table[0:1, i:i + 1], min_val=0, max_val=e.cache_nsa_cmp.shape[1] - 1)
                if i >= 4:
                    turned.wait(sp, 2 + i - 3)
                sp.dma_start(pages[i % 4][:, :], e.cache_nsa_cmp[0, ds(page, 1)].rearrange("o p c k d -> (o p) (c k d)"))\
                  .then_inc(page_in[i % 4].sem, 16)
            for u in range(W1_SLOTS, UNITS):
                load_w1(sp, u)
            out = e.nsa_cmp_p[0, 0].rearrange("(t p) c k d -> p t (c k d)", p=P)
            sp.dma_start(out, z[:, 0:4, 1024:1536]).then_inc(e.stored, 16)
            sp.dma_start(e.nsa_cmp_s[0].rearrange("b s c k d -> (b s) (c k d)"), z[0:TS, 4, 1024:1536]).then_inc(e.stored, 16)
            sp.dma_start(e.nsa_win_s[0, :, 0:255], e.state_nsa_win[0, :, 1:256]).then_inc(e.stored, 16)
            e.stores += 3

        def spread(eng, n, copy):
            turned.wait(eng, n + 1)
            done, bank = (odd_done if n % 2 else even_done), t_ps[n % 4]
            for par in range(2):
                for a in range(2):
                    rows, to = slice(par * HD, (par + 1) * HD), slice(a * HD, (a + 1) * HD)
                    if n < 2:
                        if par != a:
                            continue
                        dst = kt[rows, n, :, NB - 1, :]
                        src = bank[rows, a:64:2].unsqueeze(1).to_broadcast([HD, KV, PAIRS])
                    elif n < 18:
                        b = PB + 2 * (n - 2)
                        dst = kt[to, :, par::2, b:b + 2, :].rearrange("p c k n l -> p (c k) (n l)")
                        src = bank[rows, :].rearrange("p (j s) -> p j s", j=4)[:, :, a::2]
                    else:
                        c, chunk = (n - 18) // 2, (n - 18) % 2
                        dst = kt[to, c, 2 * chunk + par, 0:PB, :].rearrange("p n l -> p (n l)")
                        src = bank[rows, a::2]
                    ins = copy(dst, src)
            ins.then_inc(done.sem, 1)

        @block.scalar
        def _(act):
            for n in range(1, TURNS, 2):
                spread(act, n, lambda dst, src: act.activation(dst, src, ACT.Copy))
                if n // 2 < W1_SLOTS:
                    load_w1(act, n // 2)
            for c in range(2):
                bias_done.wait(act, c + 1)
                act.activation(hidden[c][:, :, :], pre_ps[c][:, 0:KV * NB].rearrange("p (k n) -> p k n", k=KV)[:, :, 0:NB - 1],
                               ACT.Gelu_apprx_tanh, bias=bias[:, c:c + 1]).then_inc(hid_done.sem, 1)

        @block.tensor
        def _(pe):
            pos_in.wait(pe, 48)
            for n in range(TURNS):
                if n >= 4:
                    emptied(pe, n - 4)
                bank = t_ps[n % 4]
                if n < 2:
                    m = pe.transpose(bank[:, 0:64], pos_rows[:, n, :, :].rearrange("p a d -> p (a d)"), e.ident[0:64, 0:64])
                elif n < 18:
                    i = n - 2
                    page_in[i % 4].wait(pe, 16 * (i // 4 + 1))
                    for j in range(4):
                        m = pe.transpose(bank[:, j * P:(j + 1) * P], pages[i % 4][:, j * P:(j + 1) * P], e.ident[:, :])
                else:
                    col = 1024 + (n - 18) * P
                    for t in range(4):
                        m = pe.transpose(bank[:, t * P:(t + 1) * P], z[:, t, col:col + P], e.ident[:, :])
                m.then_inc(turned.sem, 1)
            emptied(pe, TURNS - 2)
            emptied(pe, TURNS - 1)
            for u in range(UNITS):
                w1_in[u % W1_SLOTS].wait(pe, 16 * (u // W1_SLOTS + 1))
                c = u // (UNITS // 2)
                for l in range(LG):
                    pair = u % (UNITS // 2) * LG + l
                    m = pe.matmul(pre_ps[c][:, 0:KV * NB], w1[u % W1_SLOTS][:, l * P:(l + 1) * P],
                                  kt[:, c, :, :, pair], start=pair == 0, stop=pair == PAIRS - 1)
                m.then_inc(w1_used.sem, 1)
            for par in range(2):
                hid_done.wait(pe, 1)
                m = pe.matmul(k_ps[par * HD:(par + 1) * HD, 0:2 * (NB - 1)], w2[:, 0, :], hidden[0][:, par::2, :],
                              start=True, stop=True)
            m.then_inc(small_done.sem, 1)
            hid_done.wait(pe, 2)
            for kv in range(KV):
                pe.matmul(v_ps[0:PB, kv * HD:(kv + 1) * HD], hidden[1][:, kv, 0:PB], w2[:, 1, :], start=True, stop=True)
            for kv in range(KV):
                m = pe.matmul(v_ps[0:32, 256 + kv * HD:256 + (kv + 1) * HD], hidden[1][:, kv, PB:NB - 1], w2[:, 1, :],
                              start=True, stop=True)
            m.then_inc(small_done.sem, 1)

        @block.vector
        def _(dve):
            for n in range(0, TURNS, 2):
                spread(dve, n, dve.tensor_copy)
            for c in range(2):
                w1_used.wait(dve, UNITS // 2 * (c + 1))
                dve.tensor_copy(bias[:, c:c + 1], pre_ps[c][:, NB - 1:NB]).then_inc(bias_done.sem, 1)
            small_done.wait(dve, 1)
            dve.tensor_copy(kc_t[:, :, :].rearrange("p c n -> p (c n)"), k_ps[:, 0:2 * (NB - 1)])
            small_done.wait(dve, 2)
            dve.tensor_copy(vc_prompt[0:PB, :], v_ps[0:PB, 0:256])
            dve.tensor_copy(vc_sample[0:32, :], v_ps[0:32, 256:512])


def compressed_attention(e, qt_raw, kc_t, vc_prompt, gates, o):
    nc = e.nc
    with ExitStack() as ctx:
        def sb(n, shape, dt=F32):
            return ctx.enter_context(nc.sbuf_tensor(f"ca_{n}", shape, dt))

        def psb(n):
            return ctx.enter_context(nc.psum_tensor(f"ca_{n}", [P, 512], F32))
        kc_bd, v_bd = sb("kc_bd", [P, 2, 2, 8]), sb("v_bd", [P, HEADS, HD])
        s = sb("s", [P, 4, HEADS, 8])
        m_sb, r_sb, p_t = sb("m", [P, 4, HEADS]), sb("r", [P, 4, HEADS]), sb("pt", [P, 4, P])
        s_ps, t_ps, v_ps = psb("s_ps"), psb("t_ps"), psb("v_ps")
        o_ps = [psb(f"o_ps{i}") for i in range(4)]
        step, s_ready, v_ready, e_done, turned, o_ready, even_copied, odd_copied, zeroed = e.sig(
            "ca_step", "ca_scores", "ca_values_spread", "ca_exp_done", "ca_turned", "ca_out_ready", "ca_even_copied",
            "ca_odd_copied", "ca_keys_spread")
        STEPS_TO_SHIFTED, STEPS_TO_PROBS = KV + 3, KV + 10
        block = ctx.enter_context(nc.Block())

        @block.gpsimd
        def _(pool):
            chain = Chain(pool, zeroed)
            chain(pool.memset(kc_bd[:, :, :, :], 0.0))
            for par in range(2):
                rows = slice(par * HD, (par + 1) * HD)
                chain(pool.tensor_copy(kc_bd[rows, :, par, :], kc_t[rows, :, 0:8]))

        @block.tensor
        def _(pe):
            pe.matmul(v_ps[:, 0:256], e.rep[0:8, :], vc_prompt[0:8, :], start=True, stop=True).then_inc(v_ready.sem, 1)
            zeroed.wait(pe, 3)
            for i in range(4):
                for j in range(8):
                    m = pe.matmul(s_ps[:, (i * 8 + j) * 16:(i * 8 + j + 1) * 16], qt_raw[:, j, i * P:(i + 1) * P],
                                  kc_bd[:, j // 4, :, :].rearrange("p a n -> p (a n)"), start=True, stop=True)
            m.then_inc(s_ready.sem, 1)
            warm_up(e, pe, o_ps[0][:, 0:P], 80)
            step.wait(pe, STEPS_TO_PROBS)
            for i in range(4):
                m = pe.transpose(t_ps[:, i * P:(i + 1) * P], s[:, i, :, :].rearrange("p h n -> p (h n)"), e.ident[:, :])
            m.then_inc(turned.sem, 1)
            step.wait(pe, STEPS_TO_PROBS + 1)
            for n in range(8):
                i, half = n // 2, n % 2
                if n >= 4:
                    (odd_copied if half else even_copied).wait(pe, (n - 4) // 2 + 1)
                pe.matmul(o_ps[n % 4][:, :], p_t[:, i, :], v_bd[:, 8 * half:8 * half + 8, :].rearrange("p h d -> p (h d)"),
                          start=True, stop=True).then_inc(o_ready.sem, 1)

        @block.scalar
        def _(act):
            step.wait(act, STEPS_TO_SHIFTED)
            act.activation(s[:, :, :, :], s[:, :, :, :], ACT.Exp).then_inc(e_done.sem, 1)
            for n in range(1, 8, 2):
                o_ready.wait(act, n + 1)
                act.activation(o[:, n // 2, 512:1024], o_ps[n % 4][:, :], ACT.Copy).then_inc(odd_copied.sem, 1)

        @block.vector
        def _(dve):
            chain = Chain(dve, step)
            v_ready.wait(dve, 1)
            for kv in range(KV):
                chain(dve.tensor_tensor(v_bd[:, 4 * kv:4 * kv + 4, :],
                                        v_ps[:, kv * HD:(kv + 1) * HD].unsqueeze(1).to_broadcast([P, 4, HD]),
                                        e.hsel[:, 4 * kv:4 * kv + 4].unsqueeze(2).to_broadcast([P, 4, HD]), ALU.mult))
            wide = [P, 4, HEADS, 8]
            s_ready.wait(dve, 1)
            chain(dve.tensor_tensor(s[:, :, :, :], s_ps[:, :].rearrange("p (i h n) -> p i h n", i=4, n=8),
                                    e.cadd[:, :, :].unsqueeze(2).to_broadcast(wide), ALU.add))
            chain(dve.tensor_reduce(m_sb[:, :, :], s[:, :, :, :], AX.X, ALU.max))
            chain(dve.tensor_tensor(s[:, :, :, :], s[:, :, :, :], m_sb[:, :, :].unsqueeze(3).to_broadcast(wide), ALU.subtract))
            assert chain.n == STEPS_TO_SHIFTED
            e_done.wait(dve, 1)
            chain(dve.tensor_tensor(s[:, :, :, :], s[:, :, :, :], e.c01[:, :, :].unsqueeze(2).to_broadcast(wide), ALU.mult))
            chain(dve.tensor_reduce(r_sb[:, :, :], s[:, :, :, :], AX.X, ALU.add))
            chain(dve.tensor_scalar(r_sb[:, :, :], r_sb[:, :, :], 1e-30, None, ALU.max))
            chain(dve.reciprocal(r_sb[:, :, :], r_sb[:, :, :]))
            for c in range(2):
                r = r_sb[:, :, 8 * c:8 * c + 8].rearrange("p i (g a) -> p i a g", a=2)
                for par in range(2):
                    ins = dve.tensor_tensor(r[:, :, par, :], r[:, :, par, :],
                                            gates[:, 0:4, 24 * c + 12 * par:24 * c + 12 * par + 12:3], ALU.mult)
                chain(ins)
            chain(dve.tensor_tensor(s[:, :, :, :], s[:, :, :, :], r_sb[:, :, :].unsqueeze(3).to_broadcast(wide), ALU.mult))
            assert chain.n == STEPS_TO_PROBS
            turned.wait(dve, 1)
            chain(dve.tensor_copy(p_t[:, :, :].rearrange("p i q -> p (i q)"), t_ps[:, :]))
            for n in range(0, 8, 2):
                o_ready.wait(dve, n + 1)
                dve.tensor_copy(o[:, n // 2, 0:512], o_ps[n % 4][:, :]).then_inc(even_copied.sem, 1)


def sample_setup(e, qt_raw, qt, sb_):
    nc = e.nc
    spread, = e.sig("sample_q_spread")
    block_ctx = ExitStack()
    with block_ctx:
        block = block_ctx.enter_context(nc.Block())

        @block.vector
        def _(dve):
            dve.memset(sb_.qbd[:, :], 0.0)
            if qt_raw is not None:
                dve.memset(sb_.qz[:, :], 0.0)
            dve.memset(e.start_mark[:, :], 0.0).then_inc(spread.sem, 1)
            spread.wait(dve, 1)
            for c in range(2):
                for par in range(2):
                    rows, at = slice(par * HD, (par + 1) * HD), 8 * c + 4 * par
                    src = qt[rows, 4 * c:4 * c + 4, TP:T].rearrange("p g b -> p b g")
                    dst = sb_.qbd[rows, 0:2176].rearrange("p (b s) -> p b s", s=272)[:, :, c * P + at:c * P + at + 4]
                    dve.tensor_copy(dst, src)
                    if qt_raw is not None:
                        src = qt_raw[rows, 4 * c:4 * c + 4, TP:T].rearrange("p g b -> p b g")
                        dst = sb_.qz[rows, c * P:(c + 1) * P].rearrange("p (b h) -> p b h", h=16)[:, :, at:at + 4]
                        dve.tensor_copy(dst, src)
    spread.base += 1


def sample_loads(e, sp, rows, rows_of, table=None):
    landed = e.sig(*[f"sample_rows_landed{i}" for i in range(4)])
    sp.wait_ge(e.stored, 16 * e.stores)
    for i in range(16):
        page = None
        if table is not None:
            page = sp.value_load(table[0:1, i:i + 1], min_val=0, max_val=e.cache_nsa_slc.shape[1] - 1)
        if i >= 4:
            landed[i % 4].wait(sp, 16 * (i // 4))
        sp.dma_start(rows[i], rows_of(i, page)).then_inc(landed[i % 4].sem, 16)


def sample_attention(e, name, sb_, rows, kt_new, v_new, gate_w, first, bias=None):
    nc = e.nc
    with ExitStack() as ctx:
        def sb(n, shape, dt=F32):
            return ctx.enter_context(nc.sbuf_tensor(f"{name}_{n}", shape, dt))

        def psb(n):
            return ctx.enter_context(nc.psum_tensor(f"{name}_{n}", [P, 512], F32))
        kt = sb("kt", [P, 2, 2, 257])
        prob, p_new, neg_max, r = sb("prob", [P, 257]), sb("p_new", [P, TS]), sb("neg_max", [P, 1]), sb("r", [P, 1])
        p_t, p_nt = sb("p_t", [P, 2, 9 * P]), sb("p_nt", [TS, P])
        k_ps = [psb(f"k_ps{i}") for i in range(2)]
        s_ps, t_ps, o_ps = psb("s_ps"), psb("t_ps"), psb("o_ps")
        landed = e.sig(*[f"sample_rows_landed{i}" for i in range(4)])
        turned, copied, s_ready, used, step, exp_done, p_ready, p_turned, p_copied, o_ready = e.sig(
            "sample_k_turned", "sample_k_copied", "sample_scores", "sample_k_used", "sample_step", "sample_exp_done",
            "sample_probs", "sample_probs_turned", "sample_probs_copied", "sample_out_ready")
        zeroed, = e.sig("sample_probs_zeroed")
        block = ctx.enter_context(nc.Block())

        @block.gpsimd
        def _(pool):
            pool.memset(p_t[:, :, :], 0.0).then_inc(zeroed.sem, 1)

        def score(pe, b):
            copied.wait(pe, b + 1)
            for c in range(2):
                m = pe.matmul(s_ps[:, 0:257], sb_.qbd[:, b * 256 + c * P:b * 256 + (c + 1) * P], kt[:, b % 2, c, :],
                              start=b == 0 and c == 0, stop=b == TS - 1 and c == 1 and bias is None)
            if b < TS - 1:
                m.then_inc(used.sem, 1)
            return m

        @block.tensor
        def _(pe):
            for b in range(TS):
                if b >= 2:
                    copied.wait(pe, b - 1)
                for half in range(2):
                    i = 2 * b + half
                    landed[i % 4].wait(pe, 16 * (i // 4 + 1))
                    for c in range(2):
                        m = pe.transpose(k_ps[b % 2][:, c * 256 + half * P:c * 256 + (half + 1) * P],
                                         rows[i][:, c * P:(c + 1) * P], e.ident[:, :])
                m.then_inc(turned.sem, 1)
                if b >= 1:
                    score(pe, b - 1)
            m = score(pe, TS - 1)
            if bias is not None:
                m = pe.matmul(s_ps[:, 0:257], bias[0], bias[1][:, 0:257], start=False, stop=True)
            m.then_inc(s_ready.sem, 1)
            warm_up(e, pe, o_ps[:, 0:P], 36)
            p_ready.wait(pe, 1)
            for half in range(2):
                pe.transpose(t_ps[:, half * P:(half + 1) * P], prob[:, half * P:(half + 1) * P], e.ident[:, :])
            pe.transpose(t_ps[0:TS, 256:256 + P], p_new[:, :], e.ident[:, :]).then_inc(p_turned.sem, 1)
            p_copied.wait(pe, 1)
            for i in range(16):
                b, half = i // 2, i % 2
                pe.matmul(o_ps[:, 0:256], p_t[:, half, b * P:(b + 1) * P], rows[i][:, 256:512], start=i == 0, stop=False)
            pe.matmul(o_ps[:, 0:256], p_nt[:, :], v_new, start=False, stop=True).then_inc(o_ready.sem, 1)

        @block.scalar
        def _(act):
            step.wait(act, 1)
            act.activation(prob[:, :], s_ps[:, 0:257], ACT.Exp, bias=neg_max[:, :], accum_out=r[:, :]).then_inc(exp_done.sem, 1)

        @block.vector
        def _(dve):
            for b in range(TS):
                turned.wait(dve, b + 1)
                if b >= 2:
                    used.wait(dve, b - 1)
                dve.tensor_copy(kt[:, b % 2, :, 256:257], kt_new[:, :, b:b + 1])
                dve.tensor_copy(kt[:, b % 2, :, 0:256], k_ps[b % 2][:, :].rearrange("p (c s) -> p c s", c=2)).then_inc(copied.sem, 1)
            chain = Chain(dve, step)
            s_ready.wait(dve, 1)
            chain(dve.tensor_reduce(neg_max[:, :], s_ps[:, 0:257], AX.X, ALU.max, negate=True))
            exp_done.wait(dve, 1)
            chain(dve.reciprocal(r[:, :], r[:, :]))
            if gate_w is not None:
                chain(dve.tensor_tensor(r[:, :], r[:, :], gate_w, ALU.mult))
            chain(dve.tensor_scalar(prob[:, :], prob[:, :], r[:, :], None, ALU.mult))
            dve.tensor_scalar(p_new[:, :], e.esel[:, :], prob[:, 256:257], None, ALU.mult).then_inc(p_ready.sem, 1)
            p_turned.wait(dve, 1)
            zeroed.wait(dve, 1)
            for half in range(2):
                dve.tensor_copy(p_t[:, half, :].rearrange("p (b s) -> p b s", s=P + 16)[:, :, 0:16],
                                t_ps[:, half * P:(half + 1) * P].rearrange("p (b h) -> p b h", h=16))
            dve.tensor_copy(p_nt[:, :], t_ps[0:TS, 256:256 + P]).then_inc(p_copied.sem, 1)
            o_ready.wait(dve, 1)
            if first:
                dve.tensor_copy(sb_.o_rows[:, :], o_ps[:, 0:256])
            else:
                dve.tensor_tensor(sb_.o_rows[:, :], o_ps[:, 0:256], sb_.o_rows[:, :], ALU.add)
    for s in landed:
        s.base += 64
    for s, n in ((turned, 8), (copied, 8), (s_ready, 1), (used, 7), (step, 3 + (gate_w is not None)), (exp_done, 1),
                 (p_ready, 1), (p_turned, 1), (p_copied, 1), (o_ready, 1), (zeroed, 1)):
        s.base += n


def sample_compressed(e, sb_, kc_t, vc_sample, gate_w):
    nc = e.nc
    with ExitStack() as ctx:
        s, m, r = (ctx.enter_context(nc.sbuf_tensor(f"sc_{n}", shape, F32)) for n, shape in
                   (("s", [P, 32]), ("m", [P, 1]), ("r", [P, 1])))
        p_t = ctx.enter_context(nc.sbuf_tensor("sc_pt", [32, P], F32))
        s_ps, t_ps, o_ps = (ctx.enter_context(nc.psum_tensor(f"sc_{n}", [P, 512], F32)) for n in ("s_ps", "t_ps", "o_ps"))
        step, exp_done, pe_step = e.sig("sc_step", "sc_exp_done", "sc_turned")
        block = ctx.enter_context(nc.Block())

        @block.tensor
        def _(pe):
            for c in range(2):
                mm = pe.matmul(s_ps[:, 0:32], sb_.qz[:, c * P:(c + 1) * P], kc_t[:, c, 8:40], start=c == 0, stop=c == 1)
            mm.then_inc(pe_step.sem, 1)
            step.wait(pe, 5)
            pe.transpose(t_ps[0:32, 0:P], s[:, :], e.ident[:, :]).then_inc(pe_step.sem, 1)
            step.wait(pe, 6)
            pe.matmul(o_ps[:, 0:256], p_t[:, :], vc_sample[0:32, :], start=True, stop=True).then_inc(pe_step.sem, 1)

        @block.scalar
        def _(act):
            step.wait(act, 2)
            act.activation(s[:, :], s[:, :], ACT.Exp, bias=m[:, :], accum_out=r[:, :]).then_inc(exp_done.sem, 1)

        @block.vector
        def _(dve):
            chain = Chain(dve, step)
            pe_step.wait(dve, 1)
            chain(dve.tensor_tensor(s[:, :], s_ps[:, 0:32], e.bmask[:, :], ALU.add))
            chain(dve.tensor_reduce(m[:, :], s[:, :], AX.X, ALU.max, negate=True))
            exp_done.wait(dve, 1)
            chain(dve.reciprocal(r[:, :], r[:, :]))
            chain(dve.tensor_tensor(r[:, :], r[:, :], gate_w, ALU.mult))
            chain(dve.tensor_scalar(s[:, :], s[:, :], r[:, :], None, ALU.mult))
            pe_step.wait(dve, 2)
            chain(dve.tensor_copy(p_t[:, :], t_ps[0:32, 0:P]))
            pe_step.wait(dve, 3)
            chain(dve.tensor_tensor(sb_.o_rows[:, :], o_ps[:, 0:256], sb_.o_rows[:, :], ALU.add))
    step.base += 7
    exp_done.base += 1
    pe_step.base += 3


def sample_finish(e, name, sb_, o_sample):
    nc = e.nc
    with ExitStack() as ctx:
        o_ps = ctx.enter_context(nc.psum_tensor(f"{name}_finish_ps", [P, 512], F32))
        turned, = e.sig("sample_out_turned")
        block = ctx.enter_context(nc.Block())

        @block.tensor
        def _(pe):
            for c in range(2):
                m = pe.transpose(o_ps[:, c * P:(c + 1) * P], sb_.o_rows[:, c * P:(c + 1) * P], e.ident[:, :])
            m.then_inc(turned.sem, 1)

        @block.vector
        def _(dve):
            turned.wait(dve, 1)
            v = o_ps[:, 0:256].rearrange("p (c b h) -> p c h b", c=2, h=16)
            for c in range(2):
                for par in range(2):
                    for odd in range(2):
                        at, tile = 8 * c + 4 * par + odd, 4 * c + 2 * par
                        dve.tensor_copy(o_sample[odd * HD:(odd + 1) * HD, tile:tile + 2, :],
                                        v[par * HD:(par + 1) * HD, c, at:at + 3:2, :])
    turned.base += 1


def nsa_regions(e):
    projection_regions(e, "nsa", e.w_nsa_in[0], NSA_COLS, 5)
    out_regions(e, "nsa", e.w_nsa_out[0])


def nsa(e):
    nc = e.nc
    with ExitStack() as mix:
        def sb(n, shape, dt=F32, ctx=mix):
            return ctx.enter_context(nc.sbuf_tensor(f"nsa_{n}", shape, dt))
        z = sb("z", [P, NT, NSA_COLS])
        o, o_sample = sb("o", [P, 4, D]), sb("o_sample", [P, KC, TS])
        gates, kc_t = sb("gates", [P, NT, 3 * HEADS]), sb("kc_t", [P, 2, 40])
        vc_prompt, vc_sample = sb("vc_prompt", [8, 256]), sb("vc_sample", [32, 256])
        kn = [sb(f"k_new{i}", [P, 2, TS]) for i in range(2)]
        g_bh, last_rows = sb("g_bh", [P, 3]), sb("last_rows", [P, 512])
        projection(e, "nsa", 1, z, 5, NSA_COLS)
        gates_done, g_copied, g_spread = e.sig("gates_done", "gates_masked", "gates_spread")
        with ExitStack() as ctx:
            g_ps = ctx.enter_context(nc.psum_tensor("g_ps", [P, 512], F32))
            g_m = ctx.enter_context(nc.sbuf_tensor("g_m", [P, 3, HEADS], F32))
            block = ctx.enter_context(nc.Block())

            @block.scalar
            def _(act):
                act.activation(gates[:, :, :], z[:, :, 2560:NSA_COLS], ACT.Sigmoid).then_inc(gates_done.sem, 1)

            @block.tensor
            def _(pe):
                gates_done.wait(pe, 1)
                pe.matmul(g_ps[:, 0:48], e.esel_t[0:TS, :], gates[0:TS, 4, :], start=True, stop=True).then_inc(g_spread.sem, 1)

            @block.vector
            def _(dve):
                g_spread.wait(dve, 1)
                dve.tensor_tensor(g_m[:, :, :], g_ps[:, 0:48].rearrange("p (h r) -> p r h", r=3),
                                  e.hmask[:, :].unsqueeze(1).to_broadcast([P, 3, HEADS]), ALU.mult).then_inc(g_copied.sem, 1)
                g_copied.wait(dve, 1)
                dve.tensor_reduce(g_bh[:, :], g_m[:, :, :], AX.X, ALU.add)
        compress(e, z, kc_t, vc_prompt, vc_sample)
        sb_ = SampleBuffers(sb("qbd", [P, 2304]), sb("qz", [P, 256]), sb("o_rows", [P, 256]))
        with ExitStack() as turns:
            qt_raw, qt = sb("qt_raw", [P, 8, T], ctx=turns), sb("qt", [P, 8, T], ctx=turns)
            kts = [sb(f"kt{i}", [P, 2, T], ctx=turns) for i in range(2)]
            k_cols = (1536, 2048)
            jobs = [(lambda t, j=j: z[:, t, j * P:(j + 1) * P], qt_raw[:, j, :], SCALE, "raw") for j in range(8)]
            jobs += [(lambda t, c=c, i=i: z[:, t, k_cols[i] + c * P:k_cols[i] + (c + 1) * P], kts[i][:, c, :], 1.0, "k")
                     for i in range(2) for c in range(2)]
            jobs += [(lambda t, j=j: z[:, t, j * P:(j + 1) * P], qt[:, j, :], SCALE, "q") for j in range(8)]
            stores = []
            for i, (out_p, out_s) in enumerate(((e.nsa_slc_p, e.nsa_slc_s), (e.nsa_win_p, None))):
                v = out_p[0, 0].rearrange("(t p) c k d -> p t (c k d)", p=P)
                stores += [(v[:, t, :], z[:, t, k_cols[i]:k_cols[i] + 512]) for t in range(4)]
                if out_s is not None:
                    stores.append((out_s[0].rearrange("b s c k d -> (b s) (c k d)"), z[0:TS, 4, k_cols[i]:k_cols[i] + 512]))
                else:
                    stores.append((e.nsa_win_s[0, :, 255].rearrange("b c k d -> b (c k d)"), z[0:TS, 4, k_cols[i]:k_cols[i] + 512]))
            turn_stage(e, "nsa", z, jobs, [(0, HEADS)], [(c, KV) for c in k_cols], stores)
            compressed_attention(e, qt_raw, kc_t, vc_prompt, gates, o)
            with ExitStack() as ctx:
                block = ctx.enter_context(nc.Block())

                @block.vector
                def _(dve):
                    for i in range(2):
                        dve.tensor_copy(kn[i][:, :, :], kts[i][:, :, TP:T])
            sample_setup(e, qt_raw, qt, sb_)
            rows = [z[:, i // 3, i % 3 * 512:(i % 3 + 1) * 512] for i in range(15)] + [last_rows[:, :]]
            slc_rows = lambda i, page: e.cache_nsa_slc[0, ds(page, 1)].rearrange("o p c k d -> (o p) (c k d)")
            win_rows = lambda i, page: e.state_nsa_win[0, i // 2, (i % 2) * P:(i % 2 + 1) * P].rearrange("p c k d -> p (c k d)")
            for i, (name, rows_of, table) in enumerate((("slc", slc_rows, e.table), ("win", win_rows, None))):
                v = k_cols[i] + 256
                attention(e, name, qt, kts[i], lambda kc, kv, v=v: z[:, kc, v + kv * HD:v + (kv + 1) * HD],
                          None, (gates, 1 + i), o, True,
                          lambda sp, rows_of=rows_of, table=table: sample_loads(e, sp, rows, rows_of, table))
                sample_attention(e, "s" + name, sb_, rows, kn[i], z[0:TS, 4, v:v + 256], g_bh[:, 1 + i:2 + i], i == 0)
        sample_compressed(e, sb_, kc_t, vc_sample, g_bh[:, 0:1])
        sample_finish(e, "nsa", sb_, o_sample)
        out_projection(e, "nsa", o, o_sample, e.x_rows)



N_IDX = 8
TOPK = P
TOPK_S = 64
TAKEN = -3.0e38
IDX_SCALE = N_IDX ** -0.5


def index_prompt(e, ctx, block, z, qi_t, ki_t, wi, bias, qt):
    nc = e.nc

    def sb(n, shape, dt=F32):
        return ctx.enter_context(nc.sbuf_tensor(f"ix_{n}", shape, dt))
    relu, score, top = [sb(f"relu{i}", [P, TP]) for i in range(2)], sb("score", [P, 4, TP]), sb("top", [P, 8])
    ps = [ctx.enter_context(nc.psum_tensor(f"ix_ps{i}", [P, 512], F32)) for i in range(2)]
    q_ps = ctx.enter_context(nc.psum_tensor("ix_q_ps", [P, 2, 512], F32))
    s_ready, r_done, summed, score_done, step, q_turned, q_copied = e.sig(
        "ix_scores", "ix_relu_done", "ix_summed", "ix_score_done", "ix_step", "ix_q_turned", "ix_q_copied")
    first_summed, = e.sig("ix_first_summed")
    items = [(i, h) for i in range(1, 4) for h in range(N_IDX)]

    def relu_count(n):
        return n + 1 if n < N_IDX else 2 * n + 1 - N_IDX

    @block.tensor
    def _(pe):
        for n, (i, h) in enumerate(items):
            if n >= 2:
                r_done.wait(pe, relu_count(n - 2))
            rows = slice((h % 2) * HD, (h % 2 + 1) * HD)
            pe.matmul(ps[n % 2][:, 0:(i + 1) * P], qi_t[rows, h // 2, i * P:(i + 1) * P], ki_t[rows, 0, 0:(i + 1) * P],
                      start=True, stop=True).then_inc(s_ready.sem, 1)
            if n % 3 == 2:
                j = n // 3
                if j >= 1:
                    q_copied.wait(pe, j)
                for t in range(NT):
                    dst = q_ps[:, 0, t * P:(t + 1) * P] if t < NT - 1 else q_ps[:, 1, 0:P]
                    m = pe.transpose(dst, z[:, t, j * P:(j + 1) * P], e.ident[:, :])
                m.then_inc(q_turned.sem, 1)

    @block.scalar
    def _(act):
        def copy_q(j):
            q_turned.wait(act, j + 1)
            act.activation(qt[:, j, 0:TP], q_ps[:, 0, :], ACT.Copy, scale=SCALE)
            act.activation(qt[:, j, TP:T], q_ps[:, 1, 0:TS], ACT.Copy, scale=SCALE).then_inc(q_copied.sem, 1)

        for n, (i, h) in enumerate(items):
            s_ready.wait(act, n + 1)
            if n >= 2:
                if n < N_IDX + 2:
                    first_summed.wait(act, n - 1)
                else:
                    summed.wait(act, n - 1 - N_IDX)
            r = relu[n % 2][:, 0:(i + 1) * P]
            act.activation(r, ps[n % 2][:, 0:(i + 1) * P], ACT.Relu).then_inc(r_done.sem, 1)
            if n >= N_IDX:
                r_done.wait(act, relu_count(n))
                score_done.wait(act, 1)
                act.activation(r, r, ACT.Copy, scale=wi[:, i, h:h + 1]).then_inc(r_done.sem, 1)
            if n % 3 == 1 and n > 3:
                copy_q(n // 3 - 1)
        copy_q(len(items) // 3 - 1)

    @block.gpsimd
    def _(pool):
        pool.tensor_scalar(wi[:, :, :], z[:, :, 2112:2120], IDX_SCALE, None, ALU.mult).then_inc(score_done.sem, 1)
        for n, (i, h) in enumerate(items):
            if i == 1:
                continue
            width = (i + 1) * P
            s = score[:, i, 0:width]
            r_done.wait(pool, relu_count(n) + 1)
            if h == 0:
                ins = pool.tensor_copy(s, relu[n % 2][:, 0:width])
            else:
                ins = pool.tensor_tensor(s, relu[n % 2][:, 0:width], s, ALU.add)
            ins.then_inc(summed.sem, 1)
            summed.wait(pool, n + 1 - N_IDX)
            if h == N_IDX - 1:
                pool.tensor_tensor(score[:, i, i * P:width], score[:, i, i * P:width], e.causal_f[:, :], ALU.add)\
                    .then_inc(score_done.sem, 1)

    chains = []

    def choose(dve, i):
        chain, width = chains[0], (i + 1) * P
        s = score[:, i, 0:width]
        if i > 1:
            score_done.wait(dve, i)
        for _ in range(TOPK // 8):
            chain(dve.max(top[:, :], s))
            chain(dve.match_replace(s, top[:, :], s, TAKEN))
        chain(dve.tensor_scalar(bias[:, i, 0:width], s, TAKEN / 2, NEG, ALU.is_gt, ALU.mult))
        chain(dve.tensor_tensor(bias[:, i, i * P:width], bias[:, i, i * P:width], e.causal_b[:, :], ALU.add))

    @block.vector
    def _(dve):
        chains.append(Chain(dve, step))
        chains[0](dve.tensor_copy(bias[:, 0, 0:P], e.causal_b[:, :]))
        score_done.wait(dve, 1)
        for h in range(N_IDX):
            r_done.wait(dve, relu_count(h))
            s, r, w = score[:, 1, 0:2 * P], relu[h % 2][:, 0:2 * P], wi[:, 1, h:h + 1]
            if h == 0:
                dve.tensor_scalar(s, r, w, None, ALU.mult).then_inc(first_summed.sem, 1)
            else:
                dve.scalar_tensor_tensor(s, r, w, s, ALU.mult, ALU.add).then_inc(first_summed.sem, 1)
            first_summed.wait(dve, h + 1)
        chains[0](dve.tensor_tensor(score[:, 1, P:2 * P], score[:, 1, P:2 * P], e.causal_f[:, :], ALU.add))
        choose(dve, 1)
        choose(dve, 2)
    return choose


def index_sample(e, ctx, block, qi_t, ki_t, wi, bias_s, choose):
    nc = e.nc

    def sb(n, shape, dt=F32):
        return ctx.enter_context(nc.sbuf_tensor(f"is_{n}", shape, dt))
    rows, kt = sb("rows", [P, 16, HD]), sb("kt", [HD, TS, 256])
    qz, w_m, w_col, w_bd = sb("qz", [HD, 8 * 72]), sb("w_m", [64, 8]), sb("w_col", [64, 1]), sb("w_bd", [64, TS])
    relu, s, top = sb("relu", [64, 257]), sb("s", [TS, 257]), sb("top", [TS, 8])
    k_ps = [ctx.enter_context(nc.psum_tensor(f"is_k_ps{i}", [P, 512], F32)) for i in range(2)]
    s_ps, o_ps = (ctx.enter_context(nc.psum_tensor(f"is_{n}", [P, 512], F32)) for n in ("s_ps", "o_ps"))
    w_ps = o_ps[:, 504:512]
    landed = e.sig(*[f"sample_rows_landed{i}" for i in range(4)])
    turned, copied, ready, step, relu_done, summed = e.sig("is_turned", "is_copied", "is_ready", "is_step", "is_relu",
                                                           "is_summed")

    @block.sync
    def _(sp):
        for i in range(16):
            page = sp.value_load(e.table[0:1, i:i + 1], min_val=0, max_val=e.cache_dsa_idx.shape[1] - 1)
            if i >= 4:
                landed[i % 4].wait(sp, 16 * (i // 4))
            sp.dma_start(rows[:, i, :], e.cache_dsa_idx[0, ds(page, 1)].rearrange("o p d -> (o p) d"))\
              .then_inc(landed[i % 4].sem, 16)

    @block.tensor
    def _(pe):
        pe.matmul(w_ps[0:64, :], e.isel_t[0:TS, :], wi[0:TS, 4, :], start=True, stop=True).then_inc(turned.sem, 1)
        for n in range(4):
            if n >= 2:
                copied.wait(pe, n - 1)
            for k in range(4):
                i = 4 * n + k
                landed[i % 4].wait(pe, 16 * (i // 4 + 1))
                m = pe.transpose(k_ps[n % 2][0:HD, k * P:(k + 1) * P], rows[:, i, :], e.ident[:, :])
            m.then_inc(turned.sem, 1)
        copied.wait(pe, 4)
        step.wait(pe, 6)
        for b in range(TS):
            pe.matmul(s_ps[0:64, 0:256], qz[:, b * 64:(b + 1) * 64], kt[:, b, :], start=b == 0, stop=b == TS - 1)
        for b in range(TS):
            m = pe.matmul(s_ps[0:64, 256:257], qz[:, b * 64:(b + 1) * 64], ki_t[0:HD, 0, TP + b:TP + b + 1],
                          start=b == 0, stop=b == TS - 1)
        m.then_inc(ready.sem, 1)
        relu_done.wait(pe, 1)
        pe.matmul(o_ps[0:TS, 0:257], w_bd[:, :], relu[:, :], start=True, stop=True).then_inc(summed.sem, 1)

    @block.scalar
    def _(act):
        ready.wait(act, 1)
        act.activation(relu[:, :], s_ps[0:64, 0:257], ACT.Relu).then_inc(relu_done.sem, 1)

    @block.vector
    def _(dve):
        chain = Chain(dve, step)
        turned.wait(dve, 1)
        chain(dve.tensor_tensor(w_m[:, :], w_ps[0:64, :], e.imask[0:64, :], ALU.mult))
        chain(dve.tensor_reduce(w_col[:, :], w_m[:, :], AX.X, ALU.add))
        chain(dve.tensor_scalar(w_bd[:, :], e.isel[0:64, :], w_col[:, :], None, ALU.mult))
        chain(dve.memset(qz[:, :], 0.0))
        for par in range(2):
            chain(dve.tensor_copy(qz[:, :].rearrange("p (b s) -> p b s", s=72)[:, :, par:8:2],
                                  qi_t[par * HD:(par + 1) * HD, :, TP:T].rearrange("p h b -> p b h")))
        for n in range(4):
            turned.wait(dve, n + 2)
            dve.tensor_copy(kt[:, 2 * n:2 * n + 2, :].rearrange("p b s -> p (b s)"), k_ps[n % 2][0:HD, :]).then_inc(copied.sem, 1)
        choose(dve, 3)
        summed.wait(dve, 1)
        chain(dve.tensor_copy(s[:, :], o_ps[0:TS, 0:257]))
        for _ in range(TOPK_S // 8):
            chain(dve.max(top[:, :], s[:, :]))
            chain(dve.match_replace(s[:, :], top[:, :], s[:, :], TAKEN))
        chain(dve.tensor_scalar(bias_s[:, :], s[:, :], TAKEN / 2, NEG, ALU.is_gt, ALU.mult))
    for sig in landed:
        sig.base += 64
    for sig, n in ((turned, 5), (copied, 4), (ready, 1), (step, 8 + 2 * TOPK_S // 8), (relu_done, 1), (summed, 1)):
        sig.base += n


def dsa_regions(e):
    projection_regions(e, "dsa", e.w_dsa_in[0], DSA_COLS, 4)
    out_regions(e, "dsa", e.w_dsa_out[0])


def dsa(e):
    nc = e.nc
    with ExitStack() as mix:
        def sb(n, shape, dt=F32, ctx=mix):
            return ctx.enter_context(nc.sbuf_tensor(f"dsa_{n}", shape, dt))
        z = sb("z", [P, NT, DSA_COLS])
        o, o_sample, kn = sb("o", [P, 4, D]), sb("o_sample", [P, KC, TS]), sb("k_new", [P, 2, TS])
        bias_s, last_rows = sb("bias_s", [TS, 257]), sb("last_rows", [P, 512])
        sb_ = SampleBuffers(sb("qbd", [P, 2304]), None, sb("o_rows", [P, 256]))
        projection(e, "dsa", 4, z, 4, DSA_COLS)
        with ExitStack() as turns:
            qt, kt = sb("qt", [P, 8, T], ctx=turns), sb("kt", [P, 2, T], ctx=turns)
            qi_t, ki_t = sb("qi_t", [P, 4, T], ctx=turns), sb("ki_t", [P, 1, T], ctx=turns)
            wi, bias = sb("wi", [P, NT, N_IDX], ctx=turns), sb("bias", [P, 4, TP], BF16, ctx=turns)
            jobs = [(lambda t, c=c: z[:, t, 1024 + c * P:1024 + (c + 1) * P], kt[:, c, :], 1.0, "k") for c in range(2)]
            jobs.append((lambda t: z[:, t, 2048:2112], ki_t[:, 0, :], 1.0, "k"))
            jobs += [(lambda t, j=j: z[:, t, 1536 + j * P:1536 + (j + 1) * P], qi_t[:, j, :], SCALE, "q") for j in range(4)]
            kv, ix = (x[0, 0].rearrange(r, p=P) for x, r in ((e.dsa_kv_p, "(t p) c k d -> p t (c k d)"),
                                                             (e.dsa_idx_p, "(t p) d -> p t d")))
            stores = [(kv[:, t, :], z[:, t, 1024:1536]) for t in range(4)] + [(ix, z[:, 0:4, 2048:2112])]
            stores += [(e.dsa_kv_s[0].rearrange("b s c k d -> (b s) (c k d)"), z[0:TS, 4, 1024:1536]),
                       (e.dsa_idx_s[0].rearrange("b s d -> (b s) d"), z[0:TS, 4, 2048:2112])]
            turn_stage(e, "dsa", z, jobs, [(1536, N_IDX), (0, HEADS)], [(1024, KV), (2048, 1)], stores)
            with ExitStack() as ctx:
                block = ctx.enter_context(nc.Block())
                choose = index_prompt(e, ctx, block, z, qi_t, ki_t, wi, bias, qt)
                index_sample(e, ctx, block, qi_t, ki_t, wi, bias_s, choose)
            rows = [z[:, i // 3, c:c + 512] for i in range(15) for c in ((0, 512, 1536)[i % 3],)] + [last_rows[:, :]]
            attention(e, "dsa_att", qt, kt, lambda kc, kv: z[:, kc, 1280 + kv * HD:1280 + (kv + 1) * HD], bias, None, o, False,
                      lambda sp: sample_loads(
                          e, sp, rows, lambda i, page: e.cache_dsa_kv[0, ds(page, 1)].rearrange("o p c k d -> (o p) (c k d)"),
                          e.table))
            with ExitStack() as ctx:
                block = ctx.enter_context(nc.Block())

                @block.vector
                def _(dve):
                    dve.tensor_copy(kn[:, :, :], kt[:, :, TP:T])
            sample_setup(e, None, qt, sb_)
        sample_attention(e, "sdsa", sb_, rows, kn, z[0:TS, 4, 1280:1536], None, True, bias=(e.esel_t[0:TS, :], bias_s))
        sample_finish(e, "dsa", sb_, o_sample)
        out_projection(e, "dsa", o, o_sample, e.x_rows)


def start_stage(e, sum_squares):
    nc = e.nc
    with ExitStack() as ctx:
        rows = ctx.enter_context(nc.sbuf_tensor("x_rows", [P, NT, D], F32))
        gain_rows = ctx.enter_context(nc.sbuf_tensor("gain_rows", [7 * KC, P], F32))
        xt_ps = [ctx.enter_context(nc.psum_tensor(f"xt_ps{i}", [P, 512], F32)) for i in range(4)]
        block = ctx.enter_context(nc.Block())
        loads = [
            (e.const[:, :], e.c_const), (e.table[:, :], e.page_table.rearrange("(o b) n -> o (b n)", o=1)),
            (gain_rows[0:6 * KC, :], e.norm_g.rearrange("l s (k p) -> (l s k) p", p=P)),
            (gain_rows[6 * KC:7 * KC, :], e.final_norm_g.rearrange("(k p) -> k p", p=P)),
            (rows[:, 0:4, :], e.x_prompt[0].rearrange("(t p) d -> p t d", p=P)),
            (rows[0:TS, 4, :], e.x_sample.rearrange("b s d -> (b s) d")),
        ]

        @block.sync
        def _(sp):
            for dst, src in loads:
                sp.dma_start(dst, src).then_inc(e.start_loaded, 16)
            load_units(e, sp, 0, min(2, e.stream.total))

        @block.gpsimd
        def _(pool):
            pool.memset(e.sumsq[:, :], 1.0).then_inc(e.sum_done, 1)
            pool.memset(e.eps[:, :], EPS).then_inc(e.sq_done, 1)
            e.sums = 1
            pool.wait_ge(e.sq_done, 1)
            if sum_squares:
                square_sum_pool(e, pool, 0)

        @block.tensor
        def _(pe):
            pe.wait_ge(e.start_loaded, 16 * len(loads))
            pe.transpose(xt_ps[2][:, 0:7 * KC], gain_rows[:, :], e.ident[0:7 * KC, 0:7 * KC])
            for k in range(KC):
                m = pe.transpose(xt_ps[3][:, k * TS:(k + 1) * TS], rows[0:TS, 4, k * P:(k + 1) * P], e.ident[0:TS, 0:TS])
            m.then_inc(e.turned, 1)
            for k in range(KC):
                if k >= 2:
                    pe.wait_ge(e.x_done, k - 1)
                for t in range(4):
                    m = pe.transpose(xt_ps[k % 2][:, t * P:(t + 1) * P], rows[:, t, k * P:(k + 1) * P], e.ident[:, :])
                m.then_inc(e.turned, 1)

        @block.scalar
        def _(act):
            act.wait_ge(e.turned, 1)
            act.activation(e.x[:, :, TP:T], xt_ps[3][:, 0:KC * TS].rearrange("p (k t) -> p k t", k=KC), ACT.Copy)\
               .then_inc(e.sample_turned, 1)
            split_hi(e, act, 0, 0, e.cols_of(0))

        @block.vector
        def _(dve):
            dve.wait_ge(e.turned, 1)
            dve.memset(e.start_mark[:, :], 0.0).then_inc(e.a_lo_done, 1)
            dve.tensor_copy(e.gain[:, :], xt_ps[2][:, 0:7 * KC]).then_inc(e.start_copied, 1)
            dve.tensor_copy(e.ident_b[:, :], e.ident[:, :]).then_inc(e.start_copied, 1)
            dve.tensor_copy(e.causal_b[:, :], e.causal_f[:, :]).then_inc(e.start_copied, 1)
            dve.wait_ge(e.sample_turned, 1)
            for k in range(KC):
                dve.wait_ge(e.turned, k + 2)
                dve.tensor_copy(e.x[:, k, 0:TP], xt_ps[k % 2][:, :]).then_inc(e.x_done, 1)
            split_lo(e, dve, 0, 0, e.cols_of(0))
    e.x_rows += KC


def final_stage(e):
    nc = e.nc
    norm = 6
    with ExitStack() as ctx:
        y = ctx.enter_context(nc.sbuf_tensor("y", [P, KC, T], F32))
        rows = ctx.enter_context(nc.sbuf_tensor("y_rows", [P, NT, D], F32))
        stat_ps = ctx.enter_context(nc.psum_tensor("stat_ps", [P, 2, 512], F32))
        row_ps = [ctx.enter_context(nc.psum_tensor(f"row_ps{i}", [P, 512], F32)) for i in range(4)]
        block = ctx.enter_context(nc.Block())
        n = e.norm_n

        @block.tensor
        def _(pe):
            for half in range(2):
                m = pe.matmul(stat_ps[:, half, 0:TH], e.ones[:, :], e.sumsq[:, half * TH:(half + 1) * TH],
                              start=True, stop=True)
            m.then_inc(e.stat_ready, 1)
            for t in range(NT):
                m_rows = P if t < 4 else TS
                for half in range(2):
                    i = 2 * t + half
                    if i >= 4:
                        pe.wait_ge(e.row_copied, i - 3)
                    pe.wait_ge(e.y_done, 4 * (half + 1))
                    for k in range(4):
                        kk = 4 * half + k
                        m = pe.transpose(row_ps[i % 4][0:m_rows, k * P:(k + 1) * P],
                                         y[:, kk, t * P:t * P + m_rows], e.ident[:, :])
                    m.then_inc(e.row_turned, 1)

        @block.scalar
        def _(act):
            act.wait_ge(e.stat_ready, n + 1)
            act.activation(e.rms[:, :].rearrange("p (a t) -> p a t", a=2), stat_ps[:, :, 0:TH], ACT.Sqrt,
                           bias=e.eps[:, :], scale=1.0 / D).then_inc(e.rms_done, 1)

        @block.vector
        def _(dve):
            dve.wait_ge(e.rms_done, n + 1)
            dve.reciprocal(e.rs[:, :], e.rms[:, :]).then_inc(e.rs_done, 1)
            dve.wait_ge(e.rs_done, n + 1)
            for k in range(KC):
                dve.scalar_tensor_tensor(y[:, k, :], e.x[:, k, :], e.gain[:, norm * KC + k:norm * KC + k + 1],
                                         e.rs[:, :], ALU.mult, ALU.mult).then_inc(e.y_done, 1)
            for i in range(2 * NT):
                m_rows = P if i < 8 else TS
                dve.wait_ge(e.row_turned, i + 1)
                dve.tensor_copy(rows[0:m_rows, i // 2, (i % 2) * 512:(i % 2 + 1) * 512],
                                row_ps[i % 4][0:m_rows, :]).then_inc(e.row_copied, 1)

        @block.sync
        def _(sp):
            yp = e.y_prompt[0].rearrange("(t p) d -> p t d", p=P)
            for t in range(4):
                sp.wait_ge(e.row_copied, 2 * t + 2)
                sp.dma_start(yp[:, t, :], rows[:, t, :]).then_inc(e.stored, 16)
                e.stores += 1
            sp.wait_ge(e.row_copied, 2 * NT)
            sp.dma_start(e.y_sample.rearrange("b s d -> (b s) d"), rows[0:TS, 4, :]).then_inc(e.stored, 16)
            e.stores += 1
            sp.wait_ge(e.stored, 16 * e.stores)


CONSTS = (("ident", P), ("causal_f", P), ("ones", P), ("cos", NT * 16), ("sin", NT * 16), ("cadd", 32), ("c01", 32),
          ("hsel", HEADS), ("esel", TS), ("hmask", HEADS), ("bmask", 32), ("rep", P), ("esel_t", P),
          ("isel", TS), ("imask", 8), ("isel_t", 64))


def constants():
    import numpy as np
    i = np.arange(P)
    pos = np.full(NT * P, 256, np.int32)
    pos[0:TP] = np.arange(TP)
    inv = np.float32(500000.0) ** (-np.arange(8, dtype=np.float32) * np.float32(2.0) / np.float32(16))
    ang = pos.astype(np.float32)[:, None] * inv[None, :]
    seen = ((np.arange(8) + 1) * 64 - 1)[None, :] <= np.arange(TP)[:, None]

    ang = np.concatenate([ang, ang], axis=1)

    def tiles(a):
        return a.reshape(-1, P, a.shape[1]).transpose(1, 0, 2).reshape(P, -1)
    j, par, n = i // 16, i // 8 % 2, i % 8
    head = 8 * (j // 4) + 4 * par + j % 4
    rep = np.zeros((P, P), np.float32)
    rep[n, i] = 1
    esel_t = np.zeros((P, P), np.float32)
    esel_t[i // 16, i] = 1
    parts = {
        "ident": np.eye(P), "causal_f": np.where(i[None, :] <= i[:, None], 0, NEG), "ones": np.ones((P, P)),
        "cos": tiles(np.cos(ang)), "sin": tiles(np.sin(ang)), "cadd": tiles(np.where(seen, 0, NEG)),
        "c01": tiles(seen), "hsel": head[:, None] == np.arange(16), "esel": i[:, None] // 16 == np.arange(8),
        "hmask": i[:, None] % 16 == np.arange(16), "bmask": np.where(i[:, None] // 16 == np.arange(32) // 4, 0, NEG),
        "rep": rep, "esel_t": esel_t, "isel": i[:, None] // 8 == np.arange(8), "imask": i[:, None] % 8 == np.arange(8),
        "isel_t": i[:, None] == np.arange(64) // 8,
    }
    return {"c_const": np.concatenate([np.asarray(parts[c], np.float32) for c, _ in CONSTS], axis=1)}


OUTS = {
    "y_prompt": (1, TP, D), "y_sample": (TS, 1, D),
    "nsa_cmp_p": (1, 1, TP, 2, KV, HD), "nsa_cmp_s": (1, TS, 1, 2, KV, HD),
    "nsa_slc_p": (1, 1, TP, 2, KV, HD), "nsa_slc_s": (1, TS, 1, 2, KV, HD),
    "nsa_win_p": (1, 1, TP, 2, KV, HD), "nsa_win_s": (1, TS, 256, 2, KV, HD),
    "dsa_kv_p": (1, 1, TP, 2, KV, HD), "dsa_kv_s": (1, TS, 1, 2, KV, HD),
    "dsa_idx_p": (1, 1, TP, HD), "dsa_idx_s": (1, TS, 1, HD),
}


def build(nc, ins, outs, plan=None):
    c_const = ins["c_const"]
    plan = plan or ["ffn0", "nsa", "ffn1", "ffn2", "dsa", "ffn3"]
    with ExitStack() as ctx:
        def sb(name, shape, dt=F32):
            return ctx.enter_context(nc.sbuf_tensor(name, shape, dt))
        signals = {}

        def sig(*names):
            for name in names:
                if name not in signals:
                    signals[name] = Signal(ctx.enter_context(nc.semaphore(name)))
            return [signals[name] for name in names]
        const, views, at = sb("const", [P, sum(n for _, n in CONSTS)]), {}, 0
        for name, n in CONSTS:
            views[name] = const[:, at:at + n]
            at += n
        for name, n in (("cos", NT), ("sin", NT), ("cadd", 4), ("c01", 4)):
            views[name] = views[name].rearrange("p (t n) -> p t n", t=n)
        e = Core(nc, sig, ins, outs, c_const, const, views, lambda name: ctx.enter_context(nc.semaphore(name)))
        for step in plan:
            if step.startswith("ffn"):
                ffn_regions(e, int(step[3:]))
            elif step == "nsa":
                nsa_regions(e)
            else:
                dsa_regions(e)
        e.x = sb("x", [P, KC, T])
        e.w_stage = [sb(f"w_stage{i}", [P, UNIT]) for i in range(2)]
        e.w_hi = [sb(f"w_hi{i}", [P, UNIT], FR) for i in range(2)]
        e.w_lo = [sb(f"w_lo{i}", [P, UNIT], FR) for i in range(2)]
        e.table = sb("table", [1, 2 * TS], I32)
        e.ident_b, e.causal_b = sb("ident_b", [P, P], BF16), sb("causal_b", [P, P], BF16)
        e.gain = sb("gain", [P, 7 * KC])
        e.sq, e.sumsq = sb("sq", [P, T]), sb("sumsq", [P, NT * P])
        e.rms, e.rs = sb("rms", [P, T]), sb("rs", [P, T])
        e.eps, e.start_mark, e.start_mark2 = sb("eps", [P, 1]), sb("start_mark", [P, 1]), sb("start_mark2", [P, 1])
        e.rms_col, e.rs_col = sb("rms_col", [P, NT]), sb("rs_col", [P, NT])
        start_stage(e, plan[0] != "ffn0")
        for step in plan:
            if step.startswith("ffn"):
                n = int(step[3:])
                ffn(e, n, 3 * (n // 2) + 2 * (n % 2), e.x_rows)
                e.x_rows += 2 * KC
            elif step == "nsa":
                nsa(e)
            else:
                dsa(e)
        final_stage(e)



INS = ("x_prompt", "x_sample", "cache_nsa_cmp", "cache_nsa_slc", "state_nsa_win", "cache_dsa_kv", "cache_dsa_idx",
       "page_table", "norm_g", "w_ffn_in", "w_ffn_out", "w_nsa_in", "w_nsa_out", "nsa_cmp_pos", "nsa_cmp_w1",
       "nsa_cmp_w2", "w_dsa_in", "w_dsa_out", "final_norm_g")


def kernel(**inputs):
    import numpy as np
    import concourse.bacc as bacc
    from concourse.bass_utils import run_bass_kernel_spmd

    nc = bacc.Bacc("TRN2", target_bir_lowering=False, num_devices=1)
    arrays, ins = {}, {}
    for name in INS:
        arrays[name] = np.ascontiguousarray(inputs[name])
    arrays.update(constants())
    for name, a in arrays.items():
        ins[name] = nc.dram_tensor(name, a.shape, mybir.dt.from_np(a.dtype), kind="ExternalInput").ap()
    outs = {name: nc.dram_tensor(name, shape, F32, kind="ExternalOutput").ap() for name, shape in OUTS.items()}
    build(nc, ins, outs)
    r = run_bass_kernel_spmd(nc, [arrays], core_ids=[0])
    return tuple(r.results[0][name] for name in OUTS)
```
